# Optimizing a Trainium2 kernel written in Bass

```python
import math
import jax, jax.numpy as jnp
from jax import lax
import numpy as np

D_MODEL = 1024
BATCH = 1
SEQ = 512
DEPTH = 1
DEC_BATCH = 1
DEC_SEQ = 1024
PAST_LEN = 128

H_RET = 8
DK_RET = 64
DV_RET = 64
RET_CHUNK = 128
H_MLA = 4
MLA_Q_RANK = 256
MLA_KV_RANK = 128
MLA_NOPE = 128
MLA_ROPE = 64
MLA_V = 128
Q_BLOCK = 128
ROPE_BASE = 10000.0
D_MIX = H_RET * DV_RET + H_MLA * MLA_V
D_IN = 2 * H_RET * DK_RET + 2 * H_RET * DV_RET + MLA_Q_RANK + MLA_KV_RANK + MLA_ROPE
N_GROUPS = 4
EXPERTS_PER_GROUP = 8
N_EXPERTS = N_GROUPS * EXPERTS_PER_GROUP
TOP_K = 2
D_EXPERT = 512
MOE_BLOCK = 128
EPS = 1e-6

kernel_name = 'hymba_retnet_mla_hmoe_encoder'

def _rmsnorm(x, g):
    xf = x.astype(jnp.float32)
    y = xf * lax.rsqrt(jnp.mean(xf * xf, axis=-1, keepdims=True) + EPS)
    return (y * g.astype(jnp.float32)).astype(x.dtype)

def _rope_tables(seq, dim):
    inv = 1.0 / (ROPE_BASE ** (jnp.arange(0, dim, 2, dtype=jnp.float32) / dim))
    ang = jnp.arange(seq, dtype=jnp.float32)[:, None] * inv[None, :]
    return jnp.cos(ang), jnp.sin(ang)

def _apply_rope(x, cos, sin):
    half = x.shape[-1] // 2
    xf = x.astype(jnp.float32)
    x1, x2 = xf[..., :half], xf[..., half:]
    c = cos[None, :, None, :]
    s = sin[None, :, None, :]
    return jnp.concatenate([x1 * c - x2 * s, x2 * c + x1 * s], axis=-1).astype(x.dtype)

def _excl_scan(s_chunks, decay_c, reverse):
    def step(carry, s_n):
        return carry * decay_c[None, :, None, None] + s_n, carry
    _, out = lax.scan(step, jnp.zeros_like(s_chunks[0]), s_chunks, reverse=reverse)
    return out

def _retention_bidir(q, k, v, log_decay):
    B, S, H, dk = q.shape
    dv = v.shape[-1]
    C = RET_CHUNK
    N = S // C
    lg = -jnp.exp(log_decay.astype(jnp.float32))
    lf, lb = lg[0], lg[1]
    idx = jnp.arange(C, dtype=jnp.float32)
    diff = idx[:, None] - idx[None, :]
    d_f = jnp.where(diff >= 0, jnp.exp(lf[:, None, None] * jnp.maximum(diff, 0.0)), 0.0)
    d_b = jnp.where(diff < 0, jnp.exp(lb[:, None, None] * jnp.maximum(-diff, 0.0)), 0.0)
    dmat = d_f + d_b
    qc = q.reshape(B, N, C, H, dk)
    kc = k.reshape(B, N, C, H, dk)
    vc = v.reshape(B, N, C, H, dv)
    scores = jnp.einsum('bnihd,bnjhd->bnhij', qc, kc, preferred_element_type=jnp.float32) * dmat[None, None]
    intra = jnp.einsum('bnhij,bnjhe->bnihe', scores, vc.astype(jnp.float32))
    w_kf = jnp.exp(lf[None, :] * (C - 1 - idx)[:, None])
    w_kb = jnp.exp(lb[None, :] * idx[:, None])
    s_f = jnp.einsum('bnjhd,bnjhe->nbhde', kc * w_kf[None, None, :, :, None], vc.astype(jnp.float32))
    s_b = jnp.einsum('bnjhd,bnjhe->nbhde', kc * w_kb[None, None, :, :, None], vc.astype(jnp.float32))
    st_f = _excl_scan(s_f, jnp.exp(lf * C), reverse=False)
    st_b = _excl_scan(s_b, jnp.exp(lb * C), reverse=True)
    q_f = qc * jnp.exp(lf[None, :] * (idx + 1.0)[:, None])[None, None, :, :, None]
    q_b = qc * jnp.exp(lb[None, :] * (C - idx)[:, None])[None, None, :, :, None]
    inter = jnp.einsum('bnihd,nbhde->bnihe', q_f, st_f) + jnp.einsum('bnihd,nbhde->bnihe', q_b, st_b)
    return (intra + inter).reshape(B, S, H, dv)

def _mla_attention(qn, qr, kn, kr, v):
    B, S, H, dn = qn.shape
    dr = qr.shape[-1]
    dv = v.shape[-1]
    nq = S // Q_BLOCK
    scale = (dn + dr) ** -0.5
    qn_b = qn.reshape(B, nq, Q_BLOCK, H, dn).swapaxes(0, 1)
    qr_b = qr.reshape(B, nq, Q_BLOCK, H, dr).swapaxes(0, 1)

    def attend(args):
        qnb, qrb = args
        s = (jnp.einsum('bqhd,bkhd->bhqk', qnb, kn, preferred_element_type=jnp.float32)
             + jnp.einsum('bqhr,bkr->bhqk', qrb, kr, preferred_element_type=jnp.float32)) * scale
        p = jax.nn.softmax(s, axis=-1)
        return jnp.einsum('bhqk,bkhd->bqhd', p.astype(v.dtype), v)

    o = lax.map(attend, (qn_b, qr_b))
    return o.swapaxes(0, 1).reshape(B, S, H * dv)

def _hier_moe(h, w_rg, w_re, w_g, w_u, w_d):
    B, S, D = h.shape
    T = B * S
    xt = h.reshape(T, D)
    pg = jax.nn.softmax(jnp.einsum('td,dg->tg', xt, w_rg, preferred_element_type=jnp.float32), axis=-1)
    g_sel = jnp.argmax(pg, axis=-1)
    p_sel = jnp.take_along_axis(pg, g_sel[:, None], axis=1)
    le = jnp.einsum('td,de->te', xt, w_re, preferred_element_type=jnp.float32).reshape(T, N_GROUPS, EXPERTS_PER_GROUP)
    le_sel = jnp.take_along_axis(le, g_sel[:, None, None], axis=1)[:, 0]
    pe = jax.nn.softmax(le_sel, axis=-1)
    top_p, top_i = lax.top_k(pe, TOP_K)
    top_p = top_p / jnp.sum(top_p, axis=-1, keepdims=True)
    gate = p_sel * top_p
    eid = g_sel[:, None] * EXPERTS_PER_GROUP + top_i
    A = T * TOP_K
    flat_e = eid.reshape(A)
    flat_tok = jnp.repeat(jnp.arange(T, dtype=jnp.int32), TOP_K)
    flat_w = gate.reshape(A)
    order = jnp.argsort(flat_e)
    se = flat_e[order]
    counts = jnp.bincount(flat_e, length=N_EXPERTS)
    starts = jnp.cumsum(counts) - counts
    pcounts = (counts + MOE_BLOCK - 1) // MOE_BLOCK * MOE_BLOCK
    pends = jnp.cumsum(pcounts)
    pstarts = pends - pcounts
    dest = pstarts[se] + (jnp.arange(A, dtype=jnp.int32) - starts[se])
    P = (A + MOE_BLOCK - 1) // MOE_BLOCK * MOE_BLOCK + N_EXPERTS * MOE_BLOCK
    nb = P // MOE_BLOCK
    tok_sorted = flat_tok[order]
    x_pad = jnp.zeros((P, D), h.dtype).at[dest].set(xt[tok_sorted])
    blk_e = jnp.minimum(jnp.searchsorted(pends, jnp.arange(nb, dtype=pends.dtype) * MOE_BLOCK, side='right'), N_EXPERTS - 1)

    def expert_block(args):
        xb, e = args
        return (jax.nn.silu(xb @ w_g[e]) * (xb @ w_u[e])) @ w_d[e]

    y_pad = lax.map(expert_block, (x_pad.reshape(nb, MOE_BLOCK, D), blk_e)).reshape(P, D)
    contrib = (y_pad[dest] * flat_w[order][:, None]).astype(h.dtype)
    y = jnp.zeros((T, D), h.dtype).at[tok_sorted].add(contrib)
    return y.reshape(B, S, D)

def _layer(x, g_mix, w_in, ret_log_decay, ret_gn_g, mla_q_norm_g, w_q_up, mla_kv_norm_g, w_kv_up,
           w_out, g_ffn, w_router_group, w_router_expert, w_exp_gate, w_exp_up, w_exp_down):
    B, S, _ = x.shape
    h = _rmsnorm(x, g_mix)
    proj = jnp.einsum('bsd,de->bse', h, w_in)
    sizes = [H_RET * DK_RET, H_RET * DK_RET, H_RET * DV_RET, H_RET * DV_RET, MLA_Q_RANK, MLA_KV_RANK, MLA_ROPE]
    cuts = []
    acc = 0
    for sz in sizes[:-1]:
        acc += sz
        cuts.append(acc)
    rq, rk, rv, rg, cq, ckv, kr = jnp.split(proj, cuts, axis=-1)
    cos_r, sin_r = _rope_tables(S, DK_RET)
    q = _apply_rope(rq.reshape(B, S, H_RET, DK_RET), cos_r, sin_r)
    k = _apply_rope(rk.reshape(B, S, H_RET, DK_RET), cos_r, sin_r) * (DK_RET ** -0.5)
    v = rv.reshape(B, S, H_RET, DV_RET)
    ret = _retention_bidir(q, k, v, ret_log_decay)
    mu = jnp.mean(ret, axis=-1, keepdims=True)
    var = jnp.mean(jnp.square(ret - mu), axis=-1, keepdims=True)
    ret = ((ret - mu) * lax.rsqrt(var + EPS)).reshape(B, S, H_RET * DV_RET) * ret_gn_g.astype(jnp.float32)
    ret_out = (jax.nn.silu(rg.astype(jnp.float32)) * ret).astype(x.dtype)
    cos_m, sin_m = _rope_tables(S, MLA_ROPE)
    qh = jnp.einsum('bsr,re->bse', _rmsnorm(cq, mla_q_norm_g), w_q_up).reshape(B, S, H_MLA, MLA_NOPE + MLA_ROPE)
    qn = qh[..., :MLA_NOPE]
    qr = _apply_rope(qh[..., MLA_NOPE:], cos_m, sin_m)
    kvh = jnp.einsum('bsr,re->bse', _rmsnorm(ckv, mla_kv_norm_g), w_kv_up).reshape(B, S, H_MLA, MLA_NOPE + MLA_V)
    kn = kvh[..., :MLA_NOPE]
    vm = kvh[..., MLA_NOPE:]
    krr = _apply_rope(kr.reshape(B, S, 1, MLA_ROPE), cos_m, sin_m)[:, :, 0]
    mla_out = _mla_attention(qn, qr, kn, krr, vm)
    mix = jnp.concatenate([ret_out, mla_out], axis=-1)
    x = x + jnp.einsum('bse,ed->bsd', mix, w_out)
    x = x + _hier_moe(_rmsnorm(x, g_ffn), w_router_group, w_router_expert, w_exp_gate, w_exp_up, w_exp_down)
    return x

def setup_inputs(seed: int = 0) -> dict:
    key = jax.random.key(seed)
    ks = jax.random.split(key, 20)
    f32 = jnp.float32
    nrm = lambda k, shape, scale: jax.random.normal(k, shape, f32) * scale
    base_decay = -(5.0 + jnp.arange(H_RET, dtype=f32)) * math.log(2.0)
    return {
        'x_prompt': nrm(ks[0], (BATCH, SEQ, D_MODEL), 1.0),
        'x_sample': nrm(ks[1], (DEC_BATCH, DEC_SEQ, D_MODEL), 1.0),
        'g_mix': 1.0 + nrm(ks[2], (DEPTH, D_MODEL), 0.01),
        'w_in': nrm(ks[3], (DEPTH, D_MODEL, D_IN), D_MODEL ** -0.5),
        'ret_log_decay': base_decay[None, None, :] + nrm(ks[4], (DEPTH, 2, H_RET), 0.1),
        'ret_gn_g': 1.0 + nrm(ks[5], (DEPTH, H_RET * DV_RET), 0.01),
        'mla_q_norm_g': 1.0 + nrm(ks[6], (DEPTH, MLA_Q_RANK), 0.01),
        'w_q_up': nrm(ks[7], (DEPTH, MLA_Q_RANK, H_MLA * (MLA_NOPE + MLA_ROPE)), MLA_Q_RANK ** -0.5),
        'mla_kv_norm_g': 1.0 + nrm(ks[8], (DEPTH, MLA_KV_RANK), 0.01),
        'w_kv_up': nrm(ks[9], (DEPTH, MLA_KV_RANK, H_MLA * (MLA_NOPE + MLA_V)), MLA_KV_RANK ** -0.5),
        'w_out': nrm(ks[10], (DEPTH, D_MIX, D_MODEL), D_MIX ** -0.5),
        'g_ffn': 1.0 + nrm(ks[11], (DEPTH, D_MODEL), 0.01),
        'w_router_group': nrm(ks[12], (DEPTH, D_MODEL, N_GROUPS), D_MODEL ** -0.5),
        'w_router_expert': nrm(ks[13], (DEPTH, D_MODEL, N_EXPERTS), D_MODEL ** -0.5),
        'w_exp_gate': nrm(ks[14], (DEPTH, N_EXPERTS, D_MODEL, D_EXPERT), D_MODEL ** -0.5),
        'w_exp_up': nrm(ks[15], (DEPTH, N_EXPERTS, D_MODEL, D_EXPERT), D_MODEL ** -0.5),
        'w_exp_down': nrm(ks[16], (DEPTH, N_EXPERTS, D_EXPERT, D_MODEL), D_EXPERT ** -0.5),
        'g_final': 1.0 + nrm(ks[17], (D_MODEL,), 0.01),
    }

def reference(x_prompt, x_sample, g_mix, w_in, ret_log_decay, ret_gn_g, mla_q_norm_g, w_q_up,
              mla_kv_norm_g, w_kv_up, w_out, g_ffn, w_router_group, w_router_expert,
              w_exp_gate, w_exp_up, w_exp_down, g_final):
    def trunk(x):
        for l in range(DEPTH):
            x = _layer(x, g_mix[l], w_in[l], ret_log_decay[l], ret_gn_g[l], mla_q_norm_g[l], w_q_up[l],
                       mla_kv_norm_g[l], w_kv_up[l], w_out[l], g_ffn[l], w_router_group[l],
                       w_router_expert[l], w_exp_gate[l], w_exp_up[l], w_exp_down[l])
        return _rmsnorm(x, g_final)

    y_prompt = trunk(x_prompt)
    y_sample = trunk(x_sample)
    return (y_prompt, y_sample)


_drawn_inputs = setup_inputs


def setup_inputs(seed=0):
    import zlib

    import numpy as np

    out = dict(_drawn_inputs(seed))
    spreads = {}
    factors = {'g_mix': 3.03,
     'ret_gn_g': 5.763,
     'mla_q_norm_g': 8.0,
     'mla_kv_norm_g': 7.256,
     'g_ffn': 3.097,
     'g_final': 5.744}
    for name, (base, spread) in spreads.items():
        noise = np.random.default_rng([zlib.crc32(name.encode()), seed]).standard_normal(out[name].shape)
        drawn = base * np.exp(spread * noise) if base else spread * noise
        out[name] = __import__('jax').numpy.asarray(drawn.astype(out[name].dtype))
    for name, factor in factors.items():
        out[name] = (out[name] * factor).astype(out[name].dtype)
    return out
```

```python
from contextlib import ExitStack

import numpy as np
import concourse.bass as bass
from concourse import mybir

F32 = mybir.dt.float32
F32R = mybir.dt.float32r
BF16 = mybir.dt.bfloat16
I32 = mybir.dt.int32
U32 = mybir.dt.uint32
ALU = mybir.AluOpType
ACT = mybir.ActivationFunctionType
AX = mybir.AxisListType

P = 128
D = 1024
KD = D // P
SEQS = ((0, 4), (4, 8))
TILES = 12
TOK = TILES * P
HR, DR = 8, 64
RW = HR * DR
HM, NOPE, ROPE, VD = 4, 128, 64, 128
QRANK, KVRANK = 256, 128
CW = QRANK + KVRANK + ROPE
D_IN = 4 * RW + CW
EPS = 1e-6

M_QT, M_KT, M_K, M_V, M_G, M_CT = 0, 512, 1024, 1536, 2048, 2560
M_W = 3072


class Steps:

    def __init__(self, eng, sem, per):
        self.eng, self.sem, self.per, self.base, self.n = eng, sem, per, 0, 0

    def begin(self, i):
        self.base, self.n = i * self.per, 0

    def end(self):
        assert self.n == self.per, (self.n, self.per)

    def done(self, ins):
        ins.then_inc(self.sem, 1)
        self.n += 1

    def settle(self):
        self.eng.wait_ge(self.sem, self.base + self.n)

    def chain(self, ins):
        self.done(ins)
        self.settle()


def phase_sems(nc, ctx):
    sems = []

    def clear():
        nc.clear_and_free_semaphores(sems)
        nc.all_engine_barrier()

    ctx.callback(clear)
    return sems


def phase_sem(nc, sems, name):
    sems.append(nc.alloc_semaphore(name))
    return sems[-1]


def pairs(eng, tiles, body):
    for half in (0, 1):
        body(0, half, False)
    with eng.Fori(1, tiles // 2 - 1) as r:
        for half in (0, 1):
            body(r, half, False)
    for half in (0, 1):
        body(tiles // 2 - 1, half, half == 1)


def settle_waits(eng, tick):
    eng.sem_inc(tick, 1)


def three_passes(pe, out, st_hi, st_lo, mv_hi, mv_lo, first, last):
    pe.matmul(out, st_hi, mv_hi, start=first, stop=False)
    pe.matmul(out, st_hi, mv_lo, start=False, stop=False)
    return pe.matmul(out, st_lo, mv_hi, start=False, stop=last)


def phase_project(nc, x_all, w_in, g_mix, g_q, g_kv, rope, ident_d, mid):
    with ExitStack() as ctx:
        def sb(name, shape, dt=F32):
            return ctx.enter_context(nc.sbuf_tensor("a_" + name, shape, dt))

        sems = phase_sems(nc, ctx)

        def sem(name):
            return phase_sem(nc, sems, "a_" + name)

        w_hi, w_lo = sb("w_hi", [P, KD, D_IN], F32R), sb("w_lo", [P, KD, D_IN], F32R)
        x_sb = sb("x_sb", [P, 2, D])
        xT_hi, xT_lo = sb("xT_hi", [P, 2, KD, P], F32R), sb("xT_lo", [P, 2, KD, P], F32R)
        rec = sb("rec", [P, M_W])
        rope_sb = sb("rope_sb", [P, 2, 2, DR])
        part1, part2 = sb("part1", [P, RW]), sb("part2", [P, RW])
        q_tok, c_tok = sb("q_tok", [P, RW]), sb("c_tok", [P, 512])
        junk = sb("junk", [P, D], BF16)
        g_col = sb("g_col", [P, KD])
        gq_row, gkv_row = sb("gq_row", [P, QRANK]), sb("gkv_row", [P, KVRANK])
        ident = sb("ident", [P, P])
        eps = sb("eps", [P, 1])
        ssq = sb("ssq", [P, 3])
        root = sb("root", [P, 3])
        rstd = sb("rstd", [P, 3])
        WH = D_IN // 2
        stage = [rec[:, 0:WH], rec[:, WH:2 * WH]]

        pG = [ctx.enter_context(nc.psum_tensor(f"a_pG{g}", [P, 512], F32)) for g in range(5)]
        pX = [ctx.enter_context(nc.psum_tensor(f"a_pX{b}", [P, 512], F32)) for b in range(2)]
        pO = ctx.enter_context(nc.psum_tensor("a_pO", [P, 512], F32))
        C, Q, K, V, G = range(5)
        COLS = {Q: (0, RW), K: (RW, RW), V: (2 * RW, RW), G: (3 * RW, RW), C: (4 * RW, CW)}

        s_const = sem("const")
        s_raw = [sem("raw0"), sem("raw1")]
        s_whi, s_wlo = sem("whi"), sem("wlo")
        s_x = [sem("x0"), sem("x1")]
        s_sq = sem("sq")
        s_root, s_rstd = sem("root"), sem("rstd")
        s_croot = sem("croot")
        s_xt = sem("xt")
        s_hi, s_lo = sem("hi"), sem("lo")
        s_proj = sem("proj")
        s_ctok, s_qtok = sem("ctok"), sem("qtok")
        s_ev = {C: s_ctok, Q: s_qtok, K: sem("evk"), V: sem("evv"), G: sem("evg")}
        s_out = sem("out")
        s_outev = sem("outev")
        s_store = sem("store")
        s_dve = sem("dve")
        s_eps = sem("eps")

        block = ctx.enter_context(nc.Block())

        @block.sync
        def _(sp):
            sp.dma_start(x_sb[:, 0, :], x_all[0]).then_inc(s_x[0], 16)
            sp.dma_start(rope_sb[:, 0], rope[0]).then_inc(s_x[0], 16)
            sp.dma_start(ident[:], ident_d).then_inc(s_const, 16)
            sp.dma_start(g_col[:], g_mix.rearrange("(p k) -> p k", k=KD)).then_inc(s_const, 16)
            sp.dma_start(gq_row[:], g_q.partition_broadcast(P)).then_inc(s_const, 16)
            sp.dma_start(gkv_row[:], g_kv.partition_broadcast(P)).then_inc(s_const, 16)
            w_v = w_in.rearrange("(p k) n -> p k n", k=KD)
            for c in range(2 * KD):
                if c >= 2:
                    sp.wait_ge(s_wlo, c - 1)
                sp.dma_start(stage[c % 2], w_v[:, c // 2, (c % 2) * WH:(c % 2 + 1) * WH]).then_inc(s_raw[c % 2], 16)

            def tile(r, half, last):
                t = 2 * r + half
                if not last:
                    sp.wait_ge(s_xt, 2 * t)
                    sp.wait_ge(s_sq, t)
                    sp.wait_ge(s_ev[K], t)
                    sp.wait_ge(s_const, 64)
                    sp.dma_start(x_sb[:, 1 - half, :], x_all[t + 1]).then_inc(s_x[1 - half], 16)
                    sp.dma_start(rope_sb[:, 1 - half], rope[t + 1]).then_inc(s_x[1 - half], 16)
                sp.wait_ge(s_outev, 3 * (t + 1))
                sp.wait_ge(s_ev[V], t + 1)
                sp.wait_ge(s_ev[G], t + 1)
                sp.wait_ge(s_ev[K], t + 1)
                sp.wait_ge(s_const, 64)
                sp.dma_start(mid[t], rec[:]).then_inc(s_store, 16)

            pairs(sp, TILES, tile)
            sp.wait_ge(s_store, 16 * TILES)

        @block.gpsimd
        def _(pool):
            nc.gpsimd.memset(eps[:], EPS).then_inc(s_eps, 1)

        @block.tensor
        def _(pe):
            def transpose_x(n, half):
                for b in range(2):
                    for j in range(4):
                        k = 4 * b + j
                        ins = pe.transpose(pX[b][:, j * P:(j + 1) * P], x_sb[:, half, k:D:KD], ident[:])
                    ins.then_inc(s_xt, 1)

            pe.wait_ge(s_const, 64)
            pe.wait_ge(s_x[0], 32)
            transpose_x(0, 0)

            def project(r, half, g, i):
                t = 2 * r + half
                pe.wait_ge(s_ev[g], t)
                c0, w = COLS[g]
                for k in range(KD):
                    ins = three_passes(pe, pG[g][:, 0:w], xT_hi[:, half, k, :], xT_lo[:, half, k, :],
                                       w_hi[:, k, c0:c0 + w], w_lo[:, k, c0:c0 + w], k == 0, k == KD - 1)
                ins.then_inc(s_proj, 1)

            def transpose_out(r, half, i, src):
                t = 2 * r + half
                pe.wait_ge(s_outev, 3 * t + i)
                for j in range(4):
                    ins = pe.transpose(pO[:, j * P:(j + 1) * P], src[:, j * P:(j + 1) * P], ident[:])
                ins.then_inc(s_out, 1)

            def tile(r, half, last):
                t = 2 * r + half
                pe.wait_ge(s_lo, 2 * (t + 1))
                project(r, half, C, 0)
                project(r, half, Q, 1)
                pe.wait_ge(s_ctok, t + 1)
                transpose_out(r, half, 0, c_tok)
                project(r, half, K, 2)
                pe.wait_ge(s_qtok, t + 1)
                transpose_out(r, half, 1, q_tok)
                project(r, half, V, 3)
                pe.wait_ge(s_ev[K], t + 1)
                transpose_out(r, half, 2, rec[:, M_K:M_K + RW])
                if not last:
                    pe.wait_ge(s_x[1 - half], 32 * (r + 1 + half))
                    transpose_x(t + 1, 1 - half)
                project(r, half, G, 4)

            pe.wait_ge(s_wlo, 2 * KD)
            pairs(pe, TILES, tile)

        @block.scalar
        def _(act):
            def hi_of_x(n, half):
                for b in range(2):
                    act.wait_ge(s_xt, 2 * n + b + 1)
                    for j in range(4):
                        k = 4 * b + j
                        ins = nc.scalar.activation(xT_hi[:, half, k, :], pX[b][:, j * P:(j + 1) * P],
                                                   ACT.Copy, scale=g_col[:, k:k + 1])
                    ins.then_inc(s_hi, 1)

            act.wait_ge(s_const, 64)
            hi_of_x(0, 0)
            for c in range(2 * KD):
                act.wait_ge(s_raw[c % 2], 16 * (c // 2 + 1))
                nc.scalar.copy(w_hi[:, c // 2, (c % 2) * WH:(c % 2 + 1) * WH], stage[c % 2]).then_inc(s_whi, 1)
            act.wait_ge(s_eps, 1)

            def take_out(r, half, i, col):
                t = 2 * r + half
                act.wait_ge(s_out, 3 * t + i + 1)
                nc.scalar.copy(rec[:, col:col + 512], pO[:]).then_inc(s_outev, 1)

            def tile(r, half, last):
                t = 2 * r + half
                act.wait_ge(s_x[half], 32 * (r + 1))
                act.wait_ge(s_rstd, 2 * t)
                nc.scalar.activation(junk[:], x_sb[:, half, :], ACT.Square, accum_out=ssq[:, 0:1]).then_inc(s_sq, 1)
                act.wait_ge(s_sq, t + 1)
                nc.scalar.activation(root[:, 0:1], ssq[:, 0:1], ACT.Sqrt, bias=eps[:, 0:1],
                                     scale=1.0 / D).then_inc(s_root, 1)
                act.wait_ge(s_rstd, 2 * t + 1)
                act.wait_ge(s_proj, 5 * t + 1)
                nc.scalar.activation(junk[:, 0:QRANK], pG[C][:, 0:QRANK], ACT.Square, scale=rstd[:, 0:1],
                                     accum_out=ssq[:, 1:2])
                nc.scalar.activation(junk[:, QRANK:QRANK + KVRANK], pG[C][:, QRANK:QRANK + KVRANK], ACT.Square,
                                     scale=rstd[:, 0:1], accum_out=ssq[:, 2:3]).then_inc(s_croot, 1)
                act.wait_ge(s_croot, 2 * t + 1)
                nc.scalar.activation(root[:, 1:2], ssq[:, 1:2], ACT.Sqrt, bias=eps[:, 0:1], scale=1.0 / QRANK)
                nc.scalar.activation(root[:, 2:3], ssq[:, 2:3], ACT.Sqrt, bias=eps[:, 0:1],
                                     scale=1.0 / KVRANK).then_inc(s_croot, 1)
                act.wait_ge(s_store, 16 * t)
                take_out(r, half, 0, M_CT)
                take_out(r, half, 1, M_QT)
                act.wait_ge(s_proj, 5 * t + 4)
                nc.scalar.activation(rec[:, M_V:M_V + RW], pG[V][:], ACT.Copy, scale=rstd[:, 0:1]).then_inc(s_ev[V], 1)
                take_out(r, half, 2, M_KT)
                if not last:
                    hi_of_x(t + 1, 1 - half)
                act.wait_ge(s_proj, 5 * t + 5)
                nc.scalar.activation(rec[:, M_G:M_G + RW], pG[G][:], ACT.Copy, scale=rstd[:, 0:1]).then_inc(s_ev[G], 1)

            pairs(act, TILES, tile)

        @block.vector
        def _(dve):
            steps = Steps(dve, s_dve, 5)

            def lo_of_x(n, half):
                for b in range(2):
                    dve.wait_ge(s_hi, 2 * n + b + 1)
                    for j in range(4):
                        k = 4 * b + j
                        ins = nc.vector.scalar_tensor_tensor(
                            out=xT_lo[:, half, k, :], in0=pX[b][:, j * P:(j + 1) * P], scalar=g_col[:, k:k + 1],
                            in1=xT_hi[:, half, k, :].bitcast(F32), op0=ALU.mult, op1=ALU.subtract)
                    ins.then_inc(s_lo, 1)

            dve.wait_ge(s_const, 64)
            lo_of_x(0, 0)
            for c in range(2 * KD):
                dve.wait_ge(s_whi, c + 1)
                span = slice((c % 2) * WH, (c % 2 + 1) * WH)
                nc.vector.tensor_tensor(w_lo[:, c // 2, span], stage[c % 2], w_hi[:, c // 2, span].bitcast(F32),
                                        ALU.subtract).then_inc(s_wlo, 1)

            def rotate(out, src, heads, half, p1, p2):
                cos = rope_sb[:, half, 0, :]
                sin = rope_sb[:, half, 1, :]
                hw = DR // 2
                x3, a3, b3 = (y.rearrange("p (h d) -> p h d", h=heads) for y in (src, p1, p2))
                c3 = cos.unsqueeze(1).broadcast_to([P, heads, DR])
                s3 = sin.unsqueeze(1).broadcast_to([P, heads, DR])
                nc.vector.scalar_tensor_tensor(out=a3, in0=x3, scalar=rstd[:, 0:1], in1=c3,
                                               op0=ALU.mult, op1=ALU.mult)
                nc.vector.scalar_tensor_tensor(out=b3[:, :, 0:hw], in0=x3[:, :, hw:DR], scalar=rstd[:, 0:1],
                                               in1=s3[:, :, 0:hw], op0=ALU.mult, op1=ALU.mult)
                steps.chain(nc.vector.scalar_tensor_tensor(
                    out=b3[:, :, hw:DR], in0=x3[:, :, 0:hw], scalar=rstd[:, 0:1], in1=s3[:, :, hw:DR],
                    op0=ALU.mult, op1=ALU.mult))
                return nc.vector.tensor_tensor(out, p1, p2, ALU.add)

            def tile(r, half, last):
                t = 2 * r + half
                steps.begin(t)
                dve.wait_ge(s_root, t + 1)
                dve.wait_ge(s_proj, 5 * t)
                dve.wait_ge(s_ev[V], t)
                dve.wait_ge(s_ev[G], t)
                nc.vector.reciprocal(rstd[:, 0:1], root[:, 0:1]).then_inc(s_rstd, 1)
                dve.wait_ge(s_rstd, 2 * t + 1)
                dve.wait_ge(s_croot, 2 * t + 2)
                dve.wait_ge(s_out, 3 * t)
                steps.chain(nc.vector.reciprocal(rstd[:, 1:3], root[:, 1:3]))
                nc.vector.tensor_scalar(rstd[:, 1:3], rstd[:, 1:3], rstd[:, 0:1], None, ALU.mult).then_inc(s_rstd, 1)
                dve.wait_ge(s_rstd, 2 * t + 2)
                nc.vector.scalar_tensor_tensor(out=c_tok[:, 0:QRANK], in0=pG[C][:, 0:QRANK], scalar=rstd[:, 1:2],
                                               in1=gq_row[:], op0=ALU.mult, op1=ALU.mult)
                nc.vector.scalar_tensor_tensor(out=c_tok[:, QRANK:QRANK + KVRANK],
                                               in0=pG[C][:, QRANK:QRANK + KVRANK], scalar=rstd[:, 2:3],
                                               in1=gkv_row[:], op0=ALU.mult, op1=ALU.mult)
                kr = c_tok[:, QRANK + KVRANK:QRANK + KVRANK + ROPE]
                steps.chain(rotate(kr, pG[C][:, QRANK + KVRANK:CW], 1, half, part1[:, 0:ROPE], part2[:, 0:ROPE]))
                nc.vector.tensor_copy(c_tok[:, CW:CW + ROPE], kr).then_inc(s_ctok, 1)
                dve.wait_ge(s_proj, 5 * t + 2)
                dve.wait_ge(s_ctok, t + 1)
                dve.wait_ge(s_out, 3 * t)
                ins = rotate(q_tok[:], pG[Q][:], HR, half, part1[:], part2[:])
                ins.then_inc(s_qtok, 1)
                dve.wait_ge(s_qtok, t + 1)
                dve.wait_ge(s_proj, 5 * t + 3)
                dve.wait_ge(s_store, 16 * t)
                ins = rotate(rec[:, M_K:M_K + RW], pG[K][:], HR, half, part1[:], part2[:])
                ins.then_inc(s_ev[K], 1)
                dve.wait_ge(s_ev[K], t + 1)
                if not last:
                    lo_of_x(t + 1, 1 - half)
                steps.end()

            pairs(dve, TILES, tile)


def phase_retention(nc, mid, log_decay, gn_g, dist_d, index_d, ident_d, mixT):
    with ExitStack() as ctx:
        def sb(name, shape, dt=F32):
            return ctx.enter_context(nc.sbuf_tensor("b_" + name, shape, dt))

        sems = phase_sems(nc, ctx)

        def sem(name):
            return phase_sem(nc, sems, "b_" + name)

        PR = HR // 2
        ident, dist = sb("ident", [P, P]), sb("dist", [P, 2, P])
        index = sb("index", [P, 4])
        rate = sb("rate", [P, 2, HR])
        gn_row = sb("gn_row", [P, RW])
        eps = sb("eps", [P, 1])
        dmat = sb("dmat", [P, 2, PR, P])
        dtmp = sb("dtmp", [P, P])
        wk, wq = sb("wk", [P, 2, HR]), sb("wq", [P, 2, HR])
        dec = sb("dec", [P, 2, PR])
        kv = sb("kv", [P, 2, 2 * RW])
        vw = sb("vw", [P, 2, HR, 2, DR])
        own = sb("own", [P, TILES, PR, 2, DR])
        run = sb("run", [P, TILES, PR, 2, DR])
        cur = sb("cur", [P, 2, PR, 2 * DR])
        stmp = sb("stmp", [P, 2, PR, DR])
        qk = sb("qk", [P, 2, 2 * RW])
        vg = sb("vg", [P, 2, 2 * RW])
        sc = sb("sc", [P, 2, PR, P])
        fa, fb = sb("fa", [P, HR, DR]), sb("fb", [P, HR, DR])
        fab, o_t, ctr, sq = (sb(n, [P, HR, DR]) for n in ("fab", "o_t", "ctr", "sq"))
        gate, gate2, nrm, ret = (sb(n, [P, HR, DR]) for n in ("gate", "gate2", "nrm", "ret"))
        mu, var, rt, rs = (sb(n, [P, HR]) for n in ("mu", "var", "rt", "rs"))
        retT = sb("retT", [P, 2, RW])

        pst = [ctx.enter_context(nc.psum_tensor(f"b_pst{i}", [P, 512], F32)) for i in range(2)]
        psc = ctx.enter_context(nc.psum_tensor("b_psc", [P, 2, 512], F32))
        pin = ctx.enter_context(nc.psum_tensor("b_pin", [P, 2, 512], F32))
        pno = ctx.enter_context(nc.psum_tensor("b_pno", [P, 512], F32))
        ptr = ctx.enter_context(nc.psum_tensor("b_ptr", [P, 512], F32))

        s_const, s_eps = sem("const"), sem("eps")
        s_rate, s_lin, s_tab, s_dm = sem("rate"), sem("lin"), sem("tab"), sem("dm")
        s_kv = [sem("kv0"), sem("kv1")]
        s_vw, s_own, s_ownev = sem("vw"), sem("own"), sem("ownev")
        s_run, s_cur = sem("run"), sem("cur")
        s_qk = [sem("qk0"), sem("qk1")]
        s_sc, s_scev, s_in, s_inev, s_no, s_noev = (sem(n) for n in ("sc", "scev", "in", "inev", "no", "noev"))
        s_fab, s_ctr, s_sq, s_var, s_rt, s_rs, s_silu, s_ret = (
            sem(n) for n in ("fab", "ctr", "sq", "var", "rt", "rs", "silu", "ret"))
        s_gate, s_nrm = sem("gate"), sem("nrm")
        s_tr, s_trev, s_store = sem("tr"), sem("trev"), [sem("store0"), sem("store1")]
        s_d1, s_d2, s_d3 = sem("d1"), sem("d2"), sem("d3")

        block = ctx.enter_context(nc.Block())

        @block.sync
        def _(sp):
            sp.dma_start(ident[:], ident_d).then_inc(s_const, 16)
            sp.dma_start(dist[:], dist_d).then_inc(s_const, 16)
            sp.dma_start(index[:], index_d).then_inc(s_const, 16)
            sp.dma_start(rate[:].rearrange("p a h -> p (a h)"),
                         log_decay.rearrange("a h -> (a h)").partition_broadcast(P)).then_inc(s_const, 16)
            sp.dma_start(gn_row[:], gn_g.partition_broadcast(P)).then_inc(s_const, 16)

            def load_kv(r, half, last):
                t = 2 * r + half
                if not (isinstance(r, int) and r == 0):
                    sp.wait_ge(s_own, t - 1)
                    sp.wait_ge(s_const, 80)
                sp.dma_start(kv[:, half, :], mid[t][:, M_K:M_K + 2 * RW]).then_inc(s_kv[half], 16)

            pairs(sp, TILES, load_kv)

            def load_qk(r, half, last):
                t = 2 * r + half
                if not (isinstance(r, int) and r == 0):
                    sp.wait_ge(s_noev, t - 1)
                    sp.wait_ge(s_silu, t - 1)
                    sp.wait_ge(s_const, 80)
                sp.dma_start(qk[:, half, :], mid[t][:, M_QT:M_QT + 2 * RW]).then_inc(s_qk[half], 16)
                sp.dma_start(vg[:, half, :], mid[t][:, M_V:M_V + 2 * RW]).then_inc(s_qk[half], 16)

            pairs(sp, TILES, load_qk)

        @block.gpsimd
        def _(pool):
            nc.gpsimd.memset(eps[:], EPS).then_inc(s_eps, 1)

            def tile(r, half, last):
                t = 2 * r + half
                pool.wait_ge(s_inev, t + 1)
                pool.wait_ge(s_noev, t)
                nc.gpsimd.tensor_tensor(fab[:], fa[:], fb[:], ALU.add).then_inc(s_fab, 1)
                pool.wait_ge(s_silu, t + 1)
                nc.gpsimd.tensor_tensor(gate2[:], gate[:], gn_row[:].rearrange("p (h d) -> p h d", h=HR),
                                        ALU.mult).then_inc(s_gate, 1)
                pool.wait_ge(s_rs, t + 1)
                pool.wait_ge(s_gate, t + 1)
                nc.gpsimd.tensor_tensor(nrm[:], ctr[:], rs[:].unsqueeze(2).broadcast_to([P, HR, DR]),
                                        ALU.mult).then_inc(s_nrm, 1)
                pool.wait_ge(s_nrm, t + 1)
                pool.wait_ge(s_tr, t)
                nc.gpsimd.tensor_tensor(ret[:], nrm[:], gate2[:], ALU.mult).then_inc(s_ret, 1)
                if True:
                    pool.wait_ge(s_trev, t + 1)
                    pool.dma_start(mixT[t][:, 0:RW], retT[:, half, :]).then_inc(s_store[half], 16)

            pool.wait_ge(s_const, 80)
            pairs(pool, TILES, tile)
            pool.wait_ge(s_store[0], 16 * TILES // 2)
            pool.wait_ge(s_store[1], 16 * TILES // 2)

        @block.tensor
        def _(pe):
            def own_state(r, half, last):
                t = 2 * r + half
                pe.wait_ge(s_vw, t + 1)
                pe.wait_ge(s_ownev, t - 1 if not (isinstance(r, int) and r == 0) else 0)
                for h in range(HR):
                    pair, odd = h // 2, h % 2
                    ins = pe.matmul(pst[half][odd * DR:(odd + 1) * DR, pair * P:(pair + 1) * P],
                                    kv[:, half, h * DR:(h + 1) * DR],
                                    vw[:, half, h].rearrange("p a d -> p (a d)"), start=True, stop=True)
                ins.then_inc(s_own, 1)

            pairs(pe, TILES, own_state)

            def scores(t, r, half):
                pe.wait_ge(s_qk[half], 32 * (r + 1))
                pe.wait_ge(s_scev, t)
                for h in range(HR):
                    pair, odd = h // 2, h % 2
                    rows, cols = slice(odd * DR, (odd + 1) * DR), slice(pair * P, (pair + 1) * P)
                    ins = pe.matmul(psc[:, odd, cols], qk[rows, half, RW + pair * P:RW + (pair + 1) * P],
                                    qk[rows, half, cols], start=True, stop=True)
                ins.then_inc(s_sc, 1)

            def inter(t, r, half):
                pe.wait_ge(s_inev, t)
                pe.wait_ge(s_cur, t + 1)
                for h in range(HR):
                    pair, odd = h // 2, h % 2
                    rows, cols = slice(odd * DR, (odd + 1) * DR), slice(pair * P, (pair + 1) * P)
                    ins = pe.matmul(pin[:, odd, cols], qk[rows, half, cols],
                                    cur[rows, half, pair, :], start=True, stop=True)
                ins.then_inc(s_in, 1)

            scores(0, 0, 0)
            inter(0, 0, 0)

            def tile(r, half, last):
                t = 2 * r + half
                pe.wait_ge(s_scev, t + 1)
                pe.wait_ge(s_noev, t)
                for h in range(HR):
                    ins = pe.matmul(pno[:, h * DR:(h + 1) * DR], sc[:, h % 2, h // 2, :],
                                    vg[:, half, h * DR:(h + 1) * DR], start=True, stop=True)
                ins.then_inc(s_no, 1)
                if not last:
                    scores(t + 1, r + half, 1 - half)
                    inter(t + 1, r + half, 1 - half)
                pe.wait_ge(s_ret, t + 1)
                pe.wait_ge(s_trev, t)
                for j in range(4):
                    ins = pe.transpose(ptr[:, j * P:(j + 1) * P],
                                       ret[:, 2 * j:2 * j + 2].rearrange("p h d -> p (h d)"), ident[:])
                ins.then_inc(s_tr, 1)

            pairs(pe, TILES, tile)

        @block.scalar
        def _(act):
            act.wait_ge(s_const, 80)
            nc.scalar.activation(rate[:], rate[:], ACT.Exp).then_inc(s_rate, 1)
            act.wait_ge(s_rate, 1)
            for d in range(2):
                nc.scalar.activation(wk[:, d, :], rate[:, d, :], ACT.Exp, scale=index[:, d:d + 1])
                nc.scalar.activation(wq[:, d, :], rate[:, d, :], ACT.Exp, scale=index[:, 2 + d:3 + d])
                for odd in range(2):
                    rows = slice(odd * DR, (odd + 1) * DR)
                    ins = nc.scalar.activation(dec[rows, d, :], rate[rows, d, odd:HR:2], ACT.Exp, scale=-float(P))
            ins.then_inc(s_tab, 1)
            for h in range(HR):
                act.wait_ge(s_lin, 2 * h + 2)
                nc.scalar.activation(dmat[:, h % 2, h // 2, :], dmat[:, h % 2, h // 2, :], ACT.Exp,
                                     scale=-1.0).then_inc(s_dm, 1)

            def own_state(r, half, last):
                t = 2 * r + half
                act.wait_ge(s_own, t + 1)
                nc.scalar.copy(own[:, t].rearrange("p a b d -> p (a b d)"), pst[half][:]).then_inc(s_ownev, 1)

            pairs(act, TILES, own_state)
            act.wait_ge(s_eps, 1)

            def fetch_states(t, half):
                nc.scalar.copy(cur[:, half].rearrange("p a d -> p (a d)"),
                               run[:, t].rearrange("p a b d -> p (a b d)")).then_inc(s_cur, 1)

            act.wait_ge(s_run, 1)
            fetch_states(0, 0)

            def tile(r, half, last):
                t = 2 * r + half
                if not last:
                    act.wait_ge(s_in, t)
                    fetch_states(t + 1, 1 - half)
                act.wait_ge(s_qk[half], 32 * (r + 1))
                act.wait_ge(s_gate, t)
                nc.scalar.activation(gate[:].rearrange("p h d -> p (h d)"), vg[:, half, RW:2 * RW],
                                     ACT.Silu).then_inc(s_silu, 1)
                act.wait_ge(s_ctr, t + 1)
                nc.scalar.activation(sq[:], ctr[:], ACT.Square).then_inc(s_sq, 1)
                act.wait_ge(s_var, t + 1)
                nc.scalar.activation(rt[:], var[:], ACT.Sqrt, bias=eps[:, 0:1], scale=1.0 / DR).then_inc(s_rt, 1)
                act.wait_ge(s_tr, t + 1)
                act.wait_ge(s_store[half], 16 * r)
                nc.scalar.copy(retT[:, half, :], ptr[:]).then_inc(s_trev, 1)

            pairs(act, TILES, tile)

        @block.vector
        def _(dve):
            dve.wait_ge(s_rate, 1)
            dve.wait_ge(s_const, 80)
            for h in range(HR):
                if h:
                    dve.wait_ge(s_lin, 2 * h)
                nc.vector.tensor_scalar(dtmp[:], dist[:, 0], rate[:, 0, h:h + 1], None, ALU.mult).then_inc(s_lin, 1)
                dve.wait_ge(s_lin, 2 * h + 1)
                nc.vector.scalar_tensor_tensor(out=dmat[:, h % 2, h // 2, :], in0=dist[:, 1],
                                               scalar=rate[:, 1, h:h + 1], in1=dtmp[:], op0=ALU.mult,
                                               op1=ALU.add).then_inc(s_lin, 1)
            dve.wait_ge(s_dm, HR)
            nc.vector.tensor_scalar(dmat[:], dmat[:], float(DR) ** -0.5, None, ALU.mult).then_inc(s_d1, 1)
            dve.wait_ge(s_tab, 1)
            nc.vector.tensor_scalar(wk[:], wk[:], float(DR) ** -0.5, None, ALU.mult).then_inc(s_d1, 1)
            dve.wait_ge(s_d1, 2)

            def weigh(r, half, last):
                t = 2 * r + half
                dve.wait_ge(s_kv[half], 16 * (r + 1))
                dve.wait_ge(s_own, t - 1 if not (isinstance(r, int) and r == 0) else 0)
                v3 = kv[:, half, RW:2 * RW].rearrange("p (h d) -> p h d", h=HR)
                for d in range(2):
                    ins = nc.vector.tensor_tensor(vw[:, half, :, d, :], v3,
                                                  wk[:, d, :].unsqueeze(2).broadcast_to([P, HR, DR]), ALU.mult)
                ins.then_inc(s_vw, 1)

            pairs(dve, TILES, weigh)

            dve.wait_ge(s_ownev, TILES)
            scan = Steps(dve, s_d2, 0)
            for first, tiles in SEQS:
                nc.vector.memset(run[:, first, :, 0, :], 0.0)
                scan.chain(nc.vector.memset(run[:, first + tiles - 1, :, 1, :], 0.0))
                for i in range(tiles - 1):
                    steps2 = ((0, first + i, first + i + 1), (1, first + tiles - 1 - i, first + tiles - 2 - i))
                    for d, a, _ in steps2:
                        ins = nc.vector.tensor_tensor(stmp[:, d], run[:, a, :, d, :],
                                                      dec[:, d, :].unsqueeze(2).broadcast_to([P, PR, DR]), ALU.mult)
                    scan.chain(ins)
                    for d, a, b in steps2:
                        ins = nc.vector.tensor_tensor(run[:, b, :, d, :], stmp[:, d], own[:, a, :, d, :], ALU.add)
                    scan.chain(ins)
            nc.vector.tensor_copy(stmp[:, 0, 0, 0:1], dec[:, 0, 0:1]).then_inc(s_run, 1)

            steps = Steps(dve, s_d3, 3)
            by_half = "p (a b) d -> p b a d"

            def tile(r, half, last):
                t = 2 * r + half
                steps.begin(t)
                dve.wait_ge(s_sc, t + 1)
                dve.wait_ge(s_no, t)
                for odd in range(2):
                    ins = nc.vector.tensor_tensor(sc[:, odd].rearrange("p a i -> p (a i)"), psc[:, odd, :],
                                                  dmat[:, odd].rearrange("p a i -> p (a i)"), ALU.mult)
                ins.then_inc(s_scev, 1)
                dve.wait_ge(s_in, t + 1)
                dve.wait_ge(s_fab, t)
                for d, f in ((0, fa), (1, fb)):
                    for odd in range(2):
                        src = pin[:, odd, :].rearrange("p (a b d) -> p a b d", a=PR, b=2)[:, :, d, :]
                        ins = nc.vector.tensor_tensor(f[:, odd:HR:2, :], src,
                                                      wq[:, d, odd:HR:2].unsqueeze(2).broadcast_to([P, PR, DR]),
                                                      ALU.mult)
                ins.then_inc(s_inev, 1)
                dve.wait_ge(s_no, t + 1)
                dve.wait_ge(s_fab, t + 1)
                nc.vector.tensor_tensor(o_t[:].rearrange("p h d -> p (h d)"), pno[:],
                                        fab[:].rearrange("p h d -> p (h d)"), ALU.add).then_inc(s_noev, 1)
                dve.wait_ge(s_noev, t + 1)
                steps.chain(nc.vector.tensor_reduce(mu[:], o_t[:], AX.X, ALU.add))
                steps.chain(nc.vector.tensor_scalar(mu[:], mu[:], -1.0 / DR, None, ALU.mult))
                dve.wait_ge(s_nrm, t)
                nc.vector.tensor_tensor(ctr[:], o_t[:], mu[:].unsqueeze(2).broadcast_to([P, HR, DR]),
                                        ALU.add).then_inc(s_ctr, 1)
                dve.wait_ge(s_sq, t + 1)
                nc.vector.tensor_reduce(var[:], sq[:], AX.X, ALU.add).then_inc(s_var, 1)
                dve.wait_ge(s_rt, t + 1)
                nc.vector.reciprocal(rs[:], rt[:]).then_inc(s_rs, 1)
                steps.chain(nc.vector.tensor_copy(dtmp[:, 0:1], index[:, 0:1]))
                steps.end()

            pairs(dve, TILES, tile)


def phase_latent(nc, tag, first, tiles, mid, w_q_up, w_kv_up, rope, ident_d, mixT):
    S = tiles * P
    QB, TB = tiles // 4, 4
    SCALE = float(NOPE + ROPE) ** -0.5
    with ExitStack() as ctx:
        def sb(name, shape, dt=F32):
            return ctx.enter_context(nc.sbuf_tensor(f"{tag}_{name}", shape, dt))

        sems = phase_sems(nc, ctx)

        def sem(name):
            return phase_sem(nc, sems, f"{tag}_{name}")

        ident = sb("ident", [P, P])
        angles = sb("angles", [P, tiles, 2, DR])
        ct = sb("ct", [P, 2, 512])
        c_hi, c_lo = sb("c_hi", [P, tiles, 512], F32R), sb("c_lo", [P, tiles, 512], F32R)
        wq_sb, wkv_sb = sb("wq_sb", [P, 2, NOPE + ROPE]), sb("wkv_sb", [P, NOPE + VD])
        wq_hi, wq_lo = sb("wq_hi", [P, 2, NOPE + ROPE], F32R), sb("wq_lo", [P, 2, NOPE + ROPE], F32R)
        wkv_hi, wkv_lo = sb("wkv_hi", [P, NOPE + VD], F32R), sb("wkv_lo", [P, NOPE + VD], F32R)
        kn_hi, kn_lo = sb("kn_hi", [P, S], F32R), sb("kn_lo", [P, S], F32R)
        qn_hi, qn_lo = sb("qn_hi", [P, S], F32R), sb("qn_lo", [P, S], F32R)
        qr_hi, qr_lo = sb("qr_hi", [ROPE, S], F32R), sb("qr_lo", [ROPE, S], F32R)
        v_hi, v_lo = sb("v_hi", [P, tiles, VD], F32R), sb("v_lo", [P, tiles, VD], F32R)
        part1, part2 = (sb(n, [P, tiles, ROPE]) for n in ("part1", "part2"))
        qr_tok = sb("qr_tok", [P, tiles, P])
        p_sb, pn_sb = sb("p_sb", [P, 2, S]), sb("pn_sb", [P, 2, S])
        pT_hi, pT_lo = sb("pT_hi", [P, 2, tiles, TB * P], F32R), sb("pT_lo", [P, 2, tiles, TB * P], F32R)
        oT = sb("oT", [P, 2, TB * P])
        peak, nbias, total, share = (sb(n, [P, 2]) for n in ("peak", "nbias", "total", "share"))

        ps = [ctx.enter_context(nc.psum_tensor(f"{tag}_ps{i}", [P, 1024], F32)) for i in range(2)]
        pt = ctx.enter_context(nc.psum_tensor(f"{tag}_pt", [P, 1024], F32))
        pr = ctx.enter_context(nc.psum_tensor(f"{tag}_pr", [P, 512], F32))
        po = ctx.enter_context(nc.psum_tensor(f"{tag}_po", [P, 512], F32))

        s_const = sem("const")
        s_ct = [sem("ct0"), sem("ct1")]
        s_chi, s_clo = sem("chi"), sem("clo")
        s_w, s_whi, s_wlo = sem("w"), sem("whi"), sem("wlo")
        s_kn, s_knhi, s_knlo = sem("kn"), sem("knhi"), sem("knlo")
        s_qn, s_qnhi, s_qnlo = sem("qn"), sem("qnhi"), sem("qnlo")
        s_v, s_vhi, s_vlo = sem("v"), sem("vhi"), sem("vlo")
        s_qr, s_qrtok, s_qrt, s_qrhi, s_qrlo = sem("qr"), sem("qrtok"), sem("qrt"), sem("qrhi"), sem("qrlo")
        s_s, s_peak, s_exp, s_share, s_pn = sem("s"), sem("peak"), sem("exp"), sem("share"), sem("pn")
        s_pt, s_pthi, s_ptlo = sem("pt"), sem("pthi"), sem("ptlo")
        s_o, s_oev, s_store = sem("o"), sem("oev"), [sem("store0"), sem("store1")]
        s_d = sem("d")

        block = ctx.enter_context(nc.Block())
        wq_v = w_q_up.rearrange("(k p) (h n) -> h p k n", p=P, h=HM)
        wkv_v = w_kv_up.rearrange("p (h n) -> h p n", h=HM)
        HALVES = [(b * 512, min(512, S - b * 512)) for b in range((S + 511) // 512)]
        NB = len(HALVES)
        PAIRS = tiles // 2

        def heads(eng, body):
            body(0)
            with eng.Fori(1, HM) as h:
                body(h)

        def q_tiles():
            return [(qb, j) for qb in range(QB) for j in range(TB)]

        @block.sync
        def _(sp):
            sp.dma_start(ident[:], ident_d).then_inc(s_const, 16)
            sp.dma_start(angles[:].rearrange("p t a d -> p t (a d)"),
                         rope[first:first + tiles].rearrange("t p a d -> p t (a d)")).then_inc(s_const, 16)
            sp.dma_start(wq_sb[:], wq_v[0]).then_inc(s_w, 16)
            sp.dma_start(wkv_sb[:], wkv_v[0]).then_inc(s_w, 16)
            for t in range(tiles):
                if t >= 2:
                    sp.wait_ge(s_clo, t - 1)
                sp.dma_start(ct[:, t % 2, :], mid[first + t][:, M_CT:M_CT + 512]).then_inc(s_ct[t % 2], 16)
            with sp.Fori(1, HM) as h:
                sp.wait_ge(s_wlo, 2 * h)
                sp.dma_start(wq_sb[:], wq_v[h]).then_inc(s_w, 16)
                sp.dma_start(wkv_sb[:], wkv_v[h]).then_inc(s_w, 16)

        @block.gpsimd
        def _(pool):
            mix_v = mixT.rearrange("t p (e i) -> e p t i", e=8)

            def head(h):
                for qb in range(QB):
                    n = h * QB + qb
                    half = (qb if QB == 2 else 0)
                    pool.wait_ge(s_oev, n + 1)
                    pool.dma_start(mix_v[4 + h][:, first + qb * TB:first + (qb + 1) * TB, :],
                                   oT[:, half, :].rearrange("p (t i) -> p t i", t=TB)).then_inc(s_store[half], 16)

            heads(pool, head)
            pool.wait_ge(s_store[0], 16 * HM)
            if QB == 2:
                pool.wait_ge(s_store[1], 16 * HM)

        @block.tensor
        def _(pe):
            pe.wait_ge(s_const, 32)

            def head(h):
                pe.wait_ge(s_wlo, 2 * h + 2)
                if isinstance(h, int):
                    pe.wait_ge(s_clo, tiles)
                pe.wait_ge(s_exp, tiles * h)
                for b, (c0, w) in enumerate(HALVES):
                    cols = slice(c0 // P, (c0 + w) // P)
                    ins = three_passes(pe, ps[0][:, c0:c0 + w], wkv_hi[:, 0:NOPE], wkv_lo[:, 0:NOPE],
                                       c_hi[:, cols, 2 * P:3 * P], c_lo[:, cols, 2 * P:3 * P], True, True)
                    ins.then_inc(s_kn, 1)
                for b, (c0, w) in enumerate(HALVES):
                    cols = slice(c0 // P, (c0 + w) // P)
                    for k in range(2):
                        ins = three_passes(pe, ps[1][:, c0:c0 + w], wq_hi[:, k, 0:NOPE], wq_lo[:, k, 0:NOPE],
                                           c_hi[:, cols, k * P:(k + 1) * P], c_lo[:, cols, k * P:(k + 1) * P],
                                           k == 0, k == 1)
                    ins.then_inc(s_qn, 1)
                pe.wait_ge(s_ptlo, NB * tiles * h + NB * h + NB * h)
                for t in range(tiles):
                    for k in range(2):
                        ins = three_passes(pe, pr[:, t * ROPE:(t + 1) * ROPE],
                                           c_hi[:, t, k * P:(k + 1) * P], c_lo[:, t, k * P:(k + 1) * P],
                                           wq_hi[:, k, NOPE:], wq_lo[:, k, NOPE:], k == 0, k == 1)
                ins.then_inc(s_qr, 1)
                for t in range(tiles):
                    ins = three_passes(pe, pt[:, t * P:(t + 1) * P],
                                       c_hi[:, t, 2 * P:3 * P], c_lo[:, t, 2 * P:3 * P],
                                       wkv_hi[:, NOPE:], wkv_lo[:, NOPE:], True, True)
                    if t % 4 == 3:
                        ins.then_inc(s_v, 1)
                pe.wait_ge(s_qrtok, h + 1)
                for b in range(NB):
                    pe.wait_ge(s_ptlo, NB * tiles * h + 2 * NB * h + b + 1)
                    for j in range(4):
                        t = 4 * b + j
                        ins = pe.transpose(pt[:, t * P:(t + 1) * P], qr_tok[:, t, :], ident[:])
                    ins.then_inc(s_qrt, 1)

                def scores(i):
                    t = i
                    for c0, w in HALVES:
                        cols = slice(c0 // P, (c0 + w) // P)
                        q = slice(t * P, (t + 1) * P)
                        three_passes(pe, ps[i % 2][:, c0:c0 + w], qn_hi[:, q], qn_lo[:, q],
                                     kn_hi[:, c0:c0 + w], kn_lo[:, c0:c0 + w], True, False)
                        ins = three_passes(pe, ps[i % 2][:, c0:c0 + w], qr_hi[:, q], qr_lo[:, q],
                                           c_hi[0:ROPE, cols, 3 * P:4 * P], c_lo[0:ROPE, cols, 3 * P:4 * P],
                                           False, True)
                    ins.then_inc(s_s, 1)

                pe.wait_ge(s_knlo, NB * (h + 1))
                pe.wait_ge(s_qnlo, NB * (h + 1))
                pe.wait_ge(s_ptlo, NB * tiles * h + 2 * NB * (h + 1))
                scores(0)
                for i, (qb, j) in enumerate(q_tiles()):
                    if i + 1 < tiles:
                        if i >= 1:
                            pe.wait_ge(s_exp, tiles * h + i)
                        scores(i + 1)
                    pe.wait_ge(s_pn, tiles * h + i + 1)
                    for b in range(NB):
                        pe.wait_ge(s_ptlo, NB * tiles * h + 2 * NB * (h + 1) + max(0, NB * (i - 1) + b + 1))
                        for k in range(4):
                            t = 4 * b + k
                            ins = pe.transpose(pt[:, t * P:(t + 1) * P], pn_sb[:, i % 2, t * P:(t + 1) * P], ident[:])
                        ins.then_inc(s_pt, 1)
                    if j == TB - 1:
                        pe.wait_ge(s_ptlo, NB * tiles * h + 2 * NB * (h + 1) + NB * (i + 1))
                        pe.wait_ge(s_oev, QB * h + qb)
                        for k in range(tiles):
                            ins = three_passes(pe, po[:], v_hi[:, k, :], v_lo[:, k, :],
                                               pT_hi[:, qb % 2, k, :], pT_lo[:, qb % 2, k, :], k == 0, k == tiles - 1)
                        ins.then_inc(s_o, 1)

            heads(pe, head)

        @block.scalar
        def _(act):
            for t in range(tiles):
                act.wait_ge(s_ct[t % 2], 16 * (t // 2 + 1))
                nc.scalar.copy(c_hi[:, t, :], ct[:, t % 2, :]).then_inc(s_chi, 1)

            def head(h):
                act.wait_ge(s_w, 32 * (h + 1))
                act.wait_ge(s_o, QB * h)
                nc.scalar.copy(wq_hi[:], wq_sb[:]).then_inc(s_whi, 1)
                nc.scalar.copy(wkv_hi[:], wkv_sb[:]).then_inc(s_whi, 1)
                for b, (c0, w) in enumerate(HALVES):
                    act.wait_ge(s_kn, NB * h + b + 1)
                    nc.scalar.copy(kn_hi[:, c0:c0 + w], ps[0][:, c0:c0 + w]).then_inc(s_knhi, 1)
                for b, (c0, w) in enumerate(HALVES):
                    act.wait_ge(s_qn, NB * h + b + 1)
                    nc.scalar.copy(qn_hi[:, c0:c0 + w], ps[1][:, c0:c0 + w]).then_inc(s_qnhi, 1)
                for b, (c0, w) in enumerate(HALVES):
                    act.wait_ge(s_v, NB * h + b + 1)
                    nc.scalar.copy(v_hi[:].rearrange("p t d -> p (t d)")[:, c0:c0 + w],
                                   pt[:, c0:c0 + w]).then_inc(s_vhi, 1)
                for b, (c0, w) in enumerate(HALVES):
                    act.wait_ge(s_qrt, NB * h + b + 1)
                    nc.scalar.copy(qr_hi[:, c0:c0 + w], pt[0:ROPE, c0:c0 + w]).then_inc(s_qrhi, 1)

                def take(i):
                    qb, j = i // TB, i % TB
                    for b in range(NB):
                        act.wait_ge(s_pt, NB * tiles * h + NB * i + b + 1)
                        nc.scalar.copy(pT_hi[:, qb % 2, 4 * b:4 * b + 4, j * P:(j + 1) * P],
                                       pt[:, b * 512:(b + 1) * 512].rearrange("p (k i) -> p k i", k=4)
                                       ).then_inc(s_pthi, 1)
                    if j == TB - 1:
                        act.wait_ge(s_o, QB * h + qb + 1)
                        act.wait_ge(s_store[qb], 16 * h)
                        nc.scalar.copy(oT[:, qb, :], po[:]).then_inc(s_oev, 1)

                for i in range(tiles):
                    act.wait_ge(s_peak, tiles * h + i + 1)
                    nc.scalar.activation(p_sb[:, i % 2, :], ps[i % 2][:, 0:S], ACT.Exp, bias=nbias[:, i % 2:i % 2 + 1],
                                         scale=SCALE, accum_out=total[:, i % 2:i % 2 + 1]).then_inc(s_exp, 1)
                    if i >= 1:
                        take(i - 1)
                    act.wait_ge(s_share, tiles * h + i + 1)
                    nc.scalar.activation(pn_sb[:, i % 2, :], p_sb[:, i % 2, :], ACT.Copy,
                                         scale=share[:, i % 2:i % 2 + 1]).then_inc(s_pn, 1)
                take(tiles - 1)

            heads(act, head)

        @block.vector
        def _(dve):
            dve.wait_ge(s_const, 32)
            nc.vector.memset(qr_tok[:, :, ROPE:], 0.0)
            for t in range(tiles):
                dve.wait_ge(s_chi, t + 1)
                nc.vector.tensor_tensor(c_lo[:, t, :], ct[:, t % 2, :], c_hi[:, t, :].bitcast(F32),
                                        ALU.subtract).then_inc(s_clo, 1)
            steps = Steps(dve, s_d, 2 + tiles)

            def head(h):
                steps.begin(h)
                dve.wait_ge(s_whi, 2 * h + 1)
                nc.vector.tensor_tensor(wq_lo[:], wq_sb[:], wq_hi[:].bitcast(F32), ALU.subtract).then_inc(s_wlo, 1)
                dve.wait_ge(s_whi, 2 * h + 2)
                nc.vector.tensor_tensor(wkv_lo[:], wkv_sb[:], wkv_hi[:].bitcast(F32), ALU.subtract).then_inc(s_wlo, 1)
                for b, (c0, w) in enumerate(HALVES):
                    dve.wait_ge(s_knhi, NB * h + b + 1)
                    nc.vector.tensor_tensor(kn_lo[:, c0:c0 + w], ps[0][:, c0:c0 + w],
                                            kn_hi[:, c0:c0 + w].bitcast(F32), ALU.subtract).then_inc(s_knlo, 1)
                dve.wait_ge(s_qr, h + 1)
                dve.wait_ge(s_qrt, NB * h)
                x3 = pr[:, 0:tiles * ROPE].rearrange("p (t d) -> p t d", t=tiles)
                hw = ROPE // 2
                nc.vector.tensor_tensor(part1[:], x3, angles[:, :, 0, :], ALU.mult)
                nc.vector.tensor_tensor(part2[:, :, 0:hw], x3[:, :, hw:ROPE], angles[:, :, 1, 0:hw], ALU.mult)
                steps.chain(nc.vector.tensor_tensor(part2[:, :, hw:ROPE], x3[:, :, 0:hw], angles[:, :, 1, hw:ROPE],
                                                    ALU.mult))
                nc.vector.tensor_tensor(qr_tok[:, :, 0:ROPE], part1[:], part2[:], ALU.add).then_inc(s_qrtok, 1)
                dve.wait_ge(s_qrtok, h + 1)
                for b, (c0, w) in enumerate(HALVES):
                    dve.wait_ge(s_qnhi, NB * h + b + 1)
                    nc.vector.tensor_tensor(qn_lo[:, c0:c0 + w], ps[1][:, c0:c0 + w],
                                            qn_hi[:, c0:c0 + w].bitcast(F32), ALU.subtract).then_inc(s_qnlo, 1)
                for b, (c0, w) in enumerate(HALVES):
                    dve.wait_ge(s_vhi, NB * h + b + 1)
                    flat = slice(c0, c0 + w)
                    nc.vector.tensor_tensor(v_lo[:].rearrange("p t d -> p (t d)")[:, flat], pt[:, flat],
                                            v_hi[:].rearrange("p t d -> p (t d)")[:, flat].bitcast(F32),
                                            ALU.subtract).then_inc(s_ptlo, 1)
                for b, (c0, w) in enumerate(HALVES):
                    dve.wait_ge(s_qrhi, NB * h + b + 1)
                    nc.vector.tensor_tensor(qr_lo[:, c0:c0 + w], pt[0:ROPE, c0:c0 + w],
                                            qr_hi[:, c0:c0 + w].bitcast(F32), ALU.subtract).then_inc(s_ptlo, 1)

                def take(i):
                    qb, j = i // TB, i % TB
                    for b in range(NB):
                        dve.wait_ge(s_pthi, NB * tiles * h + NB * i + b + 1)
                        nc.vector.tensor_tensor(pT_lo[:, qb % 2, 4 * b:4 * b + 4, j * P:(j + 1) * P],
                                                pt[:, b * 512:(b + 1) * 512].rearrange("p (k i) -> p k i", k=4),
                                                pT_hi[:, qb % 2, 4 * b:4 * b + 4, j * P:(j + 1) * P].bitcast(F32),
                                                ALU.subtract).then_inc(s_ptlo, 1)

                for i in range(tiles):
                    one = slice(i % 2, i % 2 + 1)
                    dve.wait_ge(s_s, tiles * h + i + 1)
                    steps.chain(nc.vector.tensor_reduce(peak[:, one], ps[i % 2][:, 0:S], AX.X, ALU.max))
                    nc.vector.tensor_scalar(nbias[:, one], peak[:, one], -SCALE, None, ALU.mult).then_inc(s_peak, 1)
                    if i >= 1:
                        take(i - 1)
                    dve.wait_ge(s_exp, tiles * h + i + 1)
                    nc.vector.reciprocal(share[:, one], total[:, one]).then_inc(s_share, 1)
                take(tiles - 1)
                steps.chain(nc.vector.tensor_copy(part1[:, 0, 0:1], part2[:, 0, 0:1]))
                steps.end()

            heads(dve, head)


NE, NG, EPG = 32, 4, 8
FE = 512
ROWS = TILES * P
MORE = 2 * ROWS // (P + 1)
AHEAD = 5
NBLK = NE + MORE + AHEAD
NEVER = 1.0e30
NOWHERE = 1 << 20


def phase_mix(nc, mixT, x_all, w_out, g_ffn, w_rg, w_re, ident_d, route_d, blocks_d, x_mid, h_rows, table,
              gates, blocks, n_pairs, s_tick, s_tock):
    with ExitStack() as ctx:
        def sb(name, shape, dt=F32):
            return ctx.enter_context(nc.sbuf_tensor("d_" + name, shape, dt))

        sems = phase_sems(nc, ctx)

        def sem(name):
            return phase_sem(nc, sems, "d_" + name)

        ident = sb("ident", [P, P])
        route = sb("route", [P, 2 * NE + 2 * P])
        e_id, e_grp = route[:, 0:NE], route[:, NE:2 * NE]
        before, ones = route[:, 2 * NE:2 * NE + P], route[:, 2 * NE + P:]
        stage = sb("stage", [P, 2, D])
        w_hi, w_lo = sb("w_hi", [P, KD, D], F32R), sb("w_lo", [P, KD, D], F32R)
        w_r = sb("w_r", [P, KD, NG + NE])
        g_row = sb("g_row", [P, D])
        eps = sb("eps", [P, 1])
        mx, xr = sb("mx", [P, 2, D]), sb("xr", [P, 2, D])
        mT_hi, mT_lo = sb("mT_hi", [P, 2, D], F32R), sb("mT_lo", [P, 2, D], F32R)
        x2, h_sb, hT = sb("x2", [P, 2, D]), sb("h_sb", [P, 2, D]), sb("hT", [P, D])
        junk = sb("junk", [P, D], BF16)
        ssq, root, rstd = sb("ssq", [P, 1]), sb("root", [P, 1]), sb("rstd", [P, 1])
        g8, g8max, e8 = sb("g8", [P, 8]), sb("g8max", [P, 8]), sb("e8", [P, 8])
        g8i, e8i = sb("g8i", [P, 8], U32), sb("e8i", [P, 8], U32)
        gf, ef = sb("gf", [P, 1]), sb("ef", [P, 2])
        mask, pen, lem = sb("mask", [P, NE]), sb("pen", [P, NE]), sb("lem", [P, NE])
        hot = sb("hot", [P, 3, NE])
        seen = sb("seen", [P, NE])
        prod = sb("prod", [P, NE])
        place, spot = sb("place", [P, 2]), sb("spot", [P, 2])
        spot_i = sb("spot_i", [P, 2, 2], I32)
        entry = sb("entry", [P, 2, 2, 2], I32)
        empty = sb("empty", [P, NE * ROWS // P * 2], I32)
        glog, elog = sb("glog", [P, TILES, NG]), sb("elog", [P, TILES, 2])
        gm, gz, ge, gd, gr = (sb(n, [P, TILES]) for n in ("gm", "gz", "ge", "gd", "gr"))
        gx = sb("gx", [P, TILES, NG])
        many_i, many, incl = sb("many_i", [P, NE], I32), sb("many", [P, NE]), sb("incl", [P, NE])
        step_no = sb("step_no", [P, MORE + AHEAD])
        upto, uses = sb("upto", [P, MORE + AHEAD, NE]), sb("uses", [P, MORE + AHEAD, NE])
        who, gone, base = (sb(n, [P, MORE + AHEAD]) for n in ("who", "gone", "base"))

        po = [ctx.enter_context(nc.psum_tensor(f"d_po{i}", [P, 1024], F32)) for i in range(2)]
        pt = ctx.enter_context(nc.psum_tensor("d_pt", [P, 1024], F32))
        pr = ctx.enter_context(nc.psum_tensor("d_pr", [P, 512], F32))
        pp = ctx.enter_context(nc.psum_tensor("d_pp", [P, 512], F32))

        s_const, s_init, s_zero, s_clear = sem("const"), sem("init"), sem("zero"), sem("clear")
        s_raw = [sem("raw0"), sem("raw1")]
        s_whi, s_wlo = sem("whi"), sem("wlo")
        s_in = [sem("in0"), sem("in1")]
        s_mhi, s_mlo, s_po, s_x2, s_sq, s_root, s_rstd, s_h = (
            sem(n) for n in ("mhi", "mlo", "po", "x2", "sq", "root", "rstd", "h"))
        s_ht, s_htev, s_r, s_rev, s_hot, s_pp, s_spot = (sem(n) for n in ("ht", "htev", "r", "rev", "hot", "pp", "spot"))
        s_keep = [sem("keep0"), sem("keep1")]
        s_tab = [sem("tab0"), sem("tab1")]
        s_d, s_gexp, s_count, s_g = sem("d"), sem("gexp"), sem("count"), sem("g")

        block = ctx.enter_context(nc.Block())

        @block.sync
        def _(sp):
            sp.dma_start(ident[:], ident_d).then_inc(s_const, 16)
            sp.dma_start(route[:], route_d).then_inc(s_const, 16)
            sp.dma_start(g_row[:], g_ffn.partition_broadcast(P)).then_inc(s_const, 16)
            sp.dma_start(w_r[:, :, 0:NG], w_rg.rearrange("(p k) e -> p k e", k=KD)).then_inc(s_const, 16)
            sp.dma_start(w_r[:, :, NG:], w_re.rearrange("(p k) e -> p k e", k=KD)).then_inc(s_const, 16)
            sp.dma_start(blocks[:].rearrange("p a n -> p (a n)"), blocks_d).then_inc(s_const, 16)
            sp.dma_start(mx[:, 0, :], mixT[0]).then_inc(s_in[0], 16)
            sp.dma_start(xr[:, 0, :], x_all[0]).then_inc(s_in[0], 16)
            w_v = w_out.rearrange("(k p) n -> p k n", p=P)
            for k in range(KD):
                if k >= 2:
                    sp.wait_ge(s_wlo, k - 1)
                sp.dma_start(stage[:, k % 2, :], w_v[:, k, :]).then_inc(s_raw[k % 2], 16)

            def tile(r, half, last):
                t = 2 * r + half
                if not last:
                    if not (isinstance(r, int) and r == 0 and half == 0):
                        sp.wait_ge(s_mlo, t)
                        sp.wait_ge(s_x2, t)
                        sp.wait_ge(s_const, 96)
                    sp.dma_start(mx[:, 1 - half, :], mixT[t + 1]).then_inc(s_in[1 - half], 16)
                    sp.dma_start(xr[:, 1 - half, :], x_all[t + 1]).then_inc(s_in[1 - half], 16)

            pairs(sp, TILES, tile)

        @block.gpsimd
        def _(pool):
            nc.gpsimd.memset(eps[:], EPS).then_inc(s_init, 1)
            nc.gpsimd.memset(empty[:], NOWHERE).then_inc(s_zero, 1)
            nc.gpsimd.iota(entry[:, :, :, 0], pattern=[[P, 2], [0, 2]], base=0, channel_multiplier=1)
            nc.gpsimd.iota(entry[:, :, :, 1], pattern=[[2 * P, 2], [1, 2]], base=0,
                           channel_multiplier=2).then_inc(s_init, 1)
            nc.gpsimd.iota(step_no[:], pattern=[[1, MORE + AHEAD]], base=0, channel_multiplier=0,
                           allow_small_or_imprecise_dtypes=True).then_inc(s_init, 1)
            pool.wait_ge(s_zero, 1)
            pool.dma_start(table.rearrange("(p n) a -> p (n a)", p=P), empty[:]).then_inc(s_clear, 16)
            pool.wait_ge(s_clear, 16)

            def tile(r, half, last):
                t = 2 * r + half
                pool.wait_ge(s_x2, t + 1)
                settle_waits(pool, s_tick)
                pool.dma_start(x_mid[t], x2[:, half, :]).then_inc(s_keep[half], 16)
                pool.wait_ge(s_h, t + 1)
                settle_waits(pool, s_tick)
                pool.dma_start(h_rows[t], h_sb[:, half, :]).then_inc(s_keep[half], 16)
                pool.wait_ge(s_spot, t + 1)
                settle_waits(pool, s_tick)
                for c in range(2):
                    pool.indirect_dma_start(out=table, out_offset=bass.IndirectOffsetOnAxis(
                        ap=spot_i[:, half, c:c + 1], axis=0), in_=entry[:, half, c, :],
                        in_offset=None).then_inc(s_tab[half], 16)

            pairs(pool, TILES, tile)
            for half in range(2):
                pool.wait_ge(s_keep[half], 16 * TILES)
                pool.wait_ge(s_tab[half], 16 * TILES)

        @block.tensor
        def _(pe):
            pe.wait_ge(s_const, 96)
            pe.wait_ge(s_wlo, KD)

            def project(t, half):
                pe.wait_ge(s_mlo, t + 1)
                pe.wait_ge(s_x2, t - 1 if not isinstance(t, int) else max(0, t - 1))
                for b in range(2):
                    for k in range(KD):
                        rows = slice(k * P, (k + 1) * P)
                        ins = three_passes(pe, po[half][:, b * 512:(b + 1) * 512], mT_hi[:, half, rows],
                                           mT_lo[:, half, rows], w_hi[:, k, b * 512:(b + 1) * 512],
                                           w_lo[:, k, b * 512:(b + 1) * 512], k == 0, k == KD - 1)
                ins.then_inc(s_po, 1)

            project(0, 0)

            def tile(r, half, last):
                t = 2 * r + half
                if not last:
                    project(t + 1, 1 - half)
                pe.wait_ge(s_h, t + 1)
                pe.wait_ge(s_htev, 2 * t)
                for b in range(2):
                    for j in range(4):
                        k = 4 * b + j
                        ins = pe.transpose(pt[:, k * P:(k + 1) * P], h_sb[:, half, k:D:KD], ident[:])
                    ins.then_inc(s_ht, 1)
                pe.wait_ge(s_htev, 2 * t + 2)
                pe.wait_ge(s_rev, t)
                for k in range(KD):
                    ins = pe.matmul(pr[:, 0:NG + NE], hT[:, k * P:(k + 1) * P], w_r[:, k, :],
                                    start=k == 0, stop=k == KD - 1)
                ins.then_inc(s_r, 1)
                pe.wait_ge(s_hot, t + 1)
                pe.matmul(pp[:, 0:NE], before, hot[:, 2, :], start=True, stop=False)
                pe.matmul(pp[:, 0:NE], ones, seen[:], start=False, stop=True).then_inc(s_pp, 1)

            pairs(pe, TILES, tile)
            pe.wait_ge(s_spot, TILES + 1)
            pe.matmul(pp[:, 0:NE], ones, seen[:], start=True, stop=True).then_inc(s_count, 1)

        @block.scalar
        def _(act):
            act.wait_ge(s_init, 1)
            for k in range(KD):
                act.wait_ge(s_raw[k % 2], 16 * (k // 2 + 1))
                nc.scalar.copy(w_hi[:, k, :], stage[:, k % 2, :]).then_inc(s_whi, 1)

            def split(t, r, half):
                act.wait_ge(s_in[half], 32 * (r + 1))
                act.wait_ge(s_po, t - 1 if not isinstance(t, int) else max(0, t - 1))
                nc.scalar.copy(mT_hi[:, half, :], mx[:, half, :]).then_inc(s_mhi, 1)

            split(0, 0, 0)
            split(1, 0, 1)

            def tile(r, half, last):
                t = 2 * r + half
                act.wait_ge(s_x2, t + 1)
                act.wait_ge(s_rstd, t)
                nc.scalar.activation(junk[:], x2[:, half, :], ACT.Square, accum_out=ssq[:]).then_inc(s_sq, 1)
                act.wait_ge(s_sq, t + 1)
                nc.scalar.activation(root[:], ssq[:], ACT.Sqrt, bias=eps[:], scale=1.0 / D).then_inc(s_root, 1)
                for b in range(2):
                    act.wait_ge(s_ht, 2 * t + b + 1)
                    act.wait_ge(s_r, t)
                    nc.scalar.copy(hT[:, b * 512:(b + 1) * 512], pt[:, b * 512:(b + 1) * 512]).then_inc(s_htev, 1)
                if not (isinstance(r, int) and r == TILES // 2 - 1):
                    split(t + 2, r + 1, half)

            pairs(act, TILES, tile)
            act.wait_ge(s_gexp, 1)
            nc.scalar.activation(gx[:], gx[:], ACT.Exp).then_inc(s_g, 1)
            nc.scalar.activation(gd[:], gd[:], ACT.Exp).then_inc(s_g, 1)

        @block.vector
        def _(dve):
            dve.wait_ge(s_const, 96)
            nc.vector.memset(g8[:], -NEVER)
            nc.vector.memset(seen[:], 0.0)
            dve.wait_ge(s_init, 3)
            for k in range(KD):
                dve.wait_ge(s_whi, k + 1)
                nc.vector.tensor_tensor(w_lo[:, k, :], stage[:, k % 2, :], w_hi[:, k, :].bitcast(F32),
                                        ALU.subtract).then_inc(s_wlo, 1)

            def split(t, half):
                dve.wait_ge(s_mhi, t + 1)
                nc.vector.tensor_tensor(mT_lo[:, half, :], mx[:, half, :], mT_hi[:, half, :].bitcast(F32),
                                        ALU.subtract).then_inc(s_mlo, 1)

            split(0, 0)
            split(1, 1)
            steps = Steps(dve, s_d, 15)

            def tile(r, half, last):
                t = 2 * r + half
                steps.begin(t)
                dve.wait_ge(s_po, t + 1)
                dve.wait_ge(s_keep[half], 32 * r)
                nc.vector.tensor_tensor(x2[:, half, :], po[half][:], xr[:, half, :], ALU.add).then_inc(s_x2, 1)
                dve.wait_ge(s_root, t + 1)
                nc.vector.reciprocal(rstd[:], root[:]).then_inc(s_rstd, 1)
                dve.wait_ge(s_rstd, t + 1)
                nc.vector.scalar_tensor_tensor(out=h_sb[:, half, :], in0=x2[:, half, :], scalar=rstd[:, 0:1],
                                               in1=g_row[:], op0=ALU.mult, op1=ALU.mult).then_inc(s_h, 1)
                if not (isinstance(r, int) and r == TILES // 2 - 1):
                    split(t + 2, half)
                dve.wait_ge(s_r, t + 1)
                nc.vector.tensor_copy(glog[:, t, :], pr[:, 0:NG])
                steps.chain(nc.vector.tensor_copy(g8[:, 0:NG], pr[:, 0:NG]))
                settle_waits(dve, s_tock)
                steps.chain(nc.vector.max(g8max[:], g8[:]))
                settle_waits(dve, s_tock)
                steps.chain(nc.vector.max_index(g8i[:], g8max[:], g8[:]))
                steps.chain(nc.vector.tensor_copy(gf[:], g8i[:, 0:1]))
                steps.chain(nc.vector.tensor_scalar(mask[:], e_grp, gf[:, 0:1], None, ALU.is_equal))
                nc.vector.tensor_tensor(lem[:], pr[:, NG:NG + NE], mask[:], ALU.mult).then_inc(s_rev, 1)
                dve.wait_ge(s_rev, t + 1)
                steps.chain(nc.vector.tensor_scalar(pen[:], mask[:], 1.0, NEVER, ALU.subtract, ALU.mult))
                steps.chain(nc.vector.tensor_tensor(lem[:], lem[:], pen[:], ALU.add))
                settle_waits(dve, s_tock)
                steps.chain(nc.vector.max(e8[:], lem[:]))
                settle_waits(dve, s_tock)
                steps.chain(nc.vector.max_index(e8i[:], e8[:], lem[:]))
                nc.vector.tensor_copy(elog[:, t, :], e8[:, 0:2])
                steps.chain(nc.vector.tensor_copy(ef[:], e8i[:, 0:2]))
                for c in range(2):
                    ins = nc.vector.tensor_scalar(hot[:, c, :], e_id, ef[:, c:c + 1], None, ALU.is_equal)
                steps.chain(ins)
                nc.vector.tensor_tensor(hot[:, 2, :], hot[:, 0, :], hot[:, 1, :], ALU.add).then_inc(s_hot, 1)
                dve.wait_ge(s_pp, t + 1)
                for c in range(2):
                    nc.vector.tensor_tensor(pen[:] if c else prod[:], hot[:, c, :], pp[:, 0:NE], ALU.mult)
                steps.chain(nc.vector.tensor_tensor(seen[:], seen[:], hot[:, 2, :], ALU.add))
                for c in range(2):
                    ins = nc.vector.tensor_reduce(place[:, c:c + 1], pen[:] if c else prod[:], AX.X, ALU.add)
                steps.chain(ins)
                steps.chain(nc.vector.scalar_tensor_tensor(out=spot[:], in0=ef[:], scalar=float(ROWS), in1=place[:],
                                                           op0=ALU.mult, op1=ALU.add))
                dve.wait_ge(s_tab[half], 32 * r)
                if not (isinstance(r, int) and r == 0):
                    nc.vector.tensor_scalar(entry[:, half, :, 0], entry[:, half, :, 0], float(2 * P), None, ALU.add)
                    nc.vector.tensor_scalar(entry[:, half, :, 1], entry[:, half, :, 1], float(4 * P), None, ALU.add)
                steps.chain(nc.vector.tensor_copy(spot_i[:, half, :], spot[:]))
                nc.vector.tensor_copy(pen[:, 0:1], spot[:, 0:1]).then_inc(s_spot, 1)
                steps.end()

            pairs(dve, TILES, tile)
            tail = Steps(dve, s_gexp, 0)
            dve.wait_ge(s_spot, TILES)
            nc.vector.tensor_copy(prod[:, 0:1], spot[:, 0:1]).then_inc(s_spot, 1)
            nc.vector.tensor_reduce(gm[:], glog[:], AX.X, ALU.max).then_inc(s_zero, 1)
            dve.wait_ge(s_zero, 2)
            nc.vector.tensor_tensor(gx[:], glog[:], gm[:].unsqueeze(2).broadcast_to([P, TILES, NG]), ALU.subtract)
            nc.vector.tensor_tensor(gd[:], elog[:, :, 1], elog[:, :, 0], ALU.subtract).then_inc(s_gexp, 1)
            dve.wait_ge(s_g, 2)
            tail.n = 1
            nc.vector.tensor_reduce(gz[:], gx[:], AX.X, ALU.add)
            tail.chain(nc.vector.tensor_scalar(ge[:], gd[:], 1.0, None, ALU.add))
            tail.chain(nc.vector.tensor_tensor(ge[:], ge[:], gz[:], ALU.mult))
            tail.chain(nc.vector.reciprocal(gr[:], ge[:]))
            nc.vector.tensor_copy(gates[:, :, 0], gr[:])
            nc.vector.tensor_tensor(gates[:, :, 1], gr[:], gd[:], ALU.mult)
            dve.wait_ge(s_count, 1)
            tail.chain(nc.vector.tensor_scalar(many_i[:], pp[:, 0:NE], 1.0, 1.0, ALU.max, ALU.subtract))
            tail.chain(nc.vector.tensor_scalar(many_i[:], many_i[:], 7, None, ALU.logical_shift_right))
            tail.chain(nc.vector.tensor_copy(many[:], many_i[:]))
            tail.chain(nc.vector.tensor_tensor_scan(incl[:], ones[:, 0:NE], many[:], 0.0, ALU.mult, ALU.add))
            shape = [P, MORE + AHEAD, NE]
            tail.chain(nc.vector.tensor_tensor(upto[:], incl[:].unsqueeze(1).broadcast_to(shape),
                                               step_no[:].unsqueeze(2).broadcast_to(shape), ALU.is_le))
            nc.vector.tensor_reduce(who[:], upto[:], AX.X, ALU.add)
            tail.chain(nc.vector.tensor_tensor(uses[:], upto[:], many[:].unsqueeze(1).broadcast_to(shape), ALU.mult))
            nc.vector.tensor_reduce(gone[:], uses[:], AX.X, ALU.add)
            tail.chain(nc.vector.tensor_scalar(who[:], who[:], float(NE - 1), None, ALU.min))
            tail.chain(nc.vector.tensor_tensor(base[:], step_no[:], gone[:], ALU.subtract))
            tail.chain(nc.vector.tensor_scalar(base[:], base[:], 1.0, float(P), ALU.add, ALU.mult))
            tail.chain(nc.vector.scalar_tensor_tensor(out=base[:], in0=who[:], scalar=float(ROWS), in1=base[:],
                                                      op0=ALU.mult, op1=ALU.add))
            nc.vector.tensor_copy(blocks[:, 0, NE:], who[0:1, :])
            nc.vector.tensor_scalar(blocks[:, 1, NE:], base[0:1, :], float(NE * ROWS - P), None, ALU.min)
            tail.chain(nc.vector.tensor_scalar(many_i[:, 0:1], incl[:, NE - 1:NE], float(NE + 1), None, ALU.add))
            tail.chain(nc.vector.tensor_scalar(many_i[:, 0:1], many_i[:, 0:1], 1, None, ALU.logical_shift_right))
            nc.vector.tensor_copy(n_pairs[:, 0:1], many_i[0:1, 0:1])
            tail.chain(nc.vector.tensor_scalar(n_pairs[:, 1:2], many_i[0:1, 0:1], -1.0, None, ALU.add))


def phase_experts(nc, w_gate, w_up, w_down, ident_d, h_rows, table, y_rows, blocks, n_pairs, s_tick):
    KF = FE // P
    with ExitStack() as ctx:
        def sb(name, shape, dt=F32):
            return ctx.enter_context(nc.sbuf_tensor("e_" + name, shape, dt))

        sems = phase_sems(nc, ctx)

        def sem(name):
            return phase_sem(nc, sems, "e_" + name)

        ident = sb("ident", [P, P])
        raw = sb("raw", [P, 3, 4096])
        w_hi, w_lo = sb("w_hi", [P, 3, 4096], F32R), sb("w_lo", [P, 3, 4096], F32R)
        who = [sb(f"who{i}", [P, 2], I32) for i in range(2)]
        code = [sb(f"code{i}", [P, 1], I32) for i in range(2)]
        xg = [sb(f"xg{i}", [P, D]) for i in range(2)]
        xT_hi, xT_lo = sb("xT_hi", [P, D], F32R), sb("xT_lo", [P, D], F32R)
        act_g, h_sb = sb("act_g", [P, FE]), sb("h_sb", [P, FE])
        hT_hi, hT_lo = sb("hT_hi", [P, FE], F32R), sb("hT_lo", [P, FE], F32R)
        y_sb = [sb(f"y_sb{i}", [P, D]) for i in range(2)]

        pg, pu = (ctx.enter_context(nc.psum_tensor(f"e_{n}", [P, 512], F32)) for n in ("pg", "pu"))
        px = ctx.enter_context(nc.psum_tensor("e_px", [P, 1024], F32))
        ph = ctx.enter_context(nc.psum_tensor("e_ph", [P, 512], F32))
        py = ctx.enter_context(nc.psum_tensor("e_py", [P, 1024], F32))

        s_const = sem("const")
        s_raw = [sem(f"raw{j}") for j in range(6)]
        s_whi = [sem(f"whi{j}") for j in range(6)]
        s_wlo = [sem(f"wlo{j}") for j in range(6)]
        s_code = sem("code")
        s_xt, s_xhi, s_xlo = sem("xt"), sem("xhi"), sem("xlo")
        s_who, s_xg, s_store = ([sem(f"{n}{i}") for i in range(2)] for n in ("who", "xg", "store"))
        s_gate, s_up, s_silu, s_h, s_ht, s_hhi, s_hlo = (sem(n) for n in ("gate", "up", "silu", "h", "ht", "hhi", "hlo"))
        s_y, s_ya, s_yd = sem("y"), sem("ya"), sem("yd")

        block = ctx.enter_context(nc.Block())
        HALF = 2048
        w_v = [w.rearrange("e (p k) n -> e p (k n)", p=P) for w in (w_gate, w_up, w_down)]

        def span(j):
            return slice(HALF * (j % 2), HALF * (j % 2 + 1))

        def pair_count(eng):
            return eng.value_load(n_pairs[0:1, 0:1], min_val=NE // 2, max_val=(NE + MORE + 1) // 2)

        def each_block(eng, body):
            for half in range(2):
                body(0, half)
            with eng.Fori(1, pair_count(eng)) as r:
                for half in range(2):
                    body(r, half)

        @block.sync
        def _(sp):
            sp.dma_start(ident[:], ident_d).then_inc(s_const, 16)

            def load(r, half):
                n = 2 * r + half
                e = n if isinstance(r, int) else sp.value_load(blocks[0:1, 0, bass.ds(n, 1)], min_val=0,
                                                               max_val=NE - 1)
                for j in range(6):
                    if not (isinstance(r, int) and n == 0):
                        sp.wait_ge(s_wlo[j], n)
                    sp.dma_start(raw[:, j // 2, span(j)], w_v[j // 2][e][:, span(j)]).then_inc(s_raw[j], 16)

            each_block(sp, load)

        @block.gpsimd
        def _(pool):
            def gather(n, r, half, base):
                pool.dma_start(who[half][:], table[bass.ds(base, P), :]).then_inc(s_who[half], 16)
                pool.wait_ge(s_who[half], 16 * (r + 1))
                pool.wait_ge(s_xt, 2 * n - 2 if not (isinstance(r, int) and r == 0) else 0)
                settle_waits(pool, s_tick)
                pool.indirect_dma_start(out=xg[half][:], out_offset=None, in_=h_rows,
                                        in_offset=bass.IndirectOffsetOnAxis(ap=who[half][:, 0:1], axis=0),
                                        bounds_check=ROWS - 1, oob_is_err=False).then_inc(s_xg[half], 16)

            for half in range(2):
                nc.gpsimd.memset(xg[half][:], 0.0).then_inc(s_code, 1)
            pool.wait_ge(s_code, 2)
            for half in range(2):
                gather(half, 0, half, half * ROWS)

            def step(r, half):
                n = 2 * r + half
                if isinstance(r, int):
                    ahead = (n + 2) * ROWS
                else:
                    ahead = pool.value_load(blocks[0:1, 1, bass.ds(n + 2, 1)], min_val=0, max_val=NE * ROWS - P)
                pool.wait_ge(s_xg[half], 16 * (r + 1))
                pool.wait_ge(s_store[half], 16 * r)
                settle_waits(pool, s_tick)
                nc.gpsimd.tensor_copy(code[half][:], who[half][:, 1:2]).then_inc(s_code, 1)
                pool.wait_ge(s_code, n + 3)
                settle_waits(pool, s_tick)
                gather(n + 2, r + 1, half, ahead)
                pool.wait_ge(s_ya, n + 1)
                pool.wait_ge(s_yd, n + 1)
                settle_waits(pool, s_tick)
                pool.indirect_dma_start(out=y_rows, out_offset=bass.IndirectOffsetOnAxis(ap=code[half][:, 0:1], axis=0),
                                        in_=y_sb[half][:], in_offset=None, bounds_check=2 * ROWS - 1,
                                        oob_is_err=False).then_inc(s_store[half], 16)

            each_block(pool, step)
            pairs_done = pair_count(pool)
            for half in range(2):
                pool.wait_ge(s_store[half], 16 * pairs_done)

        @block.tensor
        def _(pe):
            pe.wait_ge(s_const, 16)

            def transpose_rows(b, half):
                for j in range(4):
                    k = 4 * b + j
                    ins = pe.transpose(px[:, k * P:(k + 1) * P], xg[half][:, k:D:KD], ident[:])
                ins.then_inc(s_xt, 1)

            pe.wait_ge(s_xg[0], 16)
            transpose_rows(0, 0)
            transpose_rows(1, 0)

            def step(r, half):
                n = 2 * r + half
                pe.wait_ge(s_xlo, 2 * (n + 1))
                for m, (acc, done) in enumerate(((pg, s_gate), (pu, s_up))):
                    if m == 0:
                        pe.wait_ge(s_h, n)
                    for k in range(KD):
                        if k % 4 == 0:
                            pe.wait_ge(s_wlo[2 * m + k // 4], n + 1)
                        rows, cols = slice(k * P, (k + 1) * P), slice(k * FE, (k + 1) * FE)
                        ins = three_passes(pe, acc[:], xT_hi[:, rows], xT_lo[:, rows], w_hi[:, m, cols],
                                           w_lo[:, m, cols], k == 0, k == KD - 1)
                    ins.then_inc(done, 1)
                pe.wait_ge(s_xg[1 - half], 16 * (r + half + 1))
                transpose_rows(0, 1 - half)
                pe.wait_ge(s_h, n + 1)
                pe.wait_ge(s_hlo, n)
                for k in range(KF):
                    ins = pe.transpose(ph[:, k * P:(k + 1) * P], h_sb[:, k:FE:KF], ident[:])
                ins.then_inc(s_ht, 1)
                transpose_rows(1, 1 - half)
                pe.wait_ge(s_hlo, n + 1)
                pe.wait_ge(s_ya, n)
                pe.wait_ge(s_yd, n)
                for k in range(KF):
                    if k % 2 == 0:
                        pe.wait_ge(s_wlo[4 + k // 2], n + 1)
                    for b in range(2):
                        rows, cols = slice(k * P, (k + 1) * P), slice(k * D + b * 512, k * D + (b + 1) * 512)
                        ins = three_passes(pe, py[:, b * 512:(b + 1) * 512], hT_hi[:, rows], hT_lo[:, rows],
                                           w_hi[:, 2, cols], w_lo[:, 2, cols], k == 0, k == KF - 1)
                ins.then_inc(s_y, 1)

            each_block(pe, step)

        def free_after(eng, j, n):
            eng.wait_ge((s_gate, s_up, s_y)[j // 2], n)

        @block.scalar
        def _(act):
            def split(j, n):
                act.wait_ge(s_raw[j], 16 * (n + 1))
                free_after(act, j, n)
                nc.scalar.copy(w_hi[:, j // 2, span(j)], raw[:, j // 2, span(j)]).then_inc(s_whi[j], 1)

            def rows_hi(n):
                for b in range(2):
                    act.wait_ge(s_xt, 2 * n + b + 1)
                    nc.scalar.copy(xT_hi[:, b * 512:(b + 1) * 512], px[:, b * 512:(b + 1) * 512]).then_inc(s_xhi, 1)

            def take_y(n, r, half):
                act.wait_ge(s_y, n + 1)
                act.wait_ge(s_store[half], 16 * r)
                nc.scalar.copy(y_sb[half][:, 0:512], py[:, 0:512]).then_inc(s_ya, 1)

            rows_hi(0)

            def step(r, half):
                n = 2 * r + half
                split(0, n)
                split(1, n)
                split(2, n)
                split(3, n)
                if not (isinstance(r, int) and n == 0):
                    take_y(n - 1, r if half else r - 1, 1 - half)
                act.wait_ge(s_gate, n + 1)
                nc.scalar.activation(act_g[:], pg[:], ACT.Silu).then_inc(s_silu, 1)
                split(4, n)
                split(5, n)
                act.wait_ge(s_ht, n + 1)
                nc.scalar.copy(hT_hi[:], ph[:]).then_inc(s_hhi, 1)
                rows_hi(n + 1)

            each_block(act, step)
            last = act.value_load(n_pairs[0:1, 1:2], min_val=0, max_val=(NE + MORE + 1) // 2)
            take_y(2 * last + 1, last, 1)

        @block.vector
        def _(dve):
            def split(j, n):
                dve.wait_ge(s_whi[j], n + 1)
                nc.vector.tensor_tensor(w_lo[:, j // 2, span(j)], raw[:, j // 2, span(j)],
                                        w_hi[:, j // 2, span(j)].bitcast(F32), ALU.subtract).then_inc(s_wlo[j], 1)

            def rows_lo(n):
                for b in range(2):
                    cols = slice(b * 512, (b + 1) * 512)
                    dve.wait_ge(s_xhi, 2 * n + b + 1)
                    nc.vector.tensor_tensor(xT_lo[:, cols], px[:, cols], xT_hi[:, cols].bitcast(F32),
                                            ALU.subtract).then_inc(s_xlo, 1)

            def take_y(n, r, half):
                dve.wait_ge(s_y, n + 1)
                dve.wait_ge(s_store[half], 16 * r)
                nc.vector.tensor_copy(y_sb[half][:, 512:1024], py[:, 512:1024]).then_inc(s_yd, 1)

            rows_lo(0)

            def step(r, half):
                n = 2 * r + half
                split(0, n)
                split(1, n)
                split(2, n)
                split(3, n)
                if not (isinstance(r, int) and n == 0):
                    take_y(n - 1, r if half else r - 1, 1 - half)
                split(4, n)
                dve.wait_ge(s_silu, n + 1)
                dve.wait_ge(s_up, n + 1)
                nc.vector.tensor_tensor(h_sb[:], act_g[:], pu[:], ALU.mult).then_inc(s_h, 1)
                dve.wait_ge(s_hhi, n + 1)
                nc.vector.tensor_tensor(hT_lo[:], ph[:], hT_hi[:].bitcast(F32), ALU.subtract).then_inc(s_hlo, 1)
                split(5, n)
                rows_lo(n + 1)

            each_block(dve, step)
            last = dve.value_load(n_pairs[0:1, 1:2], min_val=0, max_val=(NE + MORE + 1) // 2)
            take_y(2 * last + 1, last, 1)


def phase_combine(nc, x_mid, y_rows, g_final, gates, out):
    with ExitStack() as ctx:
        def sb(name, shape, dt=F32):
            return ctx.enter_context(nc.sbuf_tensor("f_" + name, shape, dt))

        sems = phase_sems(nc, ctx)

        def sem(name):
            return phase_sem(nc, sems, "f_" + name)

        g_row, eps = sb("g_row", [P, D]), sb("eps", [P, 1])
        share = sb("share", [P, 2, 2])
        x2 = sb("x2", [P, 2, D])
        y = sb("y", [P, 2, 2, D])
        sum_, o_sb = sb("sum", [P, 2, D]), sb("o_sb", [P, 2, D])
        junk = sb("junk", [P, D], BF16)
        ssq, root, rstd = sb("ssq", [P, 1]), sb("root", [P, 1]), sb("rstd", [P, 1])

        s_const, s_eps, s_share = sem("const"), sem("eps"), sem("share")
        s_x = [sem("x0"), sem("x1")]
        s_y = [sem("y0"), sem("y1")]
        s_scaled, s_sum, s_sq, s_root, s_rstd, s_o = (sem(n) for n in ("scaled", "sum", "sq", "root", "rstd", "o"))
        s_store = [sem("store0"), sem("store1")]
        s_d = sem("d")

        block = ctx.enter_context(nc.Block())

        @block.sync
        def _(sp):
            sp.dma_start(g_row[:], g_final.partition_broadcast(P)).then_inc(s_const, 16)
            y_v = y_rows.rearrange("(t p c) n -> t p (c n)", p=P, c=2)

            def tile(r, half, last):
                t = 2 * r + half
                if not (isinstance(r, int) and r == 0):
                    sp.wait_ge(s_sum, t - 1)
                    sp.wait_ge(s_const, 16)
                sp.dma_start(x2[:, half, :], x_mid[t]).then_inc(s_x[half], 16)
                sp.dma_start(y[:, half].rearrange("p c n -> p (c n)"), y_v[t]).then_inc(s_y[half], 16)

            pairs(sp, TILES, tile)

        @block.gpsimd
        def _(pool):
            nc.gpsimd.memset(eps[:], EPS).then_inc(s_eps, 1)

        @block.scalar
        def _(act):
            def fetch(t, r, half):
                act.wait_ge(s_sum, t - 1 if not (isinstance(r, int) and r == 0) else 0)
                nc.scalar.copy(share[:, half, :], gates[:, t, :]).then_inc(s_share, 1)

            act.wait_ge(s_eps, 1)
            fetch(0, 0, 0)
            fetch(1, 0, 1)

            def tile(r, half, last):
                t = 2 * r + half
                act.wait_ge(s_y[half], 16 * (r + 1))
                act.wait_ge(s_share, t + 1)
                nc.scalar.activation(y[:, half, 0, :], y[:, half, 0, :], ACT.Copy,
                                     scale=share[:, half, 0:1]).then_inc(s_scaled, 1)
                act.wait_ge(s_sum, t + 1)
                act.wait_ge(s_rstd, t)
                nc.scalar.activation(junk[:], sum_[:, half, :], ACT.Square, accum_out=ssq[:]).then_inc(s_sq, 1)
                act.wait_ge(s_sq, t + 1)
                nc.scalar.activation(root[:], ssq[:], ACT.Sqrt, bias=eps[:], scale=1.0 / D).then_inc(s_root, 1)
                if not (isinstance(r, int) and r == TILES // 2 - 1):
                    fetch(t + 2, r + 1, half)
                act.wait_ge(s_o, t + 1)
                act.dma_start(out[t], o_sb[:, half, :]).then_inc(s_store[half], 16)

            pairs(act, TILES, tile)
            act.wait_ge(s_store[0], 16 * TILES // 2)
            act.wait_ge(s_store[1], 16 * TILES // 2)

        @block.vector
        def _(dve):
            dve.wait_ge(s_const, 16)
            steps = Steps(dve, s_d, 1)

            def tile(r, half, last):
                t = 2 * r + half
                steps.begin(t)
                dve.wait_ge(s_scaled, t + 1)
                dve.wait_ge(s_x[half], 16 * (r + 1))
                steps.chain(nc.vector.scalar_tensor_tensor(out=y[:, half, 1, :], in0=y[:, half, 1, :],
                                                           scalar=share[:, half, 1:2], in1=y[:, half, 0, :],
                                                           op0=ALU.mult, op1=ALU.add))
                nc.vector.tensor_tensor(sum_[:, half, :], y[:, half, 1, :], x2[:, half, :], ALU.add).then_inc(s_sum, 1)
                dve.wait_ge(s_root, t + 1)
                nc.vector.reciprocal(rstd[:], root[:]).then_inc(s_rstd, 1)
                dve.wait_ge(s_rstd, t + 1)
                dve.wait_ge(s_store[half], 16 * r)
                nc.vector.scalar_tensor_tensor(out=o_sb[:, half, :], in0=sum_[:, half, :], scalar=rstd[:, 0:1],
                                               in1=g_row[:], op0=ALU.mult, op1=ALU.mult).then_inc(s_o, 1)
                steps.end()

            pairs(dve, TILES, tile)


def tables():
    inv = np.float32(1) / (10000.0 ** (np.arange(0, DR, 2) / DR)).astype(np.float32)
    pos = np.concatenate([np.arange(n * P, dtype=np.float32) for _, n in SEQS])
    ang = pos[:, None] * inv[None, :]
    cos, sin = np.cos(ang), np.sin(ang)
    rope = np.stack([np.concatenate([cos, cos], 1), np.concatenate([-sin, sin], 1)], 1)
    j, i = np.arange(P)[:, None], np.arange(P)[None, :]
    n = np.arange(P)
    return {
        "rope": rope.reshape(TILES, P, 2, DR).astype(np.float32),
        "ident": np.eye(P, dtype=np.float32),
        "dist": np.stack([np.maximum(i - j, 0), np.maximum(j - i, 0)], 1).astype(np.float32),
        "index": np.stack([-(P - 1 - n), -n, -(n + 1), -(P - n)], 1).astype(np.float32),
        "route": np.concatenate([np.broadcast_to(np.arange(NE), (P, NE)),
                                 np.broadcast_to(np.arange(NE) // EPG, (P, NE)),
                                 (j < i), np.ones((P, P))], 1).astype(np.float32),
        "blocks": np.concatenate([np.arange(NE), np.zeros(MORE + AHEAD), np.arange(NE) * ROWS,
                                  np.zeros(MORE + AHEAD)])[None, :].astype(np.int32),
    }


WEIGHTS = {"g_mix": "g_mix", "w_in": "w_in", "log_decay": "ret_log_decay", "gn_g": "ret_gn_g",
           "g_q": "mla_q_norm_g", "w_q_up": "w_q_up", "g_kv": "mla_kv_norm_g", "w_kv_up": "w_kv_up",
           "w_out": "w_out", "g_ffn": "g_ffn", "w_rg": "w_router_group", "w_re": "w_router_expert",
           "w_gate": "w_exp_gate", "w_up": "w_exp_up", "w_down": "w_exp_down"}


def build(nc, d, out):
    def scratch(name, shape, dt=F32):
        return nc.dram_tensor("s_" + name, shape, dt, kind="Internal").ap()

    mid = scratch("mid", (TILES, P, M_W))
    mixT = scratch("mixT", (TILES, P, D))
    x_mid = scratch("x_mid", (TILES, P, D))
    h_rows = scratch("h_rows", (ROWS, D))
    table = scratch("table", (NE * ROWS, 2), I32)
    y_rows = scratch("y_rows", (2 * ROWS, D))

    with ExitStack() as ctx:
        s_tick, s_tock = (ctx.enter_context(nc.semaphore(n)) for n in ("tick", "tock"))
        phase_project(nc, d["x"], d["w_in"], d["g_mix"], d["g_q"], d["g_kv"], d["rope"], d["ident"], mid)
        phase_retention(nc, mid, d["log_decay"], d["gn_g"], d["dist"], d["index"], d["ident"], mixT)
        for n, (first, tiles) in enumerate(SEQS):
            phase_latent(nc, f"c{n}", first, tiles, mid, d["w_q_up"], d["w_kv_up"], d["rope"], d["ident"], mixT)
        gates = ctx.enter_context(nc.sbuf_tensor("gates", [P, TILES, 2], F32))
        blocks = ctx.enter_context(nc.sbuf_tensor("blocks", [1, 2, NBLK], I32))
        n_pairs = ctx.enter_context(nc.sbuf_tensor("n_pairs", [1, 2], I32))
        phase_mix(nc, mixT, d["x"], d["w_out"], d["g_ffn"], d["w_rg"], d["w_re"], d["ident"], d["route"],
                  d["blocks"], x_mid, h_rows.rearrange("(t p) n -> t p n", p=P), table, gates, blocks, n_pairs,
                  s_tick, s_tock)
        phase_experts(nc, d["w_gate"], d["w_up"], d["w_down"], d["ident"], h_rows, table, y_rows, blocks, n_pairs,
                      s_tick)
        phase_combine(nc, x_mid, y_rows, d["g_final"], gates, out)


def kernel(**inputs):
    import concourse.bacc as _bacc
    from concourse.bass_utils import run_bass_kernel_spmd as _run

    nc = _bacc.Bacc("TRN2", target_bir_lowering=False, num_devices=1)
    x = np.concatenate([np.asarray(inputs["x_prompt"])[0], np.asarray(inputs["x_sample"])[0]], 0)
    arrays = {"x": x.reshape(TILES, P, D), "g_final": inputs["g_final"], **tables()}
    arrays.update({name: np.asarray(inputs[key])[0] for name, key in WEIGHTS.items()})
    arrays = {"in_" + name: np.ascontiguousarray(a) for name, a in arrays.items()}
    d = {name[3:]: nc.dram_tensor(name, a.shape, mybir.dt.from_np(a.dtype), kind="ExternalInput").ap()
         for name, a in arrays.items()}
    out = nc.dram_tensor("out", (TILES, P, D), F32, kind="ExternalOutput").ap()
    build(nc, d, out)
    r = _run(nc, [arrays], core_ids=[0])
    y = r.results[0]["out"].reshape(1, TILES * P, D)
    cut = SEQS[0][1] * P
    return y[:, :cut], y[:, cut:]
```

```python
from contextlib import ExitStack

import numpy as np
import concourse.bass as bass
from concourse import mybir

F32 = mybir.dt.float32
F32R = mybir.dt.float32r
BF16 = mybir.dt.bfloat16
I32 = mybir.dt.int32
U32 = mybir.dt.uint32
ALU = mybir.AluOpType
ACT = mybir.ActivationFunctionType
AX = mybir.AxisListType

P = 128
D = 1024
KD = D // P
SEQS = ((0, 4), (4, 8))
TILES = 12
TOK = TILES * P
HR, DR = 8, 64
RW = HR * DR
HM, NOPE, ROPE, VD = 4, 128, 64, 128
QRANK, KVRANK = 256, 128
CW = QRANK + KVRANK + ROPE
D_IN = 4 * RW + CW
EPS = 1e-6

M_QT, M_KT, M_K, M_V, M_G, M_CT = 0, 512, 1024, 1536, 2048, 2560
M_W = 3072


class Steps:

    def __init__(self, eng, sem, per):
        self.eng, self.sem, self.per, self.base, self.n = eng, sem, per, 0, 0

    def begin(self, i):
        self.base, self.n = i * self.per, 0

    def end(self):
        assert self.n == self.per, (self.n, self.per)

    def done(self, ins):
        ins.then_inc(self.sem, 1)
        self.n += 1

    def settle(self):
        self.eng.wait_ge(self.sem, self.base + self.n)

    def chain(self, ins):
        self.done(ins)
        self.settle()


def phase_sems(nc, ctx):
    sems = []

    def clear():
        nc.clear_and_free_semaphores(sems)
        nc.all_engine_barrier()

    ctx.callback(clear)
    return sems


def phase_sem(nc, sems, name):
    sems.append(nc.alloc_semaphore(name))
    return sems[-1]


def pairs(eng, tiles, body):
    for half in (0, 1):
        body(0, half, False)
    with eng.Fori(1, tiles // 2 - 1) as r:
        for half in (0, 1):
            body(r, half, False)
    for half in (0, 1):
        body(tiles // 2 - 1, half, half == 1)


def settle_waits(eng, tick):
    eng.sem_inc(tick, 1)


def three_passes(pe, out, st_hi, st_lo, mv_hi, mv_lo, first, last):
    pe.matmul(out, st_hi, mv_hi, start=first, stop=False)
    pe.matmul(out, st_hi, mv_lo, start=False, stop=False)
    return pe.matmul(out, st_lo, mv_hi, start=False, stop=last)


def phase_project(nc, x_all, w_in, g_mix, g_q, g_kv, rope, ident_d, mid):
    with ExitStack() as ctx:
        def sb(name, shape, dt=F32):
            return ctx.enter_context(nc.sbuf_tensor("a_" + name, shape, dt))

        sems = phase_sems(nc, ctx)

        def sem(name):
            return phase_sem(nc, sems, "a_" + name)

        w_hi, w_lo = sb("w_hi", [P, KD, D_IN], F32R), sb("w_lo", [P, KD, D_IN], F32R)
        x_sb = sb("x_sb", [P, 2, D])
        xT_hi, xT_lo = sb("xT_hi", [P, 2, KD, P], F32R), sb("xT_lo", [P, 2, KD, P], F32R)
        rec = sb("rec", [P, M_W])
        rope_sb = sb("rope_sb", [P, 2, 2, DR])
        work = sb("work", [P, 4, 512])
        part1, part2, q_tok, c_tok = (work[:, i, :] for i in range(4))
        junk = sb("junk", [P, D], BF16)
        g_col = sb("g_col", [P, KD])
        gq_row, gkv_row = sb("gq_row", [P, QRANK]), sb("gkv_row", [P, KVRANK])
        ident = sb("ident", [P, P])
        eps = sb("eps", [P, 1])
        ssq = sb("ssq", [P, 3])
        root = sb("root", [P, 3])
        rstd = sb("rstd", [P, 3])
        stage = [rec[:, i * 1024:(i + 1) * 1024] for i in range(3)]
        stage += [work[:, 2 * i:2 * i + 2, :].rearrange("p a n -> p (a n)") for i in range(2)]
        NST = len(stage)

        pG = [ctx.enter_context(nc.psum_tensor(f"a_pG{g}", [P, 512], F32)) for g in range(5)]
        pX = [ctx.enter_context(nc.psum_tensor(f"a_pX{b}", [P, 512], F32)) for b in range(2)]
        pO = ctx.enter_context(nc.psum_tensor("a_pO", [P, 512], F32))
        C, Q, K, V, G = range(5)
        COLS = {Q: (0, RW), K: (RW, RW), V: (2 * RW, RW), G: (3 * RW, RW), C: (4 * RW, CW)}
        PARTS = KD // 2

        def part(m):
            c0, w = COLS[m // PARTS]
            k = 2 * (m % PARTS)
            return slice(k, k + 2), slice(c0, c0 + w), stage[m % NST][:, 0:2 * w].rearrange("p (k n) -> p k n", k=2)

        s_const = sem("const")
        s_raw = [sem(f"raw{i}") for i in range(NST)]
        s_whi, s_wlo = sem("whi"), sem("wlo")
        s_x = [sem("x0"), sem("x1")]
        s_sq = sem("sq")
        s_root, s_rstd = sem("root"), sem("rstd")
        s_croot = sem("croot")
        s_xt = sem("xt")
        s_hi, s_lo = sem("hi"), sem("lo")
        s_proj = sem("proj")
        s_ctok, s_qtok = sem("ctok"), sem("qtok")
        s_ev = {C: s_ctok, Q: s_qtok, K: sem("evk"), V: sem("evv"), G: sem("evg")}
        s_out = sem("out")
        s_outev = sem("outev")
        s_store = sem("store")
        s_dve = sem("dve")
        s_eps = sem("eps")

        block = ctx.enter_context(nc.Block())

        @block.sync
        def _(sp):
            sp.dma_start(x_sb[:, 0, :], x_all[0]).then_inc(s_x[0], 16)
            sp.dma_start(rope_sb[:, 0], rope[0]).then_inc(s_x[0], 16)
            sp.dma_start(ident[:], ident_d).then_inc(s_const, 16)
            sp.dma_start(g_col[:], g_mix.rearrange("(p k) -> p k", k=KD)).then_inc(s_const, 16)
            sp.dma_start(gq_row[:], g_q.partition_broadcast(P)).then_inc(s_const, 16)
            sp.dma_start(gkv_row[:], g_kv.partition_broadcast(P)).then_inc(s_const, 16)
            w_v = w_in.rearrange("(p k) n -> p k n", k=KD)
            for m in range(5 * PARTS):
                k, cols, raw = part(m)
                if m >= NST:
                    sp.wait_ge(s_wlo, m - NST + 1)
                sp.dma_start(raw, w_v[:, k, cols]).then_inc(s_raw[m % NST], 16)

            def tile(r, half, last):
                t = 2 * r + half
                if not last:
                    sp.wait_ge(s_xt, 2 * t)
                    sp.wait_ge(s_sq, t)
                    sp.wait_ge(s_ev[K], t)
                    sp.wait_ge(s_const, 64)
                    sp.dma_start(x_sb[:, 1 - half, :], x_all[t + 1]).then_inc(s_x[1 - half], 16)
                    sp.dma_start(rope_sb[:, 1 - half], rope[t + 1]).then_inc(s_x[1 - half], 16)
                sp.wait_ge(s_outev, 3 * (t + 1))
                sp.wait_ge(s_ev[V], t + 1)
                sp.wait_ge(s_ev[G], t + 1)
                sp.wait_ge(s_ev[K], t + 1)
                sp.wait_ge(s_const, 64)
                sp.dma_start(mid[t], rec[:]).then_inc(s_store, 16)

            pairs(sp, TILES, tile)
            sp.wait_ge(s_store, 16 * TILES)

        @block.gpsimd
        def _(pool):
            nc.gpsimd.memset(eps[:], EPS).then_inc(s_eps, 1)

        @block.tensor
        def _(pe):
            def transpose_x(n, half):
                for b in range(2):
                    for j in range(4):
                        k = 4 * b + j
                        ins = pe.transpose(pX[b][:, j * P:(j + 1) * P], x_sb[:, half, k:D:KD], ident[:])
                    ins.then_inc(s_xt, 1)

            pe.wait_ge(s_const, 64)
            pe.wait_ge(s_x[0], 32)
            transpose_x(0, 0)

            def project(r, half, g, i):
                t = 2 * r + half
                first = isinstance(t, int) and t == 0
                pe.wait_ge(s_ev[g], t)
                c0, w = COLS[g]
                for k in range(KD):
                    if first and k % 2 == 0:
                        pe.wait_ge(s_wlo, i * PARTS + k // 2 + 1)
                    ins = three_passes(pe, pG[g][:, 0:w], xT_hi[:, half, k, :], xT_lo[:, half, k, :],
                                       w_hi[:, k, c0:c0 + w], w_lo[:, k, c0:c0 + w], k == 0, k == KD - 1)
                ins.then_inc(s_proj, 1)

            def transpose_out(r, half, i, src):
                t = 2 * r + half
                pe.wait_ge(s_outev, 3 * t + i)
                for j in range(4):
                    ins = pe.transpose(pO[:, j * P:(j + 1) * P], src[:, j * P:(j + 1) * P], ident[:])
                ins.then_inc(s_out, 1)

            def tile(r, half, last):
                t = 2 * r + half
                first = isinstance(t, int) and t == 0
                pe.wait_ge(s_lo, 2 * (t + 1))
                project(r, half, C, 0)
                project(r, half, Q, 1)
                if first:
                    project(r, half, K, 2)
                    project(r, half, V, 3)
                    project(r, half, G, 4)
                pe.wait_ge(s_ctok, t + 1)
                transpose_out(r, half, 0, c_tok)
                if not first:
                    project(r, half, K, 2)
                pe.wait_ge(s_qtok, t + 1)
                transpose_out(r, half, 1, q_tok)
                if not first:
                    project(r, half, V, 3)
                pe.wait_ge(s_ev[K], t + 1)
                transpose_out(r, half, 2, rec[:, M_K:M_K + RW])
                if not last:
                    pe.wait_ge(s_x[1 - half], 32 * (r + 1 + half))
                    transpose_x(t + 1, 1 - half)
                if not first:
                    project(r, half, G, 4)

            pairs(pe, TILES, tile)

        @block.scalar
        def _(act):
            def hi_of_x(n, half):
                for b in range(2):
                    act.wait_ge(s_xt, 2 * n + b + 1)
                    for j in range(4):
                        k = 4 * b + j
                        ins = nc.scalar.activation(xT_hi[:, half, k, :], pX[b][:, j * P:(j + 1) * P],
                                                   ACT.Copy, scale=g_col[:, k:k + 1])
                    ins.then_inc(s_hi, 1)

            act.wait_ge(s_const, 64)
            hi_of_x(0, 0)
            for m in range(5 * PARTS):
                k, cols, raw = part(m)
                act.wait_ge(s_raw[m % NST], 16 * (m // NST + 1))
                nc.scalar.copy(w_hi[:, k, cols], raw).then_inc(s_whi, 1)
            act.wait_ge(s_eps, 1)

            def take_out(r, half, i, col):
                t = 2 * r + half
                act.wait_ge(s_out, 3 * t + i + 1)
                nc.scalar.copy(rec[:, col:col + 512], pO[:]).then_inc(s_outev, 1)

            def tile(r, half, last):
                t = 2 * r + half
                act.wait_ge(s_x[half], 32 * (r + 1))
                act.wait_ge(s_rstd, 2 * t)
                nc.scalar.activation(junk[:], x_sb[:, half, :], ACT.Square, accum_out=ssq[:, 0:1]).then_inc(s_sq, 1)
                act.wait_ge(s_sq, t + 1)
                nc.scalar.activation(root[:, 0:1], ssq[:, 0:1], ACT.Sqrt, bias=eps[:, 0:1],
                                     scale=1.0 / D).then_inc(s_root, 1)
                act.wait_ge(s_rstd, 2 * t + 1)
                act.wait_ge(s_proj, 5 * t + 1)
                nc.scalar.activation(junk[:, 0:QRANK], pG[C][:, 0:QRANK], ACT.Square, scale=rstd[:, 0:1],
                                     accum_out=ssq[:, 1:2])
                nc.scalar.activation(junk[:, QRANK:QRANK + KVRANK], pG[C][:, QRANK:QRANK + KVRANK], ACT.Square,
                                     scale=rstd[:, 0:1], accum_out=ssq[:, 2:3]).then_inc(s_croot, 1)
                act.wait_ge(s_croot, 2 * t + 1)
                nc.scalar.activation(root[:, 1:2], ssq[:, 1:2], ACT.Sqrt, bias=eps[:, 0:1], scale=1.0 / QRANK)
                nc.scalar.activation(root[:, 2:3], ssq[:, 2:3], ACT.Sqrt, bias=eps[:, 0:1],
                                     scale=1.0 / KVRANK).then_inc(s_croot, 1)
                act.wait_ge(s_store, 16 * t)
                take_out(r, half, 0, M_CT)
                take_out(r, half, 1, M_QT)
                act.wait_ge(s_proj, 5 * t + 4)
                nc.scalar.activation(rec[:, M_V:M_V + RW], pG[V][:], ACT.Copy, scale=rstd[:, 0:1]).then_inc(s_ev[V], 1)
                take_out(r, half, 2, M_KT)
                if not last:
                    hi_of_x(t + 1, 1 - half)
                act.wait_ge(s_proj, 5 * t + 5)
                nc.scalar.activation(rec[:, M_G:M_G + RW], pG[G][:], ACT.Copy, scale=rstd[:, 0:1]).then_inc(s_ev[G], 1)

            pairs(act, TILES, tile)

        @block.vector
        def _(dve):
            steps = Steps(dve, s_dve, 5)

            def lo_of_x(n, half):
                for b in range(2):
                    dve.wait_ge(s_hi, 2 * n + b + 1)
                    for j in range(4):
                        k = 4 * b + j
                        ins = nc.vector.scalar_tensor_tensor(
                            out=xT_lo[:, half, k, :], in0=pX[b][:, j * P:(j + 1) * P], scalar=g_col[:, k:k + 1],
                            in1=xT_hi[:, half, k, :].bitcast(F32), op0=ALU.mult, op1=ALU.subtract)
                    ins.then_inc(s_lo, 1)

            dve.wait_ge(s_const, 64)
            lo_of_x(0, 0)
            for m in range(5 * PARTS):
                k, cols, raw = part(m)
                dve.wait_ge(s_whi, m + 1)
                nc.vector.tensor_tensor(w_lo[:, k, cols], raw, w_hi[:, k, cols].bitcast(F32),
                                        ALU.subtract).then_inc(s_wlo, 1)

            def rotate(out, src, heads, half, p1, p2):
                cos = rope_sb[:, half, 0, :]
                sin = rope_sb[:, half, 1, :]
                hw = DR // 2
                x3, a3, b3 = (y.rearrange("p (h d) -> p h d", h=heads) for y in (src, p1, p2))
                c3 = cos.unsqueeze(1).broadcast_to([P, heads, DR])
                s3 = sin.unsqueeze(1).broadcast_to([P, heads, DR])
                nc.vector.scalar_tensor_tensor(out=a3, in0=x3, scalar=rstd[:, 0:1], in1=c3,
                                               op0=ALU.mult, op1=ALU.mult)
                nc.vector.scalar_tensor_tensor(out=b3[:, :, 0:hw], in0=x3[:, :, hw:DR], scalar=rstd[:, 0:1],
                                               in1=s3[:, :, 0:hw], op0=ALU.mult, op1=ALU.mult)
                steps.chain(nc.vector.scalar_tensor_tensor(
                    out=b3[:, :, hw:DR], in0=x3[:, :, 0:hw], scalar=rstd[:, 0:1], in1=s3[:, :, hw:DR],
                    op0=ALU.mult, op1=ALU.mult))
                return nc.vector.tensor_tensor(out, p1, p2, ALU.add)

            def tile(r, half, last):
                t = 2 * r + half
                steps.begin(t)
                dve.wait_ge(s_root, t + 1)
                dve.wait_ge(s_proj, 5 * t)
                dve.wait_ge(s_ev[V], t)
                dve.wait_ge(s_ev[G], t)
                nc.vector.reciprocal(rstd[:, 0:1], root[:, 0:1]).then_inc(s_rstd, 1)
                dve.wait_ge(s_rstd, 2 * t + 1)
                dve.wait_ge(s_croot, 2 * t + 2)
                dve.wait_ge(s_out, 3 * t)
                steps.chain(nc.vector.reciprocal(rstd[:, 1:3], root[:, 1:3]))
                nc.vector.tensor_scalar(rstd[:, 1:3], rstd[:, 1:3], rstd[:, 0:1], None, ALU.mult).then_inc(s_rstd, 1)
                dve.wait_ge(s_rstd, 2 * t + 2)
                nc.vector.scalar_tensor_tensor(out=c_tok[:, 0:QRANK], in0=pG[C][:, 0:QRANK], scalar=rstd[:, 1:2],
                                               in1=gq_row[:], op0=ALU.mult, op1=ALU.mult)
                nc.vector.scalar_tensor_tensor(out=c_tok[:, QRANK:QRANK + KVRANK],
                                               in0=pG[C][:, QRANK:QRANK + KVRANK], scalar=rstd[:, 2:3],
                                               in1=gkv_row[:], op0=ALU.mult, op1=ALU.mult)
                kr = c_tok[:, QRANK + KVRANK:QRANK + KVRANK + ROPE]
                steps.chain(rotate(kr, pG[C][:, QRANK + KVRANK:CW], 1, half, part1[:, 0:ROPE], part2[:, 0:ROPE]))
                nc.vector.tensor_copy(c_tok[:, CW:CW + ROPE], kr).then_inc(s_ctok, 1)
                dve.wait_ge(s_proj, 5 * t + 2)
                dve.wait_ge(s_ctok, t + 1)
                dve.wait_ge(s_out, 3 * t)
                ins = rotate(q_tok[:], pG[Q][:], HR, half, part1[:], part2[:])
                ins.then_inc(s_qtok, 1)
                dve.wait_ge(s_qtok, t + 1)
                dve.wait_ge(s_proj, 5 * t + 3)
                dve.wait_ge(s_store, 16 * t)
                ins = rotate(rec[:, M_K:M_K + RW], pG[K][:], HR, half, part1[:], part2[:])
                ins.then_inc(s_ev[K], 1)
                dve.wait_ge(s_ev[K], t + 1)
                if not last:
                    lo_of_x(t + 1, 1 - half)
                steps.end()

            pairs(dve, TILES, tile)


def phase_retention(nc, mid, log_decay, gn_g, dist_d, index_d, ident_d, mixT):
    with ExitStack() as ctx:
        def sb(name, shape, dt=F32):
            return ctx.enter_context(nc.sbuf_tensor("b_" + name, shape, dt))

        sems = phase_sems(nc, ctx)

        def sem(name):
            return phase_sem(nc, sems, "b_" + name)

        PR = HR // 2
        ident, dist = sb("ident", [P, P]), sb("dist", [P, 2, P])
        index = sb("index", [P, 4])
        rate = sb("rate", [P, 2, HR])
        gn_row = sb("gn_row", [P, RW])
        eps = sb("eps", [P, 1])
        dmat = sb("dmat", [P, 2, PR, P])
        dtmp = sb("dtmp", [P, P])
        wk, wq = sb("wk", [P, 2, HR]), sb("wq", [P, 2, HR])
        dec = sb("dec", [P, 2, PR])
        kv = sb("kv", [P, 2, 2 * RW])
        vw = sb("vw", [P, 2, HR, 2, DR])
        own = sb("own", [P, TILES, PR, 2, DR])
        run = sb("run", [P, TILES, PR, 2, DR])
        cur = sb("cur", [P, 2, PR, 2 * DR])
        stmp = sb("stmp", [P, 2, PR, DR])
        qk = sb("qk", [P, 2, 2 * RW])
        vg = sb("vg", [P, 2, 2 * RW])
        sc = sb("sc", [P, 2, PR, P])
        fa, fb = sb("fa", [P, HR, DR]), sb("fb", [P, HR, DR])
        fab, o_t, ctr, sq = (sb(n, [P, HR, DR]) for n in ("fab", "o_t", "ctr", "sq"))
        gate, gate2, nrm, ret = (sb(n, [P, HR, DR]) for n in ("gate", "gate2", "nrm", "ret"))
        mu, var, rt, rs = (sb(n, [P, HR]) for n in ("mu", "var", "rt", "rs"))
        retT = sb("retT", [P, 2, RW])

        pst = [ctx.enter_context(nc.psum_tensor(f"b_pst{i}", [P, 512], F32)) for i in range(2)]
        psc = ctx.enter_context(nc.psum_tensor("b_psc", [P, 2, 512], F32))
        pin = ctx.enter_context(nc.psum_tensor("b_pin", [P, 2, 512], F32))
        pno = ctx.enter_context(nc.psum_tensor("b_pno", [P, 512], F32))
        ptr = ctx.enter_context(nc.psum_tensor("b_ptr", [P, 512], F32))

        s_const, s_eps = sem("const"), sem("eps")
        s_rate, s_lin, s_tab, s_dm = sem("rate"), sem("lin"), sem("tab"), sem("dm")
        s_kv = [sem("kv0"), sem("kv1")]
        s_vw, s_own, s_ownev = sem("vw"), sem("own"), sem("ownev")
        s_run, s_cur = sem("run"), sem("cur")
        s_qk = [sem("qk0"), sem("qk1")]
        s_sc, s_scev, s_in, s_inev, s_no, s_noev = (sem(n) for n in ("sc", "scev", "in", "inev", "no", "noev"))
        s_fab, s_ctr, s_sq, s_var, s_rt, s_rs, s_silu, s_ret = (
            sem(n) for n in ("fab", "ctr", "sq", "var", "rt", "rs", "silu", "ret"))
        s_gate, s_nrm = sem("gate"), sem("nrm")
        s_tr, s_trev, s_store = sem("tr"), sem("trev"), [sem("store0"), sem("store1")]
        s_d1, s_d2, s_d3 = sem("d1"), sem("d2"), sem("d3")

        block = ctx.enter_context(nc.Block())

        @block.sync
        def _(sp):
            sp.dma_start(ident[:], ident_d).then_inc(s_const, 16)
            sp.dma_start(dist[:], dist_d).then_inc(s_const, 16)
            sp.dma_start(index[:], index_d).then_inc(s_const, 16)
            sp.dma_start(rate[:].rearrange("p a h -> p (a h)"),
                         log_decay.rearrange("a h -> (a h)").partition_broadcast(P)).then_inc(s_const, 16)

            def load_kv(r, half, last):
                t = 2 * r + half
                if not (isinstance(r, int) and r == 0):
                    sp.wait_ge(s_own, t - 1)
                    sp.wait_ge(s_const, 64)
                sp.dma_start(kv[:, half, :], mid[t][:, M_K:M_K + 2 * RW]).then_inc(s_kv[half], 16)

            pairs(sp, TILES, load_kv)

            def load_qk(r, half, last):
                t = 2 * r + half
                if not (isinstance(r, int) and r == 0):
                    sp.wait_ge(s_noev, t - 1)
                    sp.wait_ge(s_silu, t - 1)
                    sp.wait_ge(s_const, 64)
                sp.dma_start(qk[:, half, :], mid[t][:, M_QT:M_QT + 2 * RW]).then_inc(s_qk[half], 16)
                sp.dma_start(vg[:, half, :], mid[t][:, M_V:M_V + 2 * RW]).then_inc(s_qk[half], 16)

            pairs(sp, TILES, load_qk)

        @block.gpsimd
        def _(pool):
            nc.gpsimd.memset(eps[:], EPS).then_inc(s_eps, 1)

            def carried(t):
                pool.wait_ge(s_inev, t + 1)
                pool.wait_ge(s_noev, t)
                nc.gpsimd.tensor_tensor(fab[:], fa[:], fb[:], ALU.add).then_inc(s_fab, 1)

            def tile(r, half, last):
                t = 2 * r + half
                if isinstance(t, int) and t == 0:
                    carried(0)
                pool.wait_ge(s_silu, t + 1)
                pool.wait_ge(s_ret, t)
                nc.gpsimd.tensor_tensor(gate2[:], gate[:], gn_row[:].rearrange("p (h d) -> p h d", h=HR),
                                        ALU.mult).then_inc(s_gate, 1)
                if not last:
                    carried(t + 1)
                pool.wait_ge(s_rs, t + 1)
                pool.wait_ge(s_gate, t + 1)
                nc.gpsimd.tensor_tensor(nrm[:], ctr[:], rs[:].unsqueeze(2).broadcast_to([P, HR, DR]),
                                        ALU.mult).then_inc(s_nrm, 1)
                pool.wait_ge(s_nrm, t + 1)
                pool.wait_ge(s_tr, t)
                nc.gpsimd.tensor_tensor(ret[:], nrm[:], gate2[:], ALU.mult).then_inc(s_ret, 1)
                if not (isinstance(t, int) and t == 0):
                    keep(t - 1, 1 - half)

            def keep(t, half):
                pool.wait_ge(s_trev, t + 1)
                pool.dma_start(mixT[t][:, 0:RW], retT[:, half, :]).then_inc(s_store[half], 16)

            pool.dma_start(gn_row[:], gn_g.partition_broadcast(P)).then_inc(s_store[1], 16)
            pool.wait_ge(s_const, 64)
            pool.wait_ge(s_store[1], 16)
            pairs(pool, TILES, tile)
            keep(TILES - 1, 1)
            pool.wait_ge(s_store[0], 16 * TILES // 2)
            pool.wait_ge(s_store[1], 16 * TILES // 2 + 16)

        @block.tensor
        def _(pe):
            def own_state(r, half, last):
                t = 2 * r + half
                pe.wait_ge(s_vw, t + 1)
                pe.wait_ge(s_ownev, t - 1 if not (isinstance(r, int) and r == 0) else 0)
                for h in range(HR):
                    pair, odd = h // 2, h % 2
                    ins = pe.matmul(pst[half][odd * DR:(odd + 1) * DR, pair * P:(pair + 1) * P],
                                    kv[:, half, h * DR:(h + 1) * DR],
                                    vw[:, half, h].rearrange("p a d -> p (a d)"), start=True, stop=True)
                ins.then_inc(s_own, 1)

            pairs(pe, TILES, own_state)

            def scores(t, r, half):
                pe.wait_ge(s_qk[half], 32 * (r + 1))
                pe.wait_ge(s_scev, t)
                for h in range(HR):
                    pair, odd = h // 2, h % 2
                    rows, cols = slice(odd * DR, (odd + 1) * DR), slice(pair * P, (pair + 1) * P)
                    ins = pe.matmul(psc[:, odd, cols], qk[rows, half, RW + pair * P:RW + (pair + 1) * P],
                                    qk[rows, half, cols], start=True, stop=True)
                ins.then_inc(s_sc, 1)

            def inter(t, r, half):
                pe.wait_ge(s_inev, t)
                pe.wait_ge(s_cur, t + 1)
                for h in range(HR):
                    pair, odd = h // 2, h % 2
                    rows, cols = slice(odd * DR, (odd + 1) * DR), slice(pair * P, (pair + 1) * P)
                    ins = pe.matmul(pin[:, odd, cols], qk[rows, half, cols],
                                    cur[rows, half, pair, :], start=True, stop=True)
                ins.then_inc(s_in, 1)

            scores(0, 0, 0)
            inter(0, 0, 0)

            def tile(r, half, last):
                t = 2 * r + half
                pe.wait_ge(s_scev, t + 1)
                pe.wait_ge(s_noev, t)
                for h in range(HR):
                    ins = pe.matmul(pno[:, h * DR:(h + 1) * DR], sc[:, h % 2, h // 2, :],
                                    vg[:, half, h * DR:(h + 1) * DR], start=True, stop=True)
                ins.then_inc(s_no, 1)
                if not last:
                    scores(t + 1, r + half, 1 - half)
                    inter(t + 1, r + half, 1 - half)
                if not (isinstance(t, int) and t == 0):
                    turn(t - 1)

            def turn(t):
                pe.wait_ge(s_ret, t + 1)
                pe.wait_ge(s_trev, t)
                for j in range(4):
                    ins = pe.transpose(ptr[:, j * P:(j + 1) * P],
                                       ret[:, 2 * j:2 * j + 2].rearrange("p h d -> p (h d)"), ident[:])
                ins.then_inc(s_tr, 1)

            pairs(pe, TILES, tile)
            turn(TILES - 1)

        @block.scalar
        def _(act):
            act.wait_ge(s_const, 64)
            nc.scalar.activation(rate[:], rate[:], ACT.Exp).then_inc(s_rate, 1)
            act.wait_ge(s_rate, 1)
            for d in range(2):
                nc.scalar.activation(wk[:, d, :], rate[:, d, :], ACT.Exp, scale=index[:, d:d + 1])
                nc.scalar.activation(wq[:, d, :], rate[:, d, :], ACT.Exp, scale=index[:, 2 + d:3 + d])
                for odd in range(2):
                    rows = slice(odd * DR, (odd + 1) * DR)
                    ins = nc.scalar.activation(dec[rows, d, :], rate[rows, d, odd:HR:2], ACT.Exp, scale=-float(P))
            ins.then_inc(s_tab, 1)
            for h in range(HR):
                act.wait_ge(s_lin, 2 * h + 2)
                nc.scalar.activation(dmat[:, h % 2, h // 2, :], dmat[:, h % 2, h // 2, :], ACT.Exp,
                                     scale=-1.0).then_inc(s_dm, 1)

            def own_state(r, half, last):
                t = 2 * r + half
                act.wait_ge(s_own, t + 1)
                nc.scalar.copy(own[:, t].rearrange("p a b d -> p (a b d)"), pst[half][:]).then_inc(s_ownev, 1)

            pairs(act, TILES, own_state)
            act.wait_ge(s_eps, 1)

            def fetch_states(t, half):
                nc.scalar.copy(cur[:, half].rearrange("p a d -> p (a d)"),
                               run[:, t].rearrange("p a b d -> p (a b d)")).then_inc(s_cur, 1)

            act.wait_ge(s_run, 1)
            fetch_states(0, 0)

            def tile(r, half, last):
                t = 2 * r + half
                if not last:
                    act.wait_ge(s_in, t)
                    fetch_states(t + 1, 1 - half)
                act.wait_ge(s_qk[half], 32 * (r + 1))
                act.wait_ge(s_gate, t)
                nc.scalar.activation(gate[:].rearrange("p h d -> p (h d)"), vg[:, half, RW:2 * RW],
                                     ACT.Silu).then_inc(s_silu, 1)
                act.wait_ge(s_ctr, t + 1)
                nc.scalar.activation(sq[:], ctr[:], ACT.Square).then_inc(s_sq, 1)
                if not (isinstance(t, int) and t == 0):
                    take_out(t - 1, 1 - half)
                act.wait_ge(s_var, t + 1)
                nc.scalar.activation(rt[:], var[:], ACT.Sqrt, bias=eps[:, 0:1], scale=1.0 / DR).then_inc(s_rt, 1)

            def take_out(t, half):
                act.wait_ge(s_tr, t + 1)
                act.wait_ge(s_store[half], 8 * (t + half))
                nc.scalar.copy(retT[:, half, :], ptr[:]).then_inc(s_trev, 1)

            pairs(act, TILES, tile)
            take_out(TILES - 1, 1)

        @block.vector
        def _(dve):
            dve.wait_ge(s_rate, 1)
            dve.wait_ge(s_const, 64)
            for h in range(HR):
                if h:
                    dve.wait_ge(s_lin, 2 * h)
                nc.vector.tensor_scalar(dtmp[:], dist[:, 0], rate[:, 0, h:h + 1], None, ALU.mult).then_inc(s_lin, 1)
                dve.wait_ge(s_lin, 2 * h + 1)
                nc.vector.scalar_tensor_tensor(out=dmat[:, h % 2, h // 2, :], in0=dist[:, 1],
                                               scalar=rate[:, 1, h:h + 1], in1=dtmp[:], op0=ALU.mult,
                                               op1=ALU.add).then_inc(s_lin, 1)
            dve.wait_ge(s_dm, HR)
            nc.vector.tensor_scalar(dmat[:], dmat[:], float(DR) ** -0.5, None, ALU.mult).then_inc(s_d1, 1)
            dve.wait_ge(s_tab, 1)
            nc.vector.tensor_scalar(wk[:], wk[:], float(DR) ** -0.5, None, ALU.mult).then_inc(s_d1, 1)
            dve.wait_ge(s_d1, 2)

            def weigh(r, half, last):
                t = 2 * r + half
                dve.wait_ge(s_kv[half], 16 * (r + 1))
                dve.wait_ge(s_own, t - 1 if not (isinstance(r, int) and r == 0) else 0)
                v3 = kv[:, half, RW:2 * RW].rearrange("p (h d) -> p h d", h=HR)
                for d in range(2):
                    ins = nc.vector.tensor_tensor(vw[:, half, :, d, :], v3,
                                                  wk[:, d, :].unsqueeze(2).broadcast_to([P, HR, DR]), ALU.mult)
                ins.then_inc(s_vw, 1)

            pairs(dve, TILES, weigh)

            dve.wait_ge(s_ownev, TILES)
            scan = Steps(dve, s_d2, 0)
            for first, tiles in SEQS:
                nc.vector.memset(run[:, first, :, 0, :], 0.0)
                scan.chain(nc.vector.memset(run[:, first + tiles - 1, :, 1, :], 0.0))
                for i in range(tiles - 1):
                    steps2 = ((0, first + i, first + i + 1), (1, first + tiles - 1 - i, first + tiles - 2 - i))
                    for d, a, _ in steps2:
                        ins = nc.vector.tensor_tensor(stmp[:, d], run[:, a, :, d, :],
                                                      dec[:, d, :].unsqueeze(2).broadcast_to([P, PR, DR]), ALU.mult)
                    scan.chain(ins)
                    for d, a, b in steps2:
                        ins = nc.vector.tensor_tensor(run[:, b, :, d, :], stmp[:, d], own[:, a, :, d, :], ALU.add)
                    scan.chain(ins)
            nc.vector.tensor_copy(stmp[:, 0, 0, 0:1], dec[:, 0, 0:1]).then_inc(s_run, 1)

            steps = Steps(dve, s_d3, 3)
            by_half = "p (a b) d -> p b a d"

            def decayed(t):
                dve.wait_ge(s_sc, t + 1)
                dve.wait_ge(s_no, t)
                for odd in range(2):
                    ins = nc.vector.tensor_tensor(sc[:, odd].rearrange("p a i -> p (a i)"), psc[:, odd, :],
                                                  dmat[:, odd].rearrange("p a i -> p (a i)"), ALU.mult)
                ins.then_inc(s_scev, 1)
                dve.wait_ge(s_in, t + 1)
                dve.wait_ge(s_fab, t)
                for d, f in ((0, fa), (1, fb)):
                    for odd in range(2):
                        src = pin[:, odd, :].rearrange("p (a b d) -> p a b d", a=PR, b=2)[:, :, d, :]
                        ins = nc.vector.tensor_tensor(f[:, odd:HR:2, :], src,
                                                      wq[:, d, odd:HR:2].unsqueeze(2).broadcast_to([P, PR, DR]),
                                                      ALU.mult)
                ins.then_inc(s_inev, 1)

            decayed(0)

            def tile(r, half, last):
                t = 2 * r + half
                steps.begin(t)
                dve.wait_ge(s_no, t + 1)
                dve.wait_ge(s_fab, t + 1)
                nc.vector.tensor_tensor(o_t[:].rearrange("p h d -> p (h d)"), pno[:],
                                        fab[:].rearrange("p h d -> p (h d)"), ALU.add).then_inc(s_noev, 1)
                dve.wait_ge(s_noev, t + 1)
                steps.chain(nc.vector.tensor_reduce(mu[:], o_t[:], AX.X, ALU.add))
                steps.chain(nc.vector.tensor_scalar(mu[:], mu[:], -1.0 / DR, None, ALU.mult))
                dve.wait_ge(s_nrm, t)
                nc.vector.tensor_tensor(ctr[:], o_t[:], mu[:].unsqueeze(2).broadcast_to([P, HR, DR]),
                                        ALU.add).then_inc(s_ctr, 1)
                if not last:
                    decayed(t + 1)
                dve.wait_ge(s_sq, t + 1)
                nc.vector.tensor_reduce(var[:], sq[:], AX.X, ALU.add).then_inc(s_var, 1)
                dve.wait_ge(s_rt, t + 1)
                nc.vector.reciprocal(rs[:], rt[:]).then_inc(s_rs, 1)
                steps.chain(nc.vector.tensor_copy(dtmp[:, 0:1], index[:, 0:1]))
                steps.end()

            pairs(dve, TILES, tile)


def phase_latent(nc, tag, first, tiles, mid, w_q_up, w_kv_up, rope, ident_d, mixT):
    S = tiles * P
    QB, TB = tiles // 4, 4
    SCALE = float(NOPE + ROPE) ** -0.5
    with ExitStack() as ctx:
        def sb(name, shape, dt=F32):
            return ctx.enter_context(nc.sbuf_tensor(f"{tag}_{name}", shape, dt))

        sems = phase_sems(nc, ctx)

        def sem(name):
            return phase_sem(nc, sems, f"{tag}_{name}")

        ident = sb("ident", [P, P])
        angles = sb("angles", [P, tiles, 2, DR])
        c_hi, c_lo = sb("c_hi", [P, tiles, 512], F32R), sb("c_lo", [P, tiles, 512], F32R)
        wq_sb, wkv_sb = sb("wq_sb", [P, 2, NOPE + ROPE]), sb("wkv_sb", [P, NOPE + VD])
        wq_hi, wq_lo = sb("wq_hi", [P, 2, NOPE + ROPE], F32R), sb("wq_lo", [P, 2, NOPE + ROPE], F32R)
        wkv_hi, wkv_lo = sb("wkv_hi", [P, NOPE + VD], F32R), sb("wkv_lo", [P, NOPE + VD], F32R)
        kn_hi, kn_lo = sb("kn_hi", [P, S], F32R), sb("kn_lo", [P, S], F32R)
        qn_hi, qn_lo = sb("qn_hi", [P, S], F32R), sb("qn_lo", [P, S], F32R)
        qr_hi, qr_lo = sb("qr_hi", [ROPE, S], F32R), sb("qr_lo", [ROPE, S], F32R)
        v_hi, v_lo = sb("v_hi", [P, tiles, VD], F32R), sb("v_lo", [P, tiles, VD], F32R)
        part1, part2 = (sb(n, [P, tiles, ROPE]) for n in ("part1", "part2"))
        qr_tok = sb("qr_tok", [P, tiles, P])
        p_sb, pn_sb = sb("p_sb", [P, 2, S]), sb("pn_sb", [P, 2, S])
        pT_hi, pT_lo = sb("pT_hi", [P, 2, tiles, TB * P], F32R), sb("pT_lo", [P, 2, tiles, TB * P], F32R)
        ct = [y[:].rearrange("p a s -> p (a s)")[:, t * 512:(t + 1) * 512]
              for y in (p_sb, pn_sb) for t in range(tiles // 2)]
        oT = sb("oT", [P, 2, TB * P])
        peak, nbias, total, share = (sb(n, [P, 2]) for n in ("peak", "nbias", "total", "share"))

        ps = [ctx.enter_context(nc.psum_tensor(f"{tag}_ps{i}", [P, 1024], F32)) for i in range(2)]
        pt = ctx.enter_context(nc.psum_tensor(f"{tag}_pt", [P, 1024], F32))
        pr = ctx.enter_context(nc.psum_tensor(f"{tag}_pr", [P, 512], F32))
        po = ctx.enter_context(nc.psum_tensor(f"{tag}_po", [P, 512], F32))

        s_const = sem("const")
        s_ct = [sem(f"ct{t}") for t in range(tiles)]
        s_chi, s_clo = sem("chi"), sem("clo")
        s_w, s_whi, s_wlo = sem("w"), sem("whi"), sem("wlo")
        s_kn, s_knhi, s_knlo = sem("kn"), sem("knhi"), sem("knlo")
        s_qn, s_qnhi, s_qnlo = sem("qn"), sem("qnhi"), sem("qnlo")
        s_v, s_vhi, s_vlo = sem("v"), sem("vhi"), sem("vlo")
        s_qr, s_qrtok, s_qrt, s_qrhi, s_qrlo = sem("qr"), sem("qrtok"), sem("qrt"), sem("qrhi"), sem("qrlo")
        s_s, s_peak, s_exp, s_share, s_pn = sem("s"), sem("peak"), sem("exp"), sem("share"), sem("pn")
        s_pt, s_pthi, s_ptlo = sem("pt"), sem("pthi"), sem("ptlo")
        s_o, s_oev, s_store = sem("o"), sem("oev"), [sem("store0"), sem("store1")]
        s_d, s_turn = sem("d"), sem("turn")

        block = ctx.enter_context(nc.Block())
        wq_v = w_q_up.rearrange("(k p) (h n) -> h p k n", p=P, h=HM)
        wkv_v = w_kv_up.rearrange("p (h n) -> h p n", h=HM)
        HALVES = [(b * 512, min(512, S - b * 512)) for b in range((S + 511) // 512)]
        NB = len(HALVES)

        def heads(eng, body):
            body(0, False)
            with eng.Fori(1, HM - 1) as h:
                body(h, False)
            body(HM - 1, True)

        @block.sync
        def _(sp):
            sp.dma_start(ident[:], ident_d).then_inc(s_const, 16)
            sp.dma_start(angles[:].rearrange("p t a d -> p t (a d)"),
                         rope[first:first + tiles].rearrange("t p a d -> p t (a d)")).then_inc(s_const, 16)
            sp.dma_start(wq_sb[:], wq_v[0]).then_inc(s_w, 16)
            sp.dma_start(wkv_sb[:], wkv_v[0]).then_inc(s_w, 16)
            for t in range(tiles):
                sp.dma_start(ct[t], mid[first + t][:, M_CT:M_CT + 512]).then_inc(s_ct[t], 16)
            with sp.Fori(1, HM) as h:
                sp.wait_ge(s_wlo, 2 * h)
                sp.dma_start(wq_sb[:], wq_v[h]).then_inc(s_w, 16)
                sp.dma_start(wkv_sb[:], wkv_v[h]).then_inc(s_w, 16)

        @block.gpsimd
        def _(pool):
            mix_v = mixT.rearrange("t p (e i) -> e p t i", e=8)

            def head(h, last):
                for qb in range(QB):
                    n = h * QB + qb
                    half = (qb if QB == 2 else 0)
                    pool.wait_ge(s_oev, n + 1)
                    pool.dma_start(mix_v[4 + h][:, first + qb * TB:first + (qb + 1) * TB, :],
                                   oT[:, half, :].rearrange("p (t i) -> p t i", t=TB)).then_inc(s_store[half], 16)

            heads(pool, head)
            pool.wait_ge(s_store[0], 16 * HM)
            if QB == 2:
                pool.wait_ge(s_store[1], 16 * HM)

        @block.tensor
        def _(pe):
            pe.wait_ge(s_const, 32)

            def project_keys(p):
                pe.wait_ge(s_wlo, 2 * p + 2)
                if isinstance(p, int) and p == 0:
                    pe.wait_ge(s_clo, tiles)
                else:
                    pe.wait_ge(s_exp, tiles * p - 1)
                for b, (c0, w) in enumerate(HALVES):
                    cols = slice(c0 // P, (c0 + w) // P)
                    ins = three_passes(pe, ps[0][:, c0:c0 + w], wkv_hi[:, 0:NOPE], wkv_lo[:, 0:NOPE],
                                       c_hi[:, cols, 2 * P:3 * P], c_lo[:, cols, 2 * P:3 * P], True, True)
                    ins.then_inc(s_kn, 1)
                pe.wait_ge(s_exp, tiles * p)
                for b, (c0, w) in enumerate(HALVES):
                    cols = slice(c0 // P, (c0 + w) // P)
                    for k in range(2):
                        ins = three_passes(pe, ps[1][:, c0:c0 + w], wq_hi[:, k, 0:NOPE], wq_lo[:, k, 0:NOPE],
                                           c_hi[:, cols, k * P:(k + 1) * P], c_lo[:, cols, k * P:(k + 1) * P],
                                           k == 0, k == 1)
                    ins.then_inc(s_qn, 1)

            def project_rotary(p):
                pe.wait_ge(s_qrtok, p)
                for t in range(tiles):
                    for k in range(2):
                        ins = three_passes(pe, pr[:, t * ROPE:(t + 1) * ROPE],
                                           c_hi[:, t, k * P:(k + 1) * P], c_lo[:, t, k * P:(k + 1) * P],
                                           wq_hi[:, k, NOPE:], wq_lo[:, k, NOPE:], k == 0, k == 1)
                ins.then_inc(s_qr, 1)

            def project_values(p):
                pe.wait_ge(s_ptlo, (NB * tiles + 2 * NB) * p)
                for t in range(tiles):
                    ins = three_passes(pe, pt[:, t * P:(t + 1) * P],
                                       c_hi[:, t, 2 * P:3 * P], c_lo[:, t, 2 * P:3 * P],
                                       wkv_hi[:, NOPE:], wkv_lo[:, NOPE:], True, True)
                    if t % 4 == 3:
                        ins.then_inc(s_v, 1)
                pe.wait_ge(s_qrtok, p + 1)
                for b in range(NB):
                    pe.wait_ge(s_ptlo, (NB * tiles + 2 * NB) * p + b + 1)
                    for j in range(4):
                        t = 4 * b + j
                        ins = pe.transpose(pt[:, t * P:(t + 1) * P], qr_tok[:, t, :], ident[:])
                    ins.then_inc(s_qrt, 1)

            def scores(i):
                q = slice(i * P, (i + 1) * P)
                for c0, w in HALVES:
                    cols = slice(c0 // P, (c0 + w) // P)
                    three_passes(pe, ps[i % 2][:, c0:c0 + w], qn_hi[:, q], qn_lo[:, q],
                                 kn_hi[:, c0:c0 + w], kn_lo[:, c0:c0 + w], True, False)
                    ins = three_passes(pe, ps[i % 2][:, c0:c0 + w], qr_hi[:, q], qr_lo[:, q],
                                       c_hi[0:ROPE, cols, 3 * P:4 * P], c_lo[0:ROPE, cols, 3 * P:4 * P],
                                       False, True)
                ins.then_inc(s_s, 1)

            def weigh(h, qb, ks):
                if 0 in ks:
                    pe.wait_ge(s_ptlo, (NB * tiles + 2 * NB) * h + 2 * NB + NB * TB * (qb + 1))
                    pe.wait_ge(s_oev, QB * h + qb)
                for k in ks:
                    ins = three_passes(pe, po[:], v_hi[:, k, :], v_lo[:, k, :],
                                       pT_hi[:, qb % 2, k, :], pT_lo[:, qb % 2, k, :], k == 0, k == tiles - 1)
                if tiles - 1 in ks:
                    ins.then_inc(s_o, 1)

            def head(h, last):
                out0 = (NB * tiles + 2 * NB) * h + 2 * NB
                pe.wait_ge(s_knlo, NB * (h + 1))
                pe.wait_ge(s_qnlo, NB * (h + 1))
                pe.wait_ge(s_ptlo, out0)
                scores(0)
                for i in range(tiles):
                    qb, j = i // TB, i % TB
                    if i + 1 < tiles:
                        if i >= 1:
                            pe.wait_ge(s_exp, tiles * h + i)
                        scores(i + 1)
                    elif not last:
                        project_keys(h + 1)
                    if qb >= 1:
                        weigh(h, qb - 1, range(j * tiles // TB, (j + 1) * tiles // TB))
                    pe.wait_ge(s_pn, tiles * h + i + 1)
                    for b in range(NB):
                        pe.wait_ge(s_ptlo, out0 + max(0, NB * (i - 1) + b + 1))
                        for k in range(4):
                            t = 4 * b + k
                            ins = pe.transpose(pt[:, t * P:(t + 1) * P], pn_sb[:, i % 2, t * P:(t + 1) * P], ident[:])
                        ins.then_inc(s_pt, 1)
                if not last:
                    project_rotary(h + 1)
                weigh(h, QB - 1, range(tiles))
                if not last:
                    project_values(h + 1)

            project_keys(0)
            project_rotary(0)
            project_values(0)
            heads(pe, head)

        @block.scalar
        def _(act):
            for t in range(tiles):
                act.wait_ge(s_ct[t], 16)
                nc.scalar.copy(c_hi[:, t, :], ct[t]).then_inc(s_chi, 1)

            def split_weights(p):
                act.wait_ge(s_w, 32 * (p + 1))
                act.wait_ge(s_v, NB * p)
                nc.scalar.copy(wq_hi[:], wq_sb[:]).then_inc(s_whi, 1)
                nc.scalar.copy(wkv_hi[:], wkv_sb[:]).then_inc(s_whi, 1)

            def take_keys(p):
                for b, (c0, w) in enumerate(HALVES):
                    act.wait_ge(s_kn, NB * p + b + 1)
                    nc.scalar.copy(kn_hi[:, c0:c0 + w], ps[0][:, c0:c0 + w]).then_inc(s_knhi, 1)
                for b, (c0, w) in enumerate(HALVES):
                    act.wait_ge(s_qn, NB * p + b + 1)
                    nc.scalar.copy(qn_hi[:, c0:c0 + w], ps[1][:, c0:c0 + w]).then_inc(s_qnhi, 1)

            def take_values(p):
                for b, (c0, w) in enumerate(HALVES):
                    act.wait_ge(s_v, NB * p + b + 1)
                    nc.scalar.copy(v_hi[:].rearrange("p t d -> p (t d)")[:, c0:c0 + w],
                                   pt[:, c0:c0 + w]).then_inc(s_vhi, 1)
                for b, (c0, w) in enumerate(HALVES):
                    act.wait_ge(s_qrt, NB * p + b + 1)
                    nc.scalar.copy(qr_hi[:, c0:c0 + w], pt[0:ROPE, c0:c0 + w]).then_inc(s_qrhi, 1)

            def head(h, last):
                def take(i):
                    qb, j = i // TB, i % TB
                    for b in range(NB):
                        act.wait_ge(s_pt, NB * tiles * h + NB * i + b + 1)
                        nc.scalar.copy(pT_hi[:, qb % 2, 4 * b:4 * b + 4, j * P:(j + 1) * P],
                                       pt[:, b * 512:(b + 1) * 512].rearrange("p (k i) -> p k i", k=4)
                                       ).then_inc(s_pthi, 1)

                def take_out(qb):
                    act.wait_ge(s_o, QB * h + qb + 1)
                    act.wait_ge(s_store[qb], 16 * h)
                    nc.scalar.copy(oT[:, qb, :], po[:]).then_inc(s_oev, 1)

                for i in range(tiles):
                    act.wait_ge(s_peak, tiles * h + i + 1)
                    nc.scalar.activation(p_sb[:, i % 2, :], ps[i % 2][:, 0:S], ACT.Exp, bias=nbias[:, i % 2:i % 2 + 1],
                                         scale=SCALE, accum_out=total[:, i % 2:i % 2 + 1]).then_inc(s_exp, 1)
                    if i >= 1:
                        take(i - 1)
                    act.wait_ge(s_share, tiles * h + i + 1)
                    nc.scalar.activation(pn_sb[:, i % 2, :], p_sb[:, i % 2, :], ACT.Copy,
                                         scale=share[:, i % 2:i % 2 + 1]).then_inc(s_pn, 1)
                    if i == 1 and not last:
                        split_weights(h + 1)
                    if i >= TB and i % TB == TB - 1:
                        take_out(i // TB - 1)
                if not last:
                    take_keys(h + 1)
                take(tiles - 1)
                take_out(QB - 1)
                if not last:
                    take_values(h + 1)

            split_weights(0)
            take_keys(0)
            take_values(0)
            heads(act, head)

        @block.vector
        def _(dve):
            dve.wait_ge(s_const, 32)
            nc.vector.memset(qr_tok[:, :, ROPE:], 0.0)
            for t in range(tiles):
                dve.wait_ge(s_chi, t + 1)
                nc.vector.tensor_tensor(c_lo[:, t, :], ct[t], c_hi[:, t, :].bitcast(F32),
                                        ALU.subtract).then_inc(s_clo, 1)
            steps = Steps(dve, s_d, tiles)

            def split_weights(p):
                dve.wait_ge(s_whi, 2 * p + 1)
                nc.vector.tensor_tensor(wq_lo[:], wq_sb[:], wq_hi[:].bitcast(F32), ALU.subtract).then_inc(s_wlo, 1)
                dve.wait_ge(s_whi, 2 * p + 2)
                nc.vector.tensor_tensor(wkv_lo[:], wkv_sb[:], wkv_hi[:].bitcast(F32), ALU.subtract).then_inc(s_wlo, 1)

            def take_keys(p):
                for n, (lo, hi, src, ready, taken) in enumerate(((kn_lo, kn_hi, ps[0], s_knhi, s_knlo),
                                                                 (qn_lo, qn_hi, ps[1], s_qnhi, s_qnlo))):
                    for b, (c0, w) in enumerate(HALVES):
                        dve.wait_ge(ready, NB * p + b + 1)
                        nc.vector.tensor_tensor(lo[:, c0:c0 + w], src[:, c0:c0 + w], hi[:, c0:c0 + w].bitcast(F32),
                                                ALU.subtract).then_inc(taken, 1)

            def turn_queries(p):
                dve.wait_ge(s_qr, p + 1)
                dve.wait_ge(s_qrt, NB * p)
                x3 = pr[:, 0:tiles * ROPE].rearrange("p (t d) -> p t d", t=tiles)
                hw = ROPE // 2
                nc.vector.tensor_tensor(part1[:], x3, angles[:, :, 0, :], ALU.mult)
                nc.vector.tensor_tensor(part2[:, :, 0:hw], x3[:, :, hw:ROPE], angles[:, :, 1, 0:hw], ALU.mult)
                nc.vector.tensor_tensor(part2[:, :, hw:ROPE], x3[:, :, 0:hw], angles[:, :, 1, hw:ROPE],
                                        ALU.mult).then_inc(s_turn, 1)
                dve.wait_ge(s_turn, p + 1)
                nc.vector.tensor_tensor(qr_tok[:, :, 0:ROPE], part1[:], part2[:], ALU.add).then_inc(s_qrtok, 1)
                dve.wait_ge(s_qrtok, p + 1)

            def take_values(p):
                for b, (c0, w) in enumerate(HALVES):
                    dve.wait_ge(s_vhi, NB * p + b + 1)
                    flat = slice(c0, c0 + w)
                    nc.vector.tensor_tensor(v_lo[:].rearrange("p t d -> p (t d)")[:, flat], pt[:, flat],
                                            v_hi[:].rearrange("p t d -> p (t d)")[:, flat].bitcast(F32),
                                            ALU.subtract).then_inc(s_ptlo, 1)
                for b, (c0, w) in enumerate(HALVES):
                    dve.wait_ge(s_qrhi, NB * p + b + 1)
                    nc.vector.tensor_tensor(qr_lo[:, c0:c0 + w], pt[0:ROPE, c0:c0 + w],
                                            qr_hi[:, c0:c0 + w].bitcast(F32), ALU.subtract).then_inc(s_ptlo, 1)

            def head(h, last):
                steps.begin(h)

                def take(i):
                    qb, j = i // TB, i % TB
                    for b in range(NB):
                        dve.wait_ge(s_pthi, NB * tiles * h + NB * i + b + 1)
                        nc.vector.tensor_tensor(pT_lo[:, qb % 2, 4 * b:4 * b + 4, j * P:(j + 1) * P],
                                                pt[:, b * 512:(b + 1) * 512].rearrange("p (k i) -> p k i", k=4),
                                                pT_hi[:, qb % 2, 4 * b:4 * b + 4, j * P:(j + 1) * P].bitcast(F32),
                                                ALU.subtract).then_inc(s_ptlo, 1)

                for i in range(tiles):
                    one = slice(i % 2, i % 2 + 1)
                    dve.wait_ge(s_s, tiles * h + i + 1)
                    steps.chain(nc.vector.tensor_reduce(peak[:, one], ps[i % 2][:, 0:S], AX.X, ALU.max))
                    nc.vector.tensor_scalar(nbias[:, one], peak[:, one], -SCALE, None, ALU.mult).then_inc(s_peak, 1)
                    dve.wait_ge(s_exp, tiles * h + i + 1)
                    nc.vector.reciprocal(share[:, one], total[:, one]).then_inc(s_share, 1)
                    if i >= 1:
                        take(i - 1)
                    if i == 1 and not last:
                        split_weights(h + 1)
                if not last:
                    take_keys(h + 1)
                take(tiles - 1)
                if not last:
                    turn_queries(h + 1)
                    take_values(h + 1)
                steps.end()

            split_weights(0)
            take_keys(0)
            turn_queries(0)
            take_values(0)
            heads(dve, head)


NE, NG, EPG = 32, 4, 8
FE = 512
ROWS = TILES * P
MORE = 2 * ROWS // (P + 1)
AHEAD = 5
NBLK = NE + MORE + AHEAD
NEVER = 1.0e30
NOWHERE = 1 << 20


def phase_mix(nc, mixT, x_all, w_out, g_ffn, w_rg, w_re, ident_d, route_d, blocks_d, x_mid, h_rows, table,
              gates, blocks, n_pairs, s_tick, s_tock, raw, s_raw0, w_exp):
    with ExitStack() as ctx:
        def sb(name, shape, dt=F32):
            return ctx.enter_context(nc.sbuf_tensor("d_" + name, shape, dt))

        sems = phase_sems(nc, ctx)

        def sem(name):
            return phase_sem(nc, sems, "d_" + name)

        ident = sb("ident", [P, P])
        route = sb("route", [P, 2 * NE + 2 * P])
        e_id, e_grp = route[:, 0:NE], route[:, NE:2 * NE]
        before, ones = route[:, 2 * NE:2 * NE + P], route[:, 2 * NE + P:]
        stage = sb("stage", [P, 3, D])
        w_hi, w_lo = sb("w_hi", [P, KD, D], F32R), sb("w_lo", [P, KD, D], F32R)
        w_r = sb("w_r", [P, KD, NG + NE])
        g_row = sb("g_row", [P, D])
        eps = sb("eps", [P, 1])
        mx, xr = sb("mx", [P, 2, D]), sb("xr", [P, 2, D])
        mT_hi, mT_lo = sb("mT_hi", [P, 2, D], F32R), sb("mT_lo", [P, 2, D], F32R)
        x2, h_sb, hT = sb("x2", [P, 2, D]), sb("h_sb", [P, 2, D]), sb("hT", [P, D])
        junk = sb("junk", [P, D], BF16)
        ssq, root, rstd = sb("ssq", [P, 1]), sb("root", [P, 1]), sb("rstd", [P, 1])
        g8, g8max, e8 = sb("g8", [P, 8]), sb("g8max", [P, 8]), sb("e8", [P, 8])
        g8i, e8i = sb("g8i", [P, 8], U32), sb("e8i", [P, 8], U32)
        gf, ef = sb("gf", [P, 1]), sb("ef", [P, 2])
        mask, pen, lem = sb("mask", [P, NE]), sb("pen", [P, NE]), sb("lem", [P, NE])
        hot = sb("hot", [P, 3, NE])
        seen = sb("seen", [P, NE])
        prod = sb("prod", [P, NE])
        place, spot = sb("place", [P, 2]), sb("spot", [P, 2])
        spot_i = sb("spot_i", [P, 2, 2], I32)
        entry = sb("entry", [P, 2, 2, 2], I32)
        empty = sb("empty", [P, NE * ROWS // P * 2], I32)
        glog, elog = sb("glog", [P, TILES, NG]), sb("elog", [P, TILES, 2])
        gm, gz, ge, gd, gr = (sb(n, [P, TILES]) for n in ("gm", "gz", "ge", "gd", "gr"))
        gx = sb("gx", [P, TILES, NG])
        many_i, many, incl = sb("many_i", [P, NE], I32), sb("many", [P, NE]), sb("incl", [P, NE])
        step_no = sb("step_no", [P, MORE + AHEAD])
        upto, uses = sb("upto", [P, MORE + AHEAD, NE]), sb("uses", [P, MORE + AHEAD, NE])
        who, gone, base = (sb(n, [P, MORE + AHEAD]) for n in ("who", "gone", "base"))

        po = [ctx.enter_context(nc.psum_tensor(f"d_po{i}", [P, 1024], F32)) for i in range(2)]
        pt = ctx.enter_context(nc.psum_tensor("d_pt", [P, 1024], F32))
        pr = ctx.enter_context(nc.psum_tensor("d_pr", [P, 512], F32))
        pp = ctx.enter_context(nc.psum_tensor("d_pp", [P, 512], F32))

        s_const, s_init, s_zero = sem("const"), sem("init"), sem("zero")
        s_raw = [sem(f"raw{i}") for i in range(3)]
        s_whi, s_wlo = sem("whi"), sem("wlo")
        s_in, s_xr = ([sem(f"{n}{i}") for i in range(2)] for n in ("in", "xr"))
        s_mhi, s_mlo, s_po, s_x2, s_sq, s_root, s_rstd, s_h = (
            sem(n) for n in ("mhi", "mlo", "po", "x2", "sq", "root", "rstd", "h"))
        s_ht, s_htev, s_r, s_rev, s_hot, s_pp, s_spot = (sem(n) for n in ("ht", "htev", "r", "rev", "hot", "pp", "spot"))
        s_keep = [sem("keep0"), sem("keep1")]
        s_tab = [sem("tab0"), sem("tab1")]
        s_d, s_q, s_gexp, s_count, s_g = sem("d"), sem("q"), sem("gexp"), sem("count"), sem("g")

        block = ctx.enter_context(nc.Block())

        @block.sync
        def _(sp):
            sp.dma_start(ident[:], ident_d).then_inc(s_const, 16)
            sp.dma_start(route[:], route_d).then_inc(s_const, 16)
            sp.dma_start(g_row[:], g_ffn.partition_broadcast(P)).then_inc(s_const, 16)
            sp.dma_start(w_r[:, :, 0:NG], w_rg.rearrange("(p k) e -> p k e", k=KD)).then_inc(s_const, 16)
            sp.dma_start(w_r[:, :, NG:], w_re.rearrange("(p k) e -> p k e", k=KD)).then_inc(s_const, 16)
            sp.dma_start(blocks[:].rearrange("p a n -> p (a n)"), blocks_d).then_inc(s_const, 16)
            sp.dma_start(mx[:, 0, :], mixT[0]).then_inc(s_in[0], 16)
            sp.dma_start(xr[:, 0, :], x_all[0]).then_inc(s_xr[0], 16)
            w_v = w_out.rearrange("(k p) n -> p k n", p=P)
            for k in range(KD):
                if k >= 3:
                    sp.wait_ge(s_wlo, k - 2)
                sp.dma_start(stage[:, k % 3, :], w_v[:, k, :]).then_inc(s_raw[k % 3], 16)

            def tile(r, half, last):
                t = 2 * r + half
                if not last:
                    behind = not (isinstance(r, int) and r == 0 and half == 0)
                    if behind:
                        sp.wait_ge(s_mlo, t)
                        sp.wait_ge(s_const, 96)
                    sp.dma_start(mx[:, 1 - half, :], mixT[t + 1]).then_inc(s_in[1 - half], 16)
                    if behind:
                        sp.wait_ge(s_x2, t)
                        sp.wait_ge(s_const, 96)
                    sp.dma_start(xr[:, 1 - half, :], x_all[t + 1]).then_inc(s_xr[1 - half], 16)

            pairs(sp, TILES, tile)
            for j in range(6):
                sp.dma_start(raw[:, j // 2, raw_span(j)], w_exp[j // 2][0][:, raw_span(j)]).then_inc(s_raw0[j], 16)

        @block.gpsimd
        def _(pool):
            nc.gpsimd.memset(eps[:], EPS).then_inc(s_init, 1)
            nc.gpsimd.memset(empty[:], NOWHERE).then_inc(s_zero, 1)
            nc.gpsimd.iota(entry[:, :, :, 0], pattern=[[-P, 2], [0, 2]], base=0, channel_multiplier=1)
            nc.gpsimd.iota(entry[:, :, :, 1], pattern=[[-2 * P, 2], [1, 2]], base=0,
                           channel_multiplier=2).then_inc(s_init, 1)
            nc.gpsimd.iota(step_no[:], pattern=[[1, MORE + AHEAD]], base=0, channel_multiplier=0,
                           allow_small_or_imprecise_dtypes=True).then_inc(s_init, 1)
            pool.wait_ge(s_zero, 1)
            pool.dma_start(table.rearrange("(p n) a -> p (n a)", p=P), empty[:]).then_inc(s_tab[1], 16)
            pool.wait_ge(s_tab[1], 16)

            def tile(r, half, last):
                t = 2 * r + half
                pool.wait_ge(s_x2, t + 1)
                settle_waits(pool, s_tick)
                pool.dma_start(x_mid[t], x2[:, half, :]).then_inc(s_keep[half], 16)
                pool.wait_ge(s_h, t + 1)
                settle_waits(pool, s_tick)
                pool.dma_start(h_rows[t], h_sb[:, half, :]).then_inc(s_keep[half], 16)
                if not (isinstance(t, int) and t == 0):
                    enter(t - 1, 1 - half)

            def enter(t, half):
                pool.wait_ge(s_spot, t + 1)
                settle_waits(pool, s_tick)
                for c in range(2):
                    pool.indirect_dma_start(out=table, out_offset=bass.IndirectOffsetOnAxis(
                        ap=spot_i[:, half, c:c + 1], axis=0), in_=entry[:, half, c, :],
                        in_offset=None).then_inc(s_tab[half], 16)

            pairs(pool, TILES, tile)
            enter(TILES - 1, 1)
            for half in range(2):
                pool.wait_ge(s_keep[half], 16 * TILES)
                pool.wait_ge(s_tab[half], 16 * TILES + 16 * half)

        @block.tensor
        def _(pe):
            pe.wait_ge(s_const, 96)

            def project(t, half):
                pe.wait_ge(s_mlo, t + 1)
                pe.wait_ge(s_x2, t - 1 if not isinstance(t, int) else max(0, t - 1))
                for b in range(2):
                    for k in range(KD):
                        if isinstance(t, int) and t == 0 and b == 0:
                            pe.wait_ge(s_wlo, k + 1)
                        rows = slice(k * P, (k + 1) * P)
                        ins = three_passes(pe, po[half][:, b * 512:(b + 1) * 512], mT_hi[:, half, rows],
                                           mT_lo[:, half, rows], w_hi[:, k, b * 512:(b + 1) * 512],
                                           w_lo[:, k, b * 512:(b + 1) * 512], k == 0, k == KD - 1)
                ins.then_inc(s_po, 1)

            project(0, 0)

            def place_in_queue(t):
                pe.wait_ge(s_hot, t + 1)
                pe.matmul(pp[:, 0:NE], before, hot[:, 2, :], start=True, stop=False)
                pe.matmul(pp[:, 0:NE], ones, seen[:], start=False, stop=True).then_inc(s_pp, 1)

            def tile(r, half, last):
                t = 2 * r + half
                if not last:
                    project(t + 1, 1 - half)
                pe.wait_ge(s_h, t + 1)
                pe.wait_ge(s_htev, 2 * t)
                for b in range(2):
                    for j in range(4):
                        k = 4 * b + j
                        ins = pe.transpose(pt[:, k * P:(k + 1) * P], h_sb[:, half, k:D:KD], ident[:])
                    ins.then_inc(s_ht, 1)
                if not (isinstance(t, int) and t == 0):
                    place_in_queue(t - 1)
                pe.wait_ge(s_htev, 2 * t + 2)
                pe.wait_ge(s_rev, t)
                for k in range(KD):
                    ins = pe.matmul(pr[:, 0:NG + NE], hT[:, k * P:(k + 1) * P], w_r[:, k, :],
                                    start=k == 0, stop=k == KD - 1)
                ins.then_inc(s_r, 1)

            pairs(pe, TILES, tile)
            place_in_queue(TILES - 1)
            pe.wait_ge(s_spot, TILES + 1)
            pe.matmul(pp[:, 0:NE], ones, seen[:], start=True, stop=True).then_inc(s_count, 1)

        @block.scalar
        def _(act):
            def split(t, r, half):
                act.wait_ge(s_in[half], 16 * (r + 1))
                act.wait_ge(s_po, t - 1 if not isinstance(t, int) else max(0, t - 1))
                nc.scalar.copy(mT_hi[:, half, :], mx[:, half, :]).then_inc(s_mhi, 1)

            split(0, 0, 0)
            for k in range(KD):
                act.wait_ge(s_raw[k % 3], 16 * (k // 3 + 1))
                nc.scalar.copy(w_hi[:, k, :], stage[:, k % 3, :]).then_inc(s_whi, 1)
            split(1, 0, 1)
            act.wait_ge(s_init, 1)

            def tile(r, half, last):
                t = 2 * r + half
                act.wait_ge(s_x2, t + 1)
                act.wait_ge(s_rstd, t)
                nc.scalar.activation(junk[:], x2[:, half, :], ACT.Square, accum_out=ssq[:]).then_inc(s_sq, 1)
                act.wait_ge(s_sq, t + 1)
                nc.scalar.activation(root[:], ssq[:], ACT.Sqrt, bias=eps[:], scale=1.0 / D).then_inc(s_root, 1)
                if not (isinstance(r, int) and r == TILES // 2 - 1):
                    split(t + 2, r + 1, half)
                for b in range(2):
                    act.wait_ge(s_ht, 2 * t + b + 1)
                    act.wait_ge(s_r, t)
                    nc.scalar.copy(hT[:, b * 512:(b + 1) * 512], pt[:, b * 512:(b + 1) * 512]).then_inc(s_htev, 1)

            pairs(act, TILES, tile)
            act.wait_ge(s_gexp, 1)
            nc.scalar.activation(gx[:], gx[:], ACT.Exp).then_inc(s_g, 1)
            nc.scalar.activation(gd[:], gd[:], ACT.Exp).then_inc(s_g, 1)

        @block.vector
        def _(dve):
            dve.wait_ge(s_const, 96)
            nc.vector.memset(g8[:], -NEVER)
            nc.vector.memset(seen[:], 0.0)
            dve.wait_ge(s_init, 3)
            def split(t, half):
                dve.wait_ge(s_mhi, t + 1)
                nc.vector.tensor_tensor(mT_lo[:, half, :], mx[:, half, :], mT_hi[:, half, :].bitcast(F32),
                                        ALU.subtract).then_inc(s_mlo, 1)

            split(0, 0)
            for k in range(KD):
                dve.wait_ge(s_whi, k + 1)
                nc.vector.tensor_tensor(w_lo[:, k, :], stage[:, k % 3, :], w_hi[:, k, :].bitcast(F32),
                                        ALU.subtract).then_inc(s_wlo, 1)
            split(1, 1)
            steps = Steps(dve, s_d, 11)
            queue_steps = Steps(dve, s_q, 4)

            def queue(t, half, again):
                queue_steps.begin(t)
                dve.wait_ge(s_pp, t + 1)
                for c in range(2):
                    nc.vector.tensor_tensor(pen[:] if c else prod[:], hot[:, c, :], pp[:, 0:NE], ALU.mult)
                queue_steps.chain(nc.vector.tensor_tensor(seen[:], seen[:], hot[:, 2, :], ALU.add))
                for c in range(2):
                    ins = nc.vector.tensor_reduce(place[:, c:c + 1], pen[:] if c else prod[:], AX.X, ALU.add)
                queue_steps.chain(ins)
                queue_steps.chain(nc.vector.scalar_tensor_tensor(out=spot[:], in0=ef[:], scalar=float(ROWS),
                                                                 in1=place[:], op0=ALU.mult, op1=ALU.add))
                dve.wait_ge(s_tab[half], 16 * t)
                if again:
                    nc.vector.tensor_scalar(entry[:, half, :, 0], entry[:, half, :, 0], float(2 * P), None, ALU.add)
                    nc.vector.tensor_scalar(entry[:, half, :, 1], entry[:, half, :, 1], float(4 * P), None, ALU.add)
                queue_steps.chain(nc.vector.tensor_copy(spot_i[:, half, :], spot[:]))
                nc.vector.tensor_copy(pen[:, 0:1], spot[:, 0:1]).then_inc(s_spot, 1)
                queue_steps.end()

            def tile(r, half, last):
                t = 2 * r + half
                steps.begin(t)
                dve.wait_ge(s_po, t + 1)
                dve.wait_ge(s_xr[half], 16 * (r + 1))
                dve.wait_ge(s_keep[half], 32 * r)
                nc.vector.tensor_tensor(x2[:, half, :], po[half][:], xr[:, half, :], ALU.add).then_inc(s_x2, 1)
                dve.wait_ge(s_root, t + 1)
                nc.vector.reciprocal(rstd[:], root[:]).then_inc(s_rstd, 1)
                dve.wait_ge(s_rstd, t + 1)
                nc.vector.scalar_tensor_tensor(out=h_sb[:, half, :], in0=x2[:, half, :], scalar=rstd[:, 0:1],
                                               in1=g_row[:], op0=ALU.mult, op1=ALU.mult).then_inc(s_h, 1)
                if not (isinstance(r, int) and r == TILES // 2 - 1):
                    split(t + 2, half)
                if not (isinstance(t, int) and t == 0):
                    queue(t - 1, 1 - half, not (isinstance(t, int) and t == 1))
                dve.wait_ge(s_r, t + 1)
                nc.vector.tensor_copy(glog[:, t, :], pr[:, 0:NG])
                steps.chain(nc.vector.tensor_copy(g8[:, 0:NG], pr[:, 0:NG]))
                settle_waits(dve, s_tock)
                steps.chain(nc.vector.max(g8max[:], g8[:]))
                settle_waits(dve, s_tock)
                steps.chain(nc.vector.max_index(g8i[:], g8max[:], g8[:]))
                steps.chain(nc.vector.tensor_copy(gf[:], g8i[:, 0:1]))
                steps.chain(nc.vector.tensor_scalar(mask[:], e_grp, gf[:, 0:1], None, ALU.is_equal))
                nc.vector.tensor_tensor(lem[:], pr[:, NG:NG + NE], mask[:], ALU.mult).then_inc(s_rev, 1)
                dve.wait_ge(s_rev, t + 1)
                steps.chain(nc.vector.tensor_scalar(pen[:], mask[:], 1.0, NEVER, ALU.subtract, ALU.mult))
                steps.chain(nc.vector.tensor_tensor(lem[:], lem[:], pen[:], ALU.add))
                settle_waits(dve, s_tock)
                steps.chain(nc.vector.max(e8[:], lem[:]))
                settle_waits(dve, s_tock)
                steps.chain(nc.vector.max_index(e8i[:], e8[:], lem[:]))
                nc.vector.tensor_copy(elog[:, t, :], e8[:, 0:2])
                steps.chain(nc.vector.tensor_copy(ef[:], e8i[:, 0:2]))
                for c in range(2):
                    ins = nc.vector.tensor_scalar(hot[:, c, :], e_id, ef[:, c:c + 1], None, ALU.is_equal)
                steps.chain(ins)
                nc.vector.tensor_tensor(hot[:, 2, :], hot[:, 0, :], hot[:, 1, :], ALU.add).then_inc(s_hot, 1)
                steps.end()

            pairs(dve, TILES, tile)
            queue(TILES - 1, 1, True)
            tail = Steps(dve, s_gexp, 0)
            dve.wait_ge(s_spot, TILES)
            nc.vector.tensor_copy(prod[:, 0:1], spot[:, 0:1]).then_inc(s_spot, 1)
            nc.vector.tensor_reduce(gm[:], glog[:], AX.X, ALU.max).then_inc(s_zero, 1)
            dve.wait_ge(s_zero, 2)
            nc.vector.tensor_tensor(gx[:], glog[:], gm[:].unsqueeze(2).broadcast_to([P, TILES, NG]), ALU.subtract)
            nc.vector.tensor_tensor(gd[:], elog[:, :, 1], elog[:, :, 0], ALU.subtract).then_inc(s_gexp, 1)
            dve.wait_ge(s_g, 2)
            tail.n = 1
            nc.vector.tensor_reduce(gz[:], gx[:], AX.X, ALU.add)
            tail.chain(nc.vector.tensor_scalar(ge[:], gd[:], 1.0, None, ALU.add))
            tail.chain(nc.vector.tensor_tensor(ge[:], ge[:], gz[:], ALU.mult))
            tail.chain(nc.vector.reciprocal(gr[:], ge[:]))
            nc.vector.tensor_copy(gates[:, :, 0], gr[:])
            nc.vector.tensor_tensor(gates[:, :, 1], gr[:], gd[:], ALU.mult)
            dve.wait_ge(s_count, 1)
            tail.chain(nc.vector.tensor_scalar(many_i[:], pp[:, 0:NE], 1.0, 1.0, ALU.max, ALU.subtract))
            tail.chain(nc.vector.tensor_scalar(many_i[:], many_i[:], 7, None, ALU.logical_shift_right))
            tail.chain(nc.vector.tensor_copy(many[:], many_i[:]))
            tail.chain(nc.vector.tensor_tensor_scan(incl[:], ones[:, 0:NE], many[:], 0.0, ALU.mult, ALU.add))
            shape = [P, MORE + AHEAD, NE]
            tail.chain(nc.vector.tensor_tensor(upto[:], incl[:].unsqueeze(1).broadcast_to(shape),
                                               step_no[:].unsqueeze(2).broadcast_to(shape), ALU.is_le))
            nc.vector.tensor_reduce(who[:], upto[:], AX.X, ALU.add)
            tail.chain(nc.vector.tensor_tensor(uses[:], upto[:], many[:].unsqueeze(1).broadcast_to(shape), ALU.mult))
            nc.vector.tensor_reduce(gone[:], uses[:], AX.X, ALU.add)
            tail.chain(nc.vector.tensor_scalar(who[:], who[:], float(NE - 1), None, ALU.min))
            tail.chain(nc.vector.tensor_tensor(base[:], step_no[:], gone[:], ALU.subtract))
            tail.chain(nc.vector.tensor_scalar(base[:], base[:], 1.0, float(P), ALU.add, ALU.mult))
            tail.chain(nc.vector.scalar_tensor_tensor(out=base[:], in0=who[:], scalar=float(ROWS), in1=base[:],
                                                      op0=ALU.mult, op1=ALU.add))
            nc.vector.tensor_copy(blocks[:, 0, NE:], who[0:1, :])
            nc.vector.tensor_scalar(blocks[:, 1, NE:], base[0:1, :], float(NE * ROWS - P), None, ALU.min)
            tail.chain(nc.vector.tensor_scalar(many_i[:, 0:1], incl[:, NE - 1:NE], float(NE + 1), None, ALU.add))
            tail.chain(nc.vector.tensor_scalar(many_i[:, 0:1], many_i[:, 0:1], 1, None, ALU.logical_shift_right))
            nc.vector.tensor_copy(n_pairs[:, 0:1], many_i[0:1, 0:1])
            tail.chain(nc.vector.tensor_scalar(n_pairs[:, 1:2], many_i[0:1, 0:1], -1.0, None, ALU.add))


def raw_span(j):
    return slice(2048 * (j % 2), 2048 * (j % 2 + 1))


def phase_experts(nc, w_exp, ident_d, h_rows, table, y_rows, blocks, n_pairs, s_tick, raw, s_raw):
    KF = FE // P
    with ExitStack() as ctx:
        def sb(name, shape, dt=F32):
            return ctx.enter_context(nc.sbuf_tensor("e_" + name, shape, dt))

        sems = phase_sems(nc, ctx)

        def sem(name):
            return phase_sem(nc, sems, "e_" + name)

        ident = sb("ident", [P, P])
        w_hi, w_lo = sb("w_hi", [P, 3, 4096], F32R), sb("w_lo", [P, 3, 4096], F32R)
        who = [sb(f"who{i}", [P, 2], I32) for i in range(2)]
        code = [sb(f"code{i}", [P, 1], I32) for i in range(2)]
        xg = [sb(f"xg{i}", [P, D]) for i in range(2)]
        xT_hi, xT_lo = sb("xT_hi", [P, D], F32R), sb("xT_lo", [P, D], F32R)
        act_g, h_sb = sb("act_g", [P, FE]), sb("h_sb", [P, FE])
        hT_hi, hT_lo = sb("hT_hi", [P, FE], F32R), sb("hT_lo", [P, FE], F32R)
        y_sb = [sb(f"y_sb{i}", [P, D]) for i in range(2)]

        pg, pu = (ctx.enter_context(nc.psum_tensor(f"e_{n}", [P, 512], F32)) for n in ("pg", "pu"))
        px = ctx.enter_context(nc.psum_tensor("e_px", [P, 1024], F32))
        ph = ctx.enter_context(nc.psum_tensor("e_ph", [P, 512], F32))
        py = ctx.enter_context(nc.psum_tensor("e_py", [P, 1024], F32))

        s_const = sem("const")
        s_whi = [sem(f"whi{j}") for j in range(6)]
        s_wlo = [sem(f"wlo{j}") for j in range(6)]
        s_code = sem("code")
        s_xt, s_xhi, s_xlo = sem("xt"), sem("xhi"), sem("xlo")
        s_who, s_xg, s_store = ([sem(f"{n}{i}") for i in range(2)] for n in ("who", "xg", "store"))
        s_gate, s_up, s_silu, s_h, s_ht, s_hhi, s_hlo = (sem(n) for n in ("gate", "up", "silu", "h", "ht", "hhi", "hlo"))
        s_y, s_ya, s_yd = sem("y"), sem("ya"), sem("yd")

        block = ctx.enter_context(nc.Block())
        span = raw_span

        def pair_count(eng):
            return eng.value_load(n_pairs[0:1, 0:1], min_val=NE // 2, max_val=(NE + MORE + 1) // 2)

        def each_block(eng, body):
            for half in range(2):
                body(0, half)
            with eng.Fori(1, pair_count(eng)) as r:
                for half in range(2):
                    body(r, half)

        @block.sync
        def _(sp):
            sp.dma_start(ident[:], ident_d).then_inc(s_const, 16)

            def load(r, half):
                n = 2 * r + half
                if isinstance(r, int) and n == 0:
                    return
                e = n if isinstance(r, int) else sp.value_load(blocks[0:1, 0, bass.ds(n, 1)], min_val=0,
                                                               max_val=NE - 1)
                for j in range(6):
                    sp.wait_ge(s_wlo[j], n)
                    sp.dma_start(raw[:, j // 2, span(j)], w_exp[j // 2][e][:, span(j)]).then_inc(s_raw[j], 16)

            each_block(sp, load)

        @block.gpsimd
        def _(pool):
            def gather(n, r, half, base):
                pool.dma_start(who[half][:], table[bass.ds(base, P), :]).then_inc(s_who[half], 16)
                pool.wait_ge(s_who[half], 16 * (r + 1))
                pool.wait_ge(s_xt, 2 * n - 2 if not (isinstance(r, int) and r == 0) else 0)
                settle_waits(pool, s_tick)
                pool.indirect_dma_start(out=xg[half][:], out_offset=None, in_=h_rows,
                                        in_offset=bass.IndirectOffsetOnAxis(ap=who[half][:, 0:1], axis=0),
                                        bounds_check=ROWS - 1, oob_is_err=False).then_inc(s_xg[half], 16)

            for half in range(2):
                nc.gpsimd.memset(xg[half][:], 0.0).then_inc(s_code, 1)
            pool.wait_ge(s_code, 2)
            for half in range(2):
                gather(half, 0, half, half * ROWS)

            def step(r, half):
                n = 2 * r + half
                if isinstance(r, int):
                    ahead = (n + 2) * ROWS
                else:
                    ahead = pool.value_load(blocks[0:1, 1, bass.ds(n + 2, 1)], min_val=0, max_val=NE * ROWS - P)
                pool.wait_ge(s_xg[half], 16 * (r + 1))
                pool.wait_ge(s_store[half], 16 * r)
                settle_waits(pool, s_tick)
                nc.gpsimd.tensor_copy(code[half][:], who[half][:, 1:2]).then_inc(s_code, 1)
                pool.wait_ge(s_code, n + 3)
                settle_waits(pool, s_tick)
                gather(n + 2, r + 1, half, ahead)
                pool.wait_ge(s_ya, n + 1)
                pool.wait_ge(s_yd, n + 1)
                settle_waits(pool, s_tick)
                pool.indirect_dma_start(out=y_rows, out_offset=bass.IndirectOffsetOnAxis(ap=code[half][:, 0:1], axis=0),
                                        in_=y_sb[half][:], in_offset=None, bounds_check=2 * ROWS - 1,
                                        oob_is_err=False).then_inc(s_store[half], 16)

            each_block(pool, step)
            pairs_done = pair_count(pool)
            for half in range(2):
                pool.wait_ge(s_store[half], 16 * pairs_done)

        @block.tensor
        def _(pe):
            pe.wait_ge(s_const, 16)

            def transpose_rows(b, half):
                for j in range(4):
                    k = 4 * b + j
                    ins = pe.transpose(px[:, k * P:(k + 1) * P], xg[half][:, k:D:KD], ident[:])
                ins.then_inc(s_xt, 1)

            pe.wait_ge(s_xg[0], 16)
            transpose_rows(0, 0)
            transpose_rows(1, 0)

            def step(r, half):
                n = 2 * r + half
                pe.wait_ge(s_xlo, 2 * (n + 1))
                for m, (acc, done) in enumerate(((pg, s_gate), (pu, s_up))):
                    if m == 0:
                        pe.wait_ge(s_h, n)
                    for k in range(KD):
                        if k % 4 == 0:
                            pe.wait_ge(s_wlo[2 * m + k // 4], n + 1)
                        rows, cols = slice(k * P, (k + 1) * P), slice(k * FE, (k + 1) * FE)
                        ins = three_passes(pe, acc[:], xT_hi[:, rows], xT_lo[:, rows], w_hi[:, m, cols],
                                           w_lo[:, m, cols], k == 0, k == KD - 1)
                    ins.then_inc(done, 1)
                pe.wait_ge(s_xg[1 - half], 16 * (r + half + 1))
                transpose_rows(0, 1 - half)
                pe.wait_ge(s_h, n + 1)
                pe.wait_ge(s_hlo, n)
                for k in range(KF):
                    ins = pe.transpose(ph[:, k * P:(k + 1) * P], h_sb[:, k:FE:KF], ident[:])
                ins.then_inc(s_ht, 1)
                transpose_rows(1, 1 - half)
                pe.wait_ge(s_hlo, n + 1)
                pe.wait_ge(s_ya, n)
                pe.wait_ge(s_yd, n)
                for k in range(KF):
                    if k % 2 == 0:
                        pe.wait_ge(s_wlo[4 + k // 2], n + 1)
                    for b in range(2):
                        rows, cols = slice(k * P, (k + 1) * P), slice(k * D + b * 512, k * D + (b + 1) * 512)
                        ins = three_passes(pe, py[:, b * 512:(b + 1) * 512], hT_hi[:, rows], hT_lo[:, rows],
                                           w_hi[:, 2, cols], w_lo[:, 2, cols], k == 0, k == KF - 1)
                ins.then_inc(s_y, 1)

            each_block(pe, step)

        def free_after(eng, j, n):
            eng.wait_ge((s_gate, s_up, s_y)[j // 2], n)

        @block.scalar
        def _(act):
            def split(j, n):
                act.wait_ge(s_raw[j], 16 * (n + 1))
                free_after(act, j, n)
                nc.scalar.copy(w_hi[:, j // 2, span(j)], raw[:, j // 2, span(j)]).then_inc(s_whi[j], 1)

            def rows_hi(n):
                for b in range(2):
                    act.wait_ge(s_xt, 2 * n + b + 1)
                    nc.scalar.copy(xT_hi[:, b * 512:(b + 1) * 512], px[:, b * 512:(b + 1) * 512]).then_inc(s_xhi, 1)

            def take_y(n, half):
                act.wait_ge(s_y, n + 1)
                act.wait_ge(s_code, n + 3)
                nc.scalar.copy(y_sb[half][:, 0:512], py[:, 0:512]).then_inc(s_ya, 1)

            rows_hi(0)

            def step(r, half):
                n = 2 * r + half
                split(0, n)
                split(1, n)
                split(2, n)
                split(3, n)
                if not (isinstance(r, int) and n == 0):
                    take_y(n - 1, 1 - half)
                act.wait_ge(s_gate, n + 1)
                nc.scalar.activation(act_g[:], pg[:], ACT.Silu).then_inc(s_silu, 1)
                split(4, n)
                split(5, n)
                act.wait_ge(s_ht, n + 1)
                nc.scalar.copy(hT_hi[:], ph[:]).then_inc(s_hhi, 1)
                rows_hi(n + 1)

            each_block(act, step)
            last = act.value_load(n_pairs[0:1, 1:2], min_val=0, max_val=(NE + MORE + 1) // 2)
            take_y(2 * last + 1, 1)

        @block.vector
        def _(dve):
            def split(j, n):
                dve.wait_ge(s_whi[j], n + 1)
                nc.vector.tensor_tensor(w_lo[:, j // 2, span(j)], raw[:, j // 2, span(j)],
                                        w_hi[:, j // 2, span(j)].bitcast(F32), ALU.subtract).then_inc(s_wlo[j], 1)

            def rows_lo(n):
                for b in range(2):
                    cols = slice(b * 512, (b + 1) * 512)
                    dve.wait_ge(s_xhi, 2 * n + b + 1)
                    nc.vector.tensor_tensor(xT_lo[:, cols], px[:, cols], xT_hi[:, cols].bitcast(F32),
                                            ALU.subtract).then_inc(s_xlo, 1)

            def take_y(n, half):
                dve.wait_ge(s_y, n + 1)
                dve.wait_ge(s_code, n + 3)
                nc.vector.tensor_copy(y_sb[half][:, 512:1024], py[:, 512:1024]).then_inc(s_yd, 1)

            rows_lo(0)

            def step(r, half):
                n = 2 * r + half
                split(0, n)
                split(1, n)
                split(2, n)
                split(3, n)
                if not (isinstance(r, int) and n == 0):
                    take_y(n - 1, 1 - half)
                split(4, n)
                dve.wait_ge(s_silu, n + 1)
                dve.wait_ge(s_up, n + 1)
                nc.vector.tensor_tensor(h_sb[:], act_g[:], pu[:], ALU.mult).then_inc(s_h, 1)
                dve.wait_ge(s_hhi, n + 1)
                nc.vector.tensor_tensor(hT_lo[:], ph[:], hT_hi[:].bitcast(F32), ALU.subtract).then_inc(s_hlo, 1)
                split(5, n)
                rows_lo(n + 1)

            each_block(dve, step)
            last = dve.value_load(n_pairs[0:1, 1:2], min_val=0, max_val=(NE + MORE + 1) // 2)
            take_y(2 * last + 1, 1)


def phase_combine(nc, x_mid, y_rows, g_final, gates, out):
    with ExitStack() as ctx:
        def sb(name, shape, dt=F32):
            return ctx.enter_context(nc.sbuf_tensor("f_" + name, shape, dt))

        sems = phase_sems(nc, ctx)

        def sem(name):
            return phase_sem(nc, sems, "f_" + name)

        g_row, eps = sb("g_row", [P, D]), sb("eps", [P, 1])
        share = sb("share", [P, 2, 2])
        x2 = sb("x2", [P, 2, D])
        y = sb("y", [P, 2, 2, D])
        sum_, o_sb = sb("sum", [P, 2, D]), sb("o_sb", [P, 2, D])
        junk = sb("junk", [P, D], BF16)
        ssq, root, rstd = sb("ssq", [P, 1]), sb("root", [P, 1]), sb("rstd", [P, 1])

        s_const, s_eps, s_share = sem("const"), sem("eps"), sem("share")
        s_x = [sem("x0"), sem("x1")]
        s_y = [sem("y0"), sem("y1")]
        s_scaled, s_sum, s_sq, s_root, s_rstd, s_o = (sem(n) for n in ("scaled", "sum", "sq", "root", "rstd", "o"))
        s_store = [sem("store0"), sem("store1")]
        s_d = sem("d")

        block = ctx.enter_context(nc.Block())

        @block.sync
        def _(sp):
            sp.dma_start(g_row[:], g_final.partition_broadcast(P)).then_inc(s_const, 16)
            y_v = y_rows.rearrange("(t p c) n -> t p (c n)", p=P, c=2)

            def tile(r, half, last):
                t = 2 * r + half
                if not (isinstance(r, int) and r == 0):
                    sp.wait_ge(s_sum, t - 1)
                    sp.wait_ge(s_const, 16)
                sp.dma_start(x2[:, half, :], x_mid[t]).then_inc(s_x[half], 16)
                sp.dma_start(y[:, half].rearrange("p c n -> p (c n)"), y_v[t]).then_inc(s_y[half], 16)

            pairs(sp, TILES, tile)

        @block.gpsimd
        def _(pool):
            nc.gpsimd.memset(eps[:], EPS).then_inc(s_eps, 1)

        @block.scalar
        def _(act):
            def fetch(t, r, half):
                act.wait_ge(s_sum, t - 1 if not (isinstance(r, int) and r == 0) else 0)
                nc.scalar.copy(share[:, half, :], gates[:, t, :]).then_inc(s_share, 1)

            act.wait_ge(s_eps, 1)
            fetch(0, 0, 0)
            fetch(1, 0, 1)

            def tile(r, half, last):
                t = 2 * r + half
                act.wait_ge(s_y[half], 16 * (r + 1))
                act.wait_ge(s_share, t + 1)
                nc.scalar.activation(y[:, half, 0, :], y[:, half, 0, :], ACT.Copy,
                                     scale=share[:, half, 0:1]).then_inc(s_scaled, 1)
                act.wait_ge(s_sum, t + 1)
                act.wait_ge(s_rstd, t)
                nc.scalar.activation(junk[:], sum_[:, half, :], ACT.Square, accum_out=ssq[:]).then_inc(s_sq, 1)
                act.wait_ge(s_sq, t + 1)
                nc.scalar.activation(root[:], ssq[:], ACT.Sqrt, bias=eps[:], scale=1.0 / D).then_inc(s_root, 1)
                if not (isinstance(r, int) and r == TILES // 2 - 1):
                    fetch(t + 2, r + 1, half)
                act.wait_ge(s_o, t + 1)
                act.dma_start(out[t], o_sb[:, half, :]).then_inc(s_store[half], 16)

            pairs(act, TILES, tile)
            act.wait_ge(s_store[0], 16 * TILES // 2)
            act.wait_ge(s_store[1], 16 * TILES // 2)

        @block.vector
        def _(dve):
            dve.wait_ge(s_const, 16)
            steps = Steps(dve, s_d, 1)

            def tile(r, half, last):
                t = 2 * r + half
                steps.begin(t)
                dve.wait_ge(s_scaled, t + 1)
                dve.wait_ge(s_x[half], 16 * (r + 1))
                steps.chain(nc.vector.scalar_tensor_tensor(out=y[:, half, 1, :], in0=y[:, half, 1, :],
                                                           scalar=share[:, half, 1:2], in1=y[:, half, 0, :],
                                                           op0=ALU.mult, op1=ALU.add))
                nc.vector.tensor_tensor(sum_[:, half, :], y[:, half, 1, :], x2[:, half, :], ALU.add).then_inc(s_sum, 1)
                dve.wait_ge(s_root, t + 1)
                nc.vector.reciprocal(rstd[:], root[:]).then_inc(s_rstd, 1)
                dve.wait_ge(s_rstd, t + 1)
                dve.wait_ge(s_store[half], 16 * r)
                nc.vector.scalar_tensor_tensor(out=o_sb[:, half, :], in0=sum_[:, half, :], scalar=rstd[:, 0:1],
                                               in1=g_row[:], op0=ALU.mult, op1=ALU.mult).then_inc(s_o, 1)
                steps.end()

            pairs(dve, TILES, tile)


def tables():
    inv = np.float32(1) / (10000.0 ** (np.arange(0, DR, 2) / DR)).astype(np.float32)
    pos = np.concatenate([np.arange(n * P, dtype=np.float32) for _, n in SEQS])
    ang = pos[:, None] * inv[None, :]
    cos, sin = np.cos(ang), np.sin(ang)
    rope = np.stack([np.concatenate([cos, cos], 1), np.concatenate([-sin, sin], 1)], 1)
    j, i = np.arange(P)[:, None], np.arange(P)[None, :]
    n = np.arange(P)
    return {
        "rope": rope.reshape(TILES, P, 2, DR).astype(np.float32),
        "ident": np.eye(P, dtype=np.float32),
        "dist": np.stack([np.maximum(i - j, 0), np.maximum(j - i, 0)], 1).astype(np.float32),
        "index": np.stack([-(P - 1 - n), -n, -(n + 1), -(P - n)], 1).astype(np.float32),
        "route": np.concatenate([np.broadcast_to(np.arange(NE), (P, NE)),
                                 np.broadcast_to(np.arange(NE) // EPG, (P, NE)),
                                 (j < i), np.ones((P, P))], 1).astype(np.float32),
        "blocks": np.concatenate([np.arange(NE), np.zeros(MORE + AHEAD), np.arange(NE) * ROWS,
                                  np.zeros(MORE + AHEAD)])[None, :].astype(np.int32),
    }


WEIGHTS = {"g_mix": "g_mix", "w_in": "w_in", "log_decay": "ret_log_decay", "gn_g": "ret_gn_g",
           "g_q": "mla_q_norm_g", "w_q_up": "w_q_up", "g_kv": "mla_kv_norm_g", "w_kv_up": "w_kv_up",
           "w_out": "w_out", "g_ffn": "g_ffn", "w_rg": "w_router_group", "w_re": "w_router_expert",
           "w_gate": "w_exp_gate", "w_up": "w_exp_up", "w_down": "w_exp_down"}


def build(nc, d, out):
    def scratch(name, shape, dt=F32):
        return nc.dram_tensor("s_" + name, shape, dt, kind="Internal").ap()

    mid = scratch("mid", (TILES, P, M_W))
    mixT = scratch("mixT", (TILES, P, D))
    x_mid = scratch("x_mid", (TILES, P, D))
    h_rows = scratch("h_rows", (ROWS, D))
    table = scratch("table", (NE * ROWS, 2), I32)
    y_rows = scratch("y_rows", (2 * ROWS, D))

    with ExitStack() as ctx:
        s_tick, s_tock = (ctx.enter_context(nc.semaphore(n)) for n in ("tick", "tock"))
        phase_project(nc, d["x"], d["w_in"], d["g_mix"], d["g_q"], d["g_kv"], d["rope"], d["ident"], mid)
        phase_retention(nc, mid, d["log_decay"], d["gn_g"], d["dist"], d["index"], d["ident"], mixT)
        for n, (first, tiles) in enumerate(SEQS):
            phase_latent(nc, f"c{n}", first, tiles, mid, d["w_q_up"], d["w_kv_up"], d["rope"], d["ident"], mixT)
        gates = ctx.enter_context(nc.sbuf_tensor("gates", [P, TILES, 2], F32))
        blocks = ctx.enter_context(nc.sbuf_tensor("blocks", [1, 2, NBLK], I32))
        n_pairs = ctx.enter_context(nc.sbuf_tensor("n_pairs", [1, 2], I32))
        raw = ctx.enter_context(nc.sbuf_tensor("raw", [P, 3, 4096], F32))
        s_raw = [ctx.enter_context(nc.semaphore(f"raw{j}")) for j in range(6)]
        w_exp = [d[n].rearrange("e (p k) n -> e p (k n)", p=P) for n in ("w_gate", "w_up", "w_down")]
        phase_mix(nc, mixT, d["x"], d["w_out"], d["g_ffn"], d["w_rg"], d["w_re"], d["ident"], d["route"],
                  d["blocks"], x_mid, h_rows.rearrange("(t p) n -> t p n", p=P), table, gates, blocks, n_pairs,
                  s_tick, s_tock, raw, s_raw, w_exp)
        phase_experts(nc, w_exp, d["ident"], h_rows, table, y_rows, blocks, n_pairs, s_tick, raw, s_raw)
        phase_combine(nc, x_mid, y_rows, d["g_final"], gates, out)


def kernel(**inputs):
    import concourse.bacc as _bacc
    from concourse.bass_utils import run_bass_kernel_spmd as _run

    nc = _bacc.Bacc("TRN2", target_bir_lowering=False, num_devices=1)
    x = np.concatenate([np.asarray(inputs["x_prompt"])[0], np.asarray(inputs["x_sample"])[0]], 0)
    arrays = {"x": x.reshape(TILES, P, D), "g_final": inputs["g_final"], **tables()}
    arrays.update({name: np.asarray(inputs[key])[0] for name, key in WEIGHTS.items()})
    arrays = {"in_" + name: np.ascontiguousarray(a) for name, a in arrays.items()}
    d = {name[3:]: nc.dram_tensor(name, a.shape, mybir.dt.from_np(a.dtype), kind="ExternalInput").ap()
         for name, a in arrays.items()}
    out = nc.dram_tensor("out", (TILES, P, D), F32, kind="ExternalOutput").ap()
    build(nc, d, out)
    r = _run(nc, [arrays], core_ids=[0])
    y = r.results[0]["out"].reshape(1, TILES * P, D)
    cut = SEQS[0][1] * P
    return y[:, :cut], y[:, cut:]
```
